# Optimizing a Trainium2 kernel written in Bass

```python
import jax, jax.numpy as jnp
from jax import lax
import numpy as np

D_MODEL = 2048
BATCH = 1
SEQ = 256
DEPTH = 1

HEAD_DIM = 128
MIX_WIDTH = D_MODEL
NSA_HEADS = MIX_WIDTH // 2 // HEAD_DIM
NSA_KV_GROUPS = 2
NSA_HPG = NSA_HEADS // NSA_KV_GROUPS
MOBA_HEADS = MIX_WIDTH // 2 // HEAD_DIM
CMP_LEN = 32
CMP_STRIDE = 16
CMP_HIDDEN = HEAD_DIM
SEL_LEN = 64
SEL_TOPK = 16
WINDOW = 512
MOBA_BLOCK = 256
MOBA_TOPK = 3
D_FF = 4 * D_MODEL
ROPE_THETA = 10000.0
EPS = 1e-6
NSA_Q_CHUNK = 64
MOBA_Q_CHUNK = 16

NSA_Q_W = NSA_HEADS * HEAD_DIM
NSA_KV_W = NSA_KV_GROUPS * HEAD_DIM
NSA_GATE_W = 3 * NSA_HEADS
MOBA_W = MOBA_HEADS * HEAD_DIM
IN_WIDTHS = (NSA_Q_W,) + (NSA_KV_W,) * 6 + (NSA_GATE_W, MOBA_W, MOBA_W, MOBA_W)
IN_COLS = sum(IN_WIDTHS)


def rms_norm(x, g):
    x32 = x.astype(jnp.float32)
    y = x32 * lax.rsqrt(jnp.mean(x32 * x32, axis=-1, keepdims=True) + EPS)
    return (y * g.astype(jnp.float32)).astype(x.dtype)

def modulate(h, shift, scale):
    return h * (1.0 + scale[:, None, :]) + shift[:, None, :]

def rope_tables(T):
    pos = jnp.arange(T, dtype=jnp.float32)
    inv = ROPE_THETA ** (-jnp.arange(0, HEAD_DIM, 2, dtype=jnp.float32) / HEAD_DIM)
    ang = pos[:, None] * inv[None, :]
    return jnp.cos(ang), jnp.sin(ang)

def apply_rope(x, cos, sin):
    shp = (x.shape[1],) + (1,) * (x.ndim - 3) + (HEAD_DIM // 2,)
    c_ = cos.reshape(shp)
    s_ = sin.reshape(shp)
    x32 = x.astype(jnp.float32)
    x1, x2 = jnp.split(x32, 2, axis=-1)
    return jnp.concatenate([x1 * c_ - x2 * s_, x2 * c_ + x1 * s_], axis=-1).astype(x.dtype)

def masked_softmax(s, mask):
    s = jnp.where(mask, s.astype(jnp.float32), -jnp.inf)
    m = jnp.max(s, axis=-1, keepdims=True)
    m = jnp.where(jnp.isfinite(m), m, 0.0)
    e = jnp.exp(s - m)
    return e / jnp.maximum(jnp.sum(e, axis=-1, keepdims=True), jnp.float32(1e-30))

def compress(x, pos, w1, w2):
    B, T, G, dh = x.shape
    n_cmp = (T - CMP_LEN) // CMP_STRIDE + 1
    idx = np.arange(n_cmp)[:, None] * CMP_STRIDE + np.arange(CMP_LEN)[None, :]
    blocks = x[:, idx] + pos[:, None, :].astype(x.dtype)
    blocks = blocks.transpose(0, 1, 3, 2, 4).reshape(B, n_cmp, G, CMP_LEN * dh)
    return jax.nn.silu(blocks @ w1) @ w2

def nsa_mixer(q, k_cmp, v_cmp, k_sel, v_sel, k_win, v_win, gate_logits,
              cmp_k_pos, cmp_k_w1, cmp_k_w2, cmp_v_pos, cmp_v_w1, cmp_v_w2, cos, sin):
    B, T, _ = q.shape
    G, Hg, dh = NSA_KV_GROUPS, NSA_HPG, HEAD_DIM
    Qc = NSA_Q_CHUNK
    q = apply_rope(q.reshape(B, T, G, Hg, dh), cos, sin) * (dh ** -0.5)
    kv = lambda a: a.reshape(B, T, G, dh)
    k_cmp = apply_rope(kv(k_cmp), cos, sin)
    k_sel = apply_rope(kv(k_sel), cos, sin)
    k_win = apply_rope(kv(k_win), cos, sin)
    v_cmp, v_sel, v_win = kv(v_cmp), kv(v_sel), kv(v_win)
    gates = jax.nn.sigmoid(gate_logits.astype(jnp.float32)).reshape(B, T, G, Hg, 3)

    kc = compress(k_cmp, cmp_k_pos, cmp_k_w1, cmp_k_w2)
    vc = compress(v_cmp, cmp_v_pos, cmp_v_w1, cmp_v_w2)
    n_cmp = kc.shape[1]
    cmp_start = np.arange(n_cmp) * CMP_STRIDE
    cmp_end_np = cmp_start + CMP_LEN
    cmp_end = jnp.asarray(cmp_end_np - 1)

    n_sel = T // SEL_LEN
    k_top = min(SEL_TOPK, n_sel)
    sel_start = np.arange(n_sel) * SEL_LEN
    overlap = np.clip(np.minimum(cmp_end_np[:, None], sel_start[None, :] + SEL_LEN)
                      - np.maximum(cmp_start[:, None], sel_start[None, :]), 0, None)
    sel_map = jnp.asarray((overlap / CMP_LEN).astype(np.float32))
    ks_blk = k_sel.reshape(B, n_sel, SEL_LEN, G, dh).transpose(0, 3, 1, 2, 4)
    vs_blk = v_sel.reshape(B, n_sel, SEL_LEN, G, dh).transpose(0, 3, 1, 2, 4)
    bi = jnp.arange(B)[:, None, None, None]
    gi = jnp.arange(G)[None, :, None, None]

    pad = ((0, 0), (WINDOW, 0), (0, 0), (0, 0))
    kw_pad = jnp.pad(k_win, pad)
    vw_pad = jnp.pad(v_win, pad)

    def chunk(i):
        s0 = i * Qc
        qc = lax.dynamic_slice_in_dim(q, s0, Qc, axis=1)
        gc = lax.dynamic_slice_in_dim(gates, s0, Qc, axis=1)
        tq = s0 + jnp.arange(Qc)
        sc = jnp.einsum('bqghd,bcgd->bghqc', qc, kc)
        p_c = masked_softmax(sc, cmp_end[None, :] <= tq[:, None])
        o_c = jnp.einsum('bghqc,bcgd->bqghd', p_c.astype(vc.dtype), vc)
        imp = jnp.einsum('bghqc,cs->bgqs', p_c, sel_map)
        cb = tq // SEL_LEN
        blk = jnp.arange(n_sel)[None, :]
        causal = blk <= cb[:, None]
        forced = (blk == 0) | (blk == cb[:, None]) | (blk == cb[:, None] - 1)
        score = jnp.where(causal, jnp.where(forced, jnp.inf, imp), -jnp.inf)
        _, idx = lax.top_k(score, k_top)
        ksg = ks_blk[bi, gi, idx]
        vsg = vs_blk[bi, gi, idx]
        kpos = idx[..., None] * SEL_LEN + jnp.arange(SEL_LEN)
        mask_s = (kpos <= tq[:, None, None]).reshape(B, G, 1, Qc, k_top * SEL_LEN)
        ss = jnp.einsum('bqghd,bgqkld->bghqkl', qc, ksg).reshape(B, G, Hg, Qc, k_top * SEL_LEN)
        p_s = masked_softmax(ss, mask_s)
        o_s = jnp.einsum('bghqn,bgqnd->bqghd', p_s.astype(vsg.dtype),
                         vsg.reshape(B, G, Qc, k_top * SEL_LEN, dh))
        kw = lax.dynamic_slice_in_dim(kw_pad, s0, Qc + WINDOW, axis=1)
        vw = lax.dynamic_slice_in_dim(vw_pad, s0, Qc + WINDOW, axis=1)
        kp = s0 - WINDOW + jnp.arange(Qc + WINDOW)
        dist = tq[:, None] - kp[None, :]
        mask_w = (dist >= 0) & (dist < WINDOW) & (kp[None, :] >= 0)
        sw = jnp.einsum('bqghd,bkgd->bghqk', qc, kw)
        p_w = masked_softmax(sw, mask_w)
        o_w = jnp.einsum('bghqk,bkgd->bqghd', p_w.astype(vw.dtype), vw)
        g = gc.astype(o_c.dtype)
        o = g[..., 0:1] * o_c + g[..., 1:2] * o_s + g[..., 2:3] * o_w
        return o.reshape(B, Qc, NSA_HEADS * dh)

    out = lax.map(chunk, jnp.arange(T // Qc))
    return jnp.moveaxis(out, 0, 1).reshape(B, T, NSA_HEADS * dh)

def moba_mixer(q, k, v, cos, sin):
    B, T, _ = q.shape
    H, dh, BLK, Qc = MOBA_HEADS, HEAD_DIM, MOBA_BLOCK, MOBA_Q_CHUNK
    q = apply_rope(q.reshape(B, T, H, dh), cos, sin) * (dh ** -0.5)
    k = apply_rope(k.reshape(B, T, H, dh), cos, sin)
    v = v.reshape(B, T, H, dh)
    nb = -(-T // BLK)
    pad = ((0, 0), (0, nb * BLK - T), (0, 0), (0, 0))
    k_pad = jnp.pad(k, pad)
    v_pad = jnp.pad(v, pad)
    k_blk = k_pad.reshape(B, nb, BLK, H, dh).transpose(0, 3, 1, 2, 4)
    v_blk = v_pad.reshape(B, nb, BLK, H, dh).transpose(0, 3, 1, 2, 4)
    k_mean = jnp.mean(k_blk.astype(jnp.float32), axis=3).astype(k.dtype)
    k_past = min(MOBA_TOPK, nb - 1)
    bi = jnp.arange(B)[:, None, None, None]
    hi = jnp.arange(H)[None, :, None, None]

    def chunk(i):
        s0 = i * Qc
        qc = lax.dynamic_slice_in_dim(q, s0, Qc, axis=1)
        tq = s0 + jnp.arange(Qc)
        cur = s0 // BLK
        ko = lax.dynamic_slice_in_dim(k_pad, cur * BLK, BLK, axis=1)
        vo = lax.dynamic_slice_in_dim(v_pad, cur * BLK, BLK, axis=1)
        opos = cur * BLK + jnp.arange(BLK)
        s_own = jnp.einsum('bqhd,blhd->bhql', qc, ko)
        m_own = jnp.broadcast_to(opos[None, :] <= tq[:, None], (B, H, Qc, BLK))
        if k_past > 0:
            gsc = jnp.einsum('bqhd,bhnd->bhqn', qc, k_mean).astype(jnp.float32)
            gsc = jnp.where(jnp.arange(nb) < cur, gsc, -jnp.inf)
            _, idx = lax.top_k(gsc, k_past)
            kg = k_blk[bi, hi, idx]
            vg = v_blk[bi, hi, idx]
            s_past = jnp.einsum('bqhd,bhqkld->bhqkl', qc, kg).reshape(B, H, Qc, k_past * BLK)
            m_past = jnp.broadcast_to((idx < cur)[..., None],
                                      (B, H, Qc, k_past, BLK)).reshape(B, H, Qc, k_past * BLK)
            p = masked_softmax(jnp.concatenate([s_past, s_own], axis=-1),
                               jnp.concatenate([m_past, m_own], axis=-1))
            p = p.astype(v.dtype)
            o = (jnp.einsum('bhqn,bhqnd->bqhd', p[..., :k_past * BLK],
                            vg.reshape(B, H, Qc, k_past * BLK, dh))
                 + jnp.einsum('bhql,blhd->bqhd', p[..., k_past * BLK:], vo))
        else:
            p = masked_softmax(s_own, m_own).astype(v.dtype)
            o = jnp.einsum('bhql,blhd->bqhd', p, vo)
        return o.reshape(B, Qc, H * dh)

    out = lax.map(chunk, jnp.arange(T // Qc))
    return jnp.moveaxis(out, 0, 1).reshape(B, T, H * dh)

def first_inputs(seed: int = 0) -> dict:
    key = jax.random.key(seed)
    ks = jax.random.split(key, 18)
    nrm = lambda k, shape, s: jax.random.normal(k, shape, jnp.float32) * s
    L = DEPTH
    return {
        'x': nrm(ks[0], (BATCH, SEQ, D_MODEL), 1.0),
        'c': nrm(ks[1], (BATCH, D_MODEL), 1.0),
        'w_ada': nrm(ks[2], (L, D_MODEL, 6 * D_MODEL), 0.5 * D_MODEL ** -0.5),
        'b_ada': nrm(ks[3], (L, 6 * D_MODEL), 0.01),
        'pre_norm_mix': 1.0 + nrm(ks[4], (L, D_MODEL), 0.05),
        'post_norm_mix': 1.0 + nrm(ks[5], (L, D_MODEL), 0.05),
        'w_in': nrm(ks[6], (L, D_MODEL, IN_COLS), D_MODEL ** -0.5),
        'cmp_k_pos': nrm(ks[7], (L, CMP_LEN, HEAD_DIM), 0.1),
        'cmp_k_w1': nrm(ks[8], (L, CMP_LEN * HEAD_DIM, CMP_HIDDEN), (CMP_LEN * HEAD_DIM) ** -0.5),
        'cmp_k_w2': nrm(ks[9], (L, CMP_HIDDEN, HEAD_DIM), CMP_HIDDEN ** -0.5),
        'cmp_v_pos': nrm(ks[10], (L, CMP_LEN, HEAD_DIM), 0.1),
        'cmp_v_w1': nrm(ks[11], (L, CMP_LEN * HEAD_DIM, CMP_HIDDEN), (CMP_LEN * HEAD_DIM) ** -0.5),
        'cmp_v_w2': nrm(ks[12], (L, CMP_HIDDEN, HEAD_DIM), CMP_HIDDEN ** -0.5),
        'w_o': nrm(ks[13], (L, MIX_WIDTH, D_MODEL), MIX_WIDTH ** -0.5),
        'pre_norm_ffn': 1.0 + nrm(ks[14], (L, D_MODEL), 0.05),
        'post_norm_ffn': 1.0 + nrm(ks[15], (L, D_MODEL), 0.05),
        'w_up': nrm(ks[16], (L, D_MODEL, D_FF), D_MODEL ** -0.5),
        'w_down': nrm(ks[17], (L, D_FF, D_MODEL), D_FF ** -0.5),
    }

def first_block(x, c, w_ada, b_ada, pre_norm_mix, post_norm_mix, w_in,
              cmp_k_pos, cmp_k_w1, cmp_k_w2, cmp_v_pos, cmp_v_w1, cmp_v_w2,
              w_o, pre_norm_ffn, post_norm_ffn, w_up, w_down):
    T = x.shape[1]
    cos, sin = rope_tables(T)
    split_at = np.cumsum(IN_WIDTHS)[:-1].tolist()
    for l in range(DEPTH):
        mod = jax.nn.silu(c) @ w_ada[l] + b_ada[l]
        shift_m, scale_m, gate_m, shift_f, scale_f, gate_f = jnp.split(mod, 6, axis=-1)
        h = modulate(rms_norm(x, pre_norm_mix[l]), shift_m, scale_m)
        (q_n, k_c, v_c, k_s, v_s, k_w, v_w, g_n,
         q_m, k_m, v_m) = jnp.split(h @ w_in[l], split_at, axis=-1)
        o_n = nsa_mixer(q_n, k_c, v_c, k_s, v_s, k_w, v_w, g_n,
                        cmp_k_pos[l], cmp_k_w1[l], cmp_k_w2[l],
                        cmp_v_pos[l], cmp_v_w1[l], cmp_v_w2[l], cos, sin)
        o_m = moba_mixer(q_m, k_m, v_m, cos, sin)
        o = jnp.concatenate([o_n, o_m], axis=-1) @ w_o[l]
        x = x + gate_m[:, None, :] * rms_norm(o, post_norm_mix[l])
        h = modulate(rms_norm(x, pre_norm_ffn[l]), shift_f, scale_f)
        f = jnp.square(jax.nn.relu(h @ w_up[l])) @ w_down[l]
        x = x + gate_f[:, None, :] * rms_norm(f, post_norm_ffn[l])
    return x


CHUNK = 64
Q_BLOCK = 128
SB_HEAD_DIM = 128
SB_WIDTH = D_MODEL // 4
SB_HEADS = SB_WIDTH // SB_HEAD_DIM
FOX_HEAD_DIM = 128
FOX_WIDTH = D_MODEL // 4
FOX_HEADS = FOX_WIDTH // FOX_HEAD_DIM
RWKV_HEAD_DIM = 64
RWKV_WIDTH = D_MODEL // 2
RWKV_HEADS = RWKV_WIDTH // RWKV_HEAD_DIM
DECAY_LORA = 64
AAA_LORA = 64
GATE_LORA = 160
RWKV_IN = 3 * RWKV_WIDTH + DECAY_LORA + AAA_LORA + GATE_LORA
N_BRANCHES = 3
N_IN = 3 * SB_WIDTH + 3 * FOX_WIDTH + FOX_HEADS + RWKV_IN + N_BRANCHES * D_MODEL
D_FF_2 = 4 * D_MODEL
RMS_EPS = 1e-6
RWKV_GN_EPS = 64e-5


def _split(x, sizes):
    points = np.cumsum(sizes)[:-1].tolist()
    return jnp.split(x, points, axis=-1)

def _rms_norm(x, gain):
    xf = x.astype(jnp.float32)
    y = xf * lax.rsqrt(jnp.mean(xf * xf, axis=-1, keepdims=True) + RMS_EPS)
    return (y * gain.astype(jnp.float32)).astype(x.dtype)

def _heads(x, n_heads):
    b, s, _ = x.shape
    return x.reshape(b, s, n_heads, -1).transpose(0, 2, 1, 3)

def _merge_heads(x):
    b, h, s, d = x.shape
    return x.transpose(0, 2, 1, 3).reshape(b, s, h * d)

def _query_blocks(x):
    b, h, s = x.shape[:3]
    x = x.reshape((b, h, s // Q_BLOCK, Q_BLOCK) + x.shape[3:])
    return jnp.moveaxis(x, 2, 0)

def _unblock(o):
    nb, b, h, qb, d = o.shape
    return o.transpose(1, 2, 0, 3, 4).reshape(b, h, nb * qb, d)

def stick_breaking_attention(q, k, v):
    s, d = q.shape[2], q.shape[3]
    scale = d ** -0.5
    kpos = jnp.arange(s)

    def block(args):
        qb, start = args
        z = jnp.einsum('bhqd,bhkd->bhqk', qb, k).astype(jnp.float32) * scale
        qpos = start + jnp.arange(Q_BLOCK)
        strict = kpos[None, :] < qpos[:, None]
        log_beta = jax.nn.log_sigmoid(z)
        log_rest = jnp.where(strict, jax.nn.log_sigmoid(-z), 0.0)
        between = lax.cumsum(log_rest, axis=3, reverse=True) - log_rest
        a = jnp.where(strict, jnp.exp(log_beta + between), 0.0)
        return jnp.einsum('bhqk,bhkd->bhqd', a.astype(v.dtype), v)

    starts = jnp.arange(s // Q_BLOCK, dtype=jnp.int32) * Q_BLOCK
    return _unblock(lax.map(block, (_query_blocks(q), starts)))

def forgetting_attention(q, k, v, log_f):
    s, d = q.shape[2], q.shape[3]
    scale = d ** -0.5
    kpos = jnp.arange(s)
    c = lax.cumsum(log_f.astype(jnp.float32), axis=2)

    def block(args):
        qb, cb, start = args
        z = jnp.einsum('bhqd,bhkd->bhqk', qb, k).astype(jnp.float32) * scale
        z = z + (cb[..., :, None] - c[..., None, :])
        qpos = start + jnp.arange(Q_BLOCK)
        causal = kpos[None, :] <= qpos[:, None]
        p = jax.nn.softmax(jnp.where(causal, z, -jnp.inf), axis=-1)
        return jnp.einsum('bhqk,bhkd->bhqd', p.astype(v.dtype), v)

    starts = jnp.arange(s // Q_BLOCK, dtype=jnp.int32) * Q_BLOCK
    return _unblock(lax.map(block, (_query_blocks(q), _query_blocks(c), starts)))

def rwkv7_time_mix(z, mu, w0, w_up, a0, a_up, g_up, k_k, k_a, r_k, ln_w, ln_b):
    b, s, _ = z.shape
    h, n = RWKV_HEADS, RWKV_HEAD_DIM
    z_prev = jnp.pad(z[:, :-1], ((0, 0), (1, 0), (0, 0)))
    z = z + (z_prev - z) * mu
    r, k, v, wd, ad, gd = _split(z, (RWKV_WIDTH,) * 3 + (DECAY_LORA, AAA_LORA, GATE_LORA))
    w_log = -jax.nn.softplus(-(w0 + jnp.tanh(wd) @ w_up)) - 0.5
    a = jax.nn.sigmoid(a0 + ad @ a_up)
    g = jax.nn.sigmoid(gd) @ g_up
    kk_raw = k * k_k
    k = k * (1 + (a - 1) * k_a)

    def per_head(t):
        return t.reshape(b, s, h, n).astype(jnp.float32)

    r_h, k_h, v_h, a_h, kk = map(per_head, (r, k, v, a, kk_raw))
    kk = kk / jnp.maximum(jnp.sqrt(jnp.sum(kk * kk, axis=-1, keepdims=True)), 1e-12)
    decay = jnp.exp(-jnp.exp(per_head(w_log)))

    def time_major(t):
        return t.transpose(1, 0, 2, 3).reshape(s // CHUNK, CHUNK, b, h, n)

    inputs = tuple(time_major(t) for t in (r_h, decay, k_h, v_h, kk, kk * a_h))

    def frame(state, inp):
        r_t, w_t, k_t, v_t, kk_t, kka_t = inp
        sa = jnp.einsum('bhvk,bhk->bhv', state, kk_t)
        state = (state * w_t[:, :, None, :] - sa[..., None] * kka_t[:, :, None, :]
                 + v_t[..., None] * k_t[:, :, None, :])
        return state, jnp.einsum('bhvk,bhk->bhv', state, r_t)

    def chunk(state, inp):
        return lax.scan(frame, state, inp)

    _, y = lax.scan(chunk, jnp.zeros((b, h, n, n), jnp.float32), inputs)
    y = y.reshape(s, b, h, n).transpose(1, 0, 2, 3)
    mean = jnp.mean(y, axis=-1, keepdims=True)
    var = jnp.mean(jnp.square(y - mean), axis=-1, keepdims=True)
    y = ((y - mean) * lax.rsqrt(var + RWKV_GN_EPS) * ln_w.astype(jnp.float32).reshape(h, n)
         + ln_b.astype(jnp.float32).reshape(h, n))
    y = y + jnp.sum(r_h * k_h * r_k.astype(jnp.float32), axis=-1, keepdims=True) * v_h
    return y.reshape(b, s, RWKV_WIDTH).astype(z.dtype) * g

def hybrid_mixer(u, w_in, b_forget, rwkv_mu, rwkv_w0, rwkv_w_up, rwkv_a0, rwkv_a_up, rwkv_g_up,
                 rwkv_k_k, rwkv_k_a, rwkv_r_k, rwkv_ln_w, rwkv_ln_b,
                 w_branch_a, w_branch_b, w_branch_c, w_out):
    proj = u @ w_in
    sb, fox, rw, gates = _split(proj, (3 * SB_WIDTH, 3 * FOX_WIDTH + FOX_HEADS, RWKV_IN,
                                       N_BRANCHES * D_MODEL))
    q_a, k_a, v_a = _split(sb, (SB_WIDTH,) * 3)
    y_a = _merge_heads(stick_breaking_attention(_heads(q_a, SB_HEADS), _heads(k_a, SB_HEADS),
                                                _heads(v_a, SB_HEADS)))
    q_b, k_b, v_b, f_b = _split(fox, (FOX_WIDTH,) * 3 + (FOX_HEADS,))
    log_f = jax.nn.log_sigmoid((f_b + b_forget).astype(jnp.float32)).transpose(0, 2, 1)
    y_b = _merge_heads(forgetting_attention(_heads(q_b, FOX_HEADS), _heads(k_b, FOX_HEADS),
                                            _heads(v_b, FOX_HEADS), log_f))
    y_c = rwkv7_time_mix(rw, rwkv_mu, rwkv_w0, rwkv_w_up, rwkv_a0, rwkv_a_up, rwkv_g_up,
                         rwkv_k_k, rwkv_k_a, rwkv_r_k, rwkv_ln_w, rwkv_ln_b)
    g_a, g_b, g_c = _split(jax.nn.sigmoid(gates), (D_MODEL,) * 3)
    m = g_a * (y_a @ w_branch_a) + g_b * (y_b @ w_branch_b) + g_c * (y_c @ w_branch_c)
    return m @ w_out

def second_inputs(seed: int = 0) -> dict:
    key = jax.random.key(seed)
    ks = jax.random.split(key, 24)
    L, D = DEPTH, D_MODEL

    def nrm(k, shape, scale):
        return jax.random.normal(k, shape, jnp.float32) * scale

    return {
        'x': nrm(ks[0], (BATCH, SEQ, D), 1.0),
        'norm_mix_pre': 1.0 + nrm(ks[1], (L, D), 0.05),
        'norm_mix_post': 1.0 + nrm(ks[2], (L, D), 0.05),
        'norm_mlp_pre': 1.0 + nrm(ks[3], (L, D), 0.05),
        'norm_mlp_post': 1.0 + nrm(ks[4], (L, D), 0.05),
        'w_in': nrm(ks[5], (L, D, N_IN), D ** -0.5),
        'b_forget': 1.0 + nrm(ks[6], (L, FOX_HEADS), 0.5),
        'rwkv_mu': jax.random.uniform(ks[7], (L, RWKV_IN), jnp.float32),
        'rwkv_w0': nrm(ks[8], (L, RWKV_WIDTH), 0.5),
        'rwkv_w_up': nrm(ks[9], (L, DECAY_LORA, RWKV_WIDTH), 0.5 * DECAY_LORA ** -0.5),
        'rwkv_a0': nrm(ks[10], (L, RWKV_WIDTH), 0.1),
        'rwkv_a_up': nrm(ks[11], (L, AAA_LORA, RWKV_WIDTH), 0.5 * AAA_LORA ** -0.5),
        'rwkv_g_up': nrm(ks[12], (L, GATE_LORA, RWKV_WIDTH), GATE_LORA ** -0.5),
        'rwkv_k_k': 0.85 + nrm(ks[13], (L, RWKV_WIDTH), 0.05),
        'rwkv_k_a': 1.0 + nrm(ks[14], (L, RWKV_WIDTH), 0.05),
        'rwkv_r_k': nrm(ks[15], (L, RWKV_HEADS, RWKV_HEAD_DIM), 0.1),
        'rwkv_ln_w': 1.0 + nrm(ks[16], (L, RWKV_WIDTH), 0.05),
        'rwkv_ln_b': nrm(ks[17], (L, RWKV_WIDTH), 0.01),
        'w_branch_a': nrm(ks[18], (L, SB_WIDTH, D), SB_WIDTH ** -0.5),
        'w_branch_b': nrm(ks[19], (L, FOX_WIDTH, D), FOX_WIDTH ** -0.5),
        'w_branch_c': nrm(ks[20], (L, RWKV_WIDTH, D), RWKV_WIDTH ** -0.5),
        'w_out': nrm(ks[21], (L, D, D), D ** -0.5),
        'w_mlp_up': nrm(ks[22], (L, D, D_FF_2), D ** -0.5),
        'w_mlp_down': nrm(ks[23], (L, D_FF_2, D), D_FF_2 ** -0.5),
    }

def second_block(x, norm_mix_pre, norm_mix_post, norm_mlp_pre, norm_mlp_post, w_in, b_forget,
              rwkv_mu, rwkv_w0, rwkv_w_up, rwkv_a0, rwkv_a_up, rwkv_g_up, rwkv_k_k, rwkv_k_a,
              rwkv_r_k, rwkv_ln_w, rwkv_ln_b, w_branch_a, w_branch_b, w_branch_c, w_out,
              w_mlp_up, w_mlp_down):
    for l in range(DEPTH):
        u = _rms_norm(x, norm_mix_pre[l])
        mix = hybrid_mixer(u, w_in[l], b_forget[l], rwkv_mu[l], rwkv_w0[l], rwkv_w_up[l],
                           rwkv_a0[l], rwkv_a_up[l], rwkv_g_up[l], rwkv_k_k[l], rwkv_k_a[l],
                           rwkv_r_k[l], rwkv_ln_w[l], rwkv_ln_b[l], w_branch_a[l], w_branch_b[l],
                           w_branch_c[l], w_out[l])
        x = x + _rms_norm(mix, norm_mix_post[l])
        hdn = jnp.square(jax.nn.relu(_rms_norm(x, norm_mlp_pre[l]) @ w_mlp_up[l]))
        x = x + _rms_norm(hdn @ w_mlp_down[l], norm_mlp_post[l])
    return x


def setup_inputs(seed=0):
    out = dict(first_inputs(seed))
    for name, value in second_inputs(seed + 1).items():
        if name != "x":
            out[name + "_2"] = value
    return out


def reference(
    x, c, w_ada, b_ada, pre_norm_mix, post_norm_mix, w_in, cmp_k_pos, cmp_k_w1, cmp_k_w2,
    cmp_v_pos, cmp_v_w1, cmp_v_w2, w_o, pre_norm_ffn, post_norm_ffn, w_up, w_down,
    norm_mix_pre_2, norm_mix_post_2, norm_mlp_pre_2, norm_mlp_post_2, w_in_2, b_forget_2,
    rwkv_mu_2, rwkv_w0_2, rwkv_w_up_2, rwkv_a0_2, rwkv_a_up_2, rwkv_g_up_2, rwkv_k_k_2,
    rwkv_k_a_2, rwkv_r_k_2, rwkv_ln_w_2, rwkv_ln_b_2, w_branch_a_2, w_branch_b_2, w_branch_c_2,
    w_out_2, w_mlp_up_2, w_mlp_down_2,
):
    x = first_block(
        x, c, w_ada, b_ada, pre_norm_mix, post_norm_mix, w_in, cmp_k_pos, cmp_k_w1, cmp_k_w2,
        cmp_v_pos, cmp_v_w1, cmp_v_w2, w_o, pre_norm_ffn, post_norm_ffn, w_up, w_down,
    )
    return second_block(
        x, norm_mix_pre_2, norm_mix_post_2, norm_mlp_pre_2, norm_mlp_post_2, w_in_2, b_forget_2,
        rwkv_mu_2, rwkv_w0_2, rwkv_w_up_2, rwkv_a0_2, rwkv_a_up_2, rwkv_g_up_2, rwkv_k_k_2,
        rwkv_k_a_2, rwkv_r_k_2, rwkv_ln_w_2, rwkv_ln_b_2, w_branch_a_2, w_branch_b_2,
        w_branch_c_2, w_out_2, w_mlp_up_2, w_mlp_down_2,
    )


_drawn_inputs = setup_inputs


def setup_inputs(seed=0):
    import zlib

    import numpy as np

    out = dict(_drawn_inputs(seed))
    spreads = {}
    factors = {'pre_norm_mix': 2.926,
     'cmp_k_pos': 8.0,
     'pre_norm_ffn': 2.689,
     'post_norm_ffn': 2.793,
     'rwkv_a0_2': 2.833,
     'rwkv_k_k_2': 47.485,
     'rwkv_ln_w_2': 2.933,
     'rwkv_ln_b_2': 32.023,
     'cmp_v_pos': 8.0}
    for name, (base, spread) in spreads.items():
        noise = np.random.default_rng([zlib.crc32(name.encode()), seed]).standard_normal(out[name].shape)
        drawn = base * np.exp(spread * noise) if base else spread * noise
        out[name] = __import__('jax').numpy.asarray(drawn.astype(out[name].dtype))
    for name, factor in factors.items():
        out[name] = (out[name] * factor).astype(out[name].dtype)
    return out
```

```python
from contextlib import ExitStack

import numpy as np

import concourse.bass as bass
from concourse import mybir

F32 = mybir.dt.float32
F32R = mybir.dt.float32r
ACT = mybir.ActivationFunctionType
ALU = mybir.AluOpType
AX = mybir.AxisListType

P = 128
D = 2048
T = 256
KT = D // P
TT = T // P
DH = 128
D_FF = 4 * D
HT = D_FF // 2 // P
EPS = 1e-6
SCALE = DH ** -0.5
NEG = -1e30

STEP_K = 4
GC = 512
GT = GC // P
RAW, SPLIT = 4, 2

CMP_LEN, CMP_STRIDE = 32, 16
NCMP = (T - CMP_LEN) // CMP_STRIDE + 1
NSA_H, GROUPS = 8, 2

QN, KC, VC, KS, VS, KW, VW, QM, KM, VM = 0, 8, 10, 12, 14, 16, 18, 20, 28, 36
PROJ1 = 44
GATES = 3 * NSA_H

SBQ, SBK, SBV, FXQ, FXK, FXV, RR, RK, RV, SPEC = 0, 4, 8, 12, 16, 20, 24, 32, 40, 48
PROJ2 = 52
RW = 1024
RT_ = RW // P
CHUNK = 64
LEVELS = [1, 2, 4, 8, 16, 32]
RHEAD = 64
RJ = 2
RTURNS = RT_ // RJ
RHEADS = 2 * RJ
MATS = RHEADS * TT
GN_EPS = 64e-5
FORGET_H, GATE_RANK = 4, 160
DECAY = float(np.exp(-0.5))
MU_R, MU_K, MU_V, W0, A0, K_K, K_A, R_K, LN_W, LN_B = range(10)


RWKV_LINKS = 32


class Layers:

    def __init__(self, layers):
        self.at = {}
        t = lin = ada = g = 0
        for name, kind, groups, spg in layers:
            self.at[name] = dict(kind=kind, groups=groups, spg=spg, t0=t, l0=lin, a0=ada, g0=g)
            assert t % RAW == 0
            n = groups * spg
            t += n
            if kind == "lin":
                lin += n
                g += groups
            else:
                ada += n
        self.order = [x[0] for x in layers]

    def __getitem__(self, name):
        return self.at[name]

    def unroll(self, name):
        L = self.at[name]
        return 1 if L["kind"] == "ada" else max(2, RAW // L["spg"])


def first_consts():
    pos = np.arange(T, dtype=np.float32)
    inv = (np.float32(10000.0) ** (-np.arange(0, DH, 2, dtype=np.float32) / np.float32(DH))).astype(np.float32)
    ang = inv[:, None] * pos[None, :]
    cos, sin = np.cos(ang).astype(np.float32), np.sin(ang).astype(np.float32)
    h = DH // 2
    rot = np.zeros((P, P), np.float32)
    rot[np.arange(h) + h, np.arange(h)] = -1
    rot[np.arange(h), np.arange(h) + h] = 1
    cend = np.arange(NCMP) * CMP_STRIDE + CMP_LEN - 1
    tok = np.arange(T).reshape(TT, P).T
    seen = (cend[None, None, :] <= tok[:, :, None]).astype(np.float32)
    return np.concatenate([rot, np.tile(cos, (2, 1)), np.tile(sin, (2, 1)), seen.reshape(P, -1),
                           ((1 - seen) * np.float32(NEG)).reshape(P, -1)], axis=1)


def common_consts():
    i = np.arange(P)
    causal = np.where(i[None, :] <= i[:, None], 0, NEG).astype(np.float32)
    return np.concatenate([np.eye(P, dtype=np.float32), np.ones((P, P), np.float32), np.zeros((P, P), np.float32),
                           causal, np.full((P, 1), EPS, np.float32)], axis=1)


def second_consts():
    i = np.arange(P)
    strict = np.where(i[None, :] < i[:, None], 0, NEG).astype(np.float32)
    same_head = (i[:, None] // RHEAD == i[None, :] // RHEAD).astype(np.float32) / np.float32(RHEAD)
    same = i[:, None] // CHUNK == i[None, :] // CHUNK
    before = same & (i[:, None] < i[None, :])
    upto = same & (i[:, None] <= i[None, :])
    levels = [(i[:, None] // (2 * b) == i[None, :] // (2 * b)) & (i[:, None] // b % 2 == 0) & (i[None, :] // b % 2 == 1)
              for b in LEVELS]
    reset = np.tile((np.arange(T) % CHUNK != 0), (P, 1))
    return np.concatenate([np.zeros((P, P)), strict, same_head, before, upto, *levels, reset], axis=1).astype(np.float32)


VECS = ["pre_norm_mix", "post_norm_mix", "pre_norm_ffn", "post_norm_ffn",
        "norm_mix_pre_2", "norm_mix_post_2", "norm_mlp_pre_2", "norm_mlp_post_2"]


def build_program(nc, a, blocks=(1, 2)):
    layers = []
    if 1 in blocks:
        layers += [("ada_a", "ada", 8, 4), ("w_in", "lin", PROJ1 // GT, 4), ("ada_b", "ada", 16, 4), ("w_o", "lin", 4, 4),
                   ("up_0", "lin", 8, 4), ("down_0", "lin", 4, 8), ("up_1", "lin", 8, 4), ("down_1", "lin", 4, 8)]
    if 2 in blocks:
        layers += [("w_in2", "lin", PROJ2 // GT, 4), ("gates2", "lin", 12, 4), ("branch", "lin", 4, 4), ("w_out2", "lin", 4, 4),
                   ("up2_0", "lin", 8, 4), ("down2_0", "lin", 4, 8), ("up2_1", "lin", 8, 4), ("down2_1", "lin", 4, 8)]
    L = Layers(layers)

    def matrix(ap):
        return ap.rearrange("(k p) n -> p k n", p=P)

    weights = {}
    if 1 in blocks:
        w_ada, w_up, w_down = matrix(a["w_ada"]), matrix(a["w_up"]), matrix(a["w_down"])
        weights |= {"ada_a": (w_ada, 0, 0), "ada_b": (w_ada, 0, 8 * GC), "w_in": (matrix(a["w_in"]), 0, 0),
                    "w_o": (matrix(a["w_o"]), 0, 0), "up_0": (w_up, 0, 0), "up_1": (w_up, 0, D_FF // 2),
                    "down_0": (w_down, 0, 0), "down_1": (w_down, HT, 0)}

    if 2 in blocks:
        w_up2, w_down2 = matrix(a["w_mlp_up_2"]), matrix(a["w_mlp_down_2"])
        weights |= {"w_in2": (matrix(a["w_in_2"]), 0, 0), "gates2": (matrix(a["w_gates_2"]), 0, 0),
                    "w_out2": (matrix(a["w_out_2"]), 0, 0), "up2_0": (w_up2, 0, 0), "up2_1": (w_up2, 0, D_FF // 2),
                    "down2_0": (w_down2, 0, 0), "down2_1": (w_down2, HT, 0)}

    top = [16512]
    made = {}

    def at(name, shape, dt, offset):
        made[name] = nc.alloc_sbuf_tensor_at(name, shape, dt, offset=offset)
        return made[name]

    def new(name, shape, dt=F32):
        off = top[0]
        n = 4 * int(np.prod(shape[1:]))
        top[0] = (off + n + 31) // 32 * 32
        return at(name, shape, dt, off)

    x = new("x", [P, KT, T])
    ACT0 = top[0]
    actH = new("actH", [P, KT, T], F32R)
    actL = new("actL", [P, KT, T], F32R)
    RING0 = top[0]
    raw = new("raw", [P, RAW, STEP_K, GC])
    SPLIT0 = top[0]
    wH = new("wH", [P, SPLIT, STEP_K, GC], F32R)
    wL = new("wL", [P, SPLIT, STEP_K, GC], F32R)
    common = new("common", [P, 4 * P + 1])
    ident, ones = common[:, 0:P], common[:, P:2 * P]
    eps = common[:, 4 * P:]
    causal = common[:, 2 * P:4 * P]
    vecs = new("vecs", [P, len(VECS), KT])
    mod = new("mod", [P, 6, KT])
    b_ada = new("b_ada", [P, 6, KT])
    cvec = new("cvec", [P, KT])
    csig = new("csig", [P, KT])
    coef = new("coef", [P, 8, KT])
    nmx = new("nmx", [P, 2, TT, 4])
    rsum = new("rsum", [P, 2, TT, 4])
    B0 = top[0]
    R0 = 229368 // 32 * 32 - 84 * 1024 - 512
    std = at("std", [P, T], F32, R0 + 83 * 1024)
    NC1 = P + 2 * T + 2 * TT * NCMP
    c1 = at("c1", [P, NC1], F32, B0)
    rot, cos, sin = c1[:, 0:P], c1[:, P:P + T], c1[:, P + T:P + 2 * T]
    seen = c1[:, P + 2 * T:P + 2 * T + TT * NCMP].rearrange("p (t n) -> p t n", t=TT)
    unseen = c1[:, P + 2 * T + TT * NCMP:].rearrange("p (t n) -> p t n", t=TT)
    assert B0 + 4 * NC1 <= R0, (B0 + 4 * NC1, R0)

    hidH = at("hidH", [P, HT, T], F32R, R0)
    hidL = at("hidL", [P, HT, T], F32R, R0 + 32 * 1024)
    o = at("o", [P, KT, T], F32, R0 + 64 * 1024)
    hid = at("hid_sq", [P, GT * T], F32, R0 + 80 * 1024)
    sq = at("sq", [P, KT, T], F32, R0)
    K1 = 1024
    proj = at("proj", [P, PROJ1, T], F32, R0)
    vtok = at("vtok", [P, 12, TT, P], F32, R0 + 44 * K1)
    probs0 = at("probs0", [P, 2, 4, P], F32, R0 + 56 * K1)
    probs1 = at("probs1", [P, 2, 4, T], F32, R0 + 60 * K1)
    pT0 = at("pT0", [P, 4, T], F32, R0 + 68 * K1)
    pT1 = at("pT1", [P, 4, P], F32, R0 + 72 * K1)
    rope_c = at("rope_c", [P, 2, 2, T], F32, R0 + 56 * K1)
    rope_s = at("rope_s", [P, 2, 2, T], F32, R0 + 60 * K1)
    gw = at("gw", [P, KT, GATES], F32, R0 + 74 * K1)
    gwH = at("gwH", [P, KT, GATES], F32R, R0 + 76 * K1)
    gwL = at("gwL", [P, KT, GATES], F32R, R0 + 78 * K1)
    gate = at("gate", [P, TT, GATES], F32, R0 + 80 * K1)
    posk = at("posk", [P, 2, CMP_LEN], F32, R0 + 80 * K1 + 256)
    cw2 = at("cw2", [P, 2, P], F32, R0 + 80 * K1 + 512)
    cbias = at("cbias", [P, 2], F32, R0 + 80 * K1 + 1536)
    chid = at("chid", [P, 2, GROUPS * NCMP], F32, R0 + 80 * K1 + 1568)
    kcT = at("kcT", [P, GROUPS * NCMP], F32, R0 + 80 * K1 + 1824)
    vc = at("vc", [NCMP, GROUPS, P], F32, R0 + 80 * K1 + 1952)
    pcmp = at("pcmp", [P, TT, 4, NCMP], F32, R0 + 74 * K1)
    pcT = at("pcT", [NCMP, 4, T], F32, R0 + 75 * K1)
    cw1 = at("cw1", [P, 2, CMP_LEN, P], F32, ACT0)

    NC2 = 5 * P + len(LEVELS) * P + T
    c2 = at("c2", [P, NC2], F32, B0)
    strict, same_head = c2[:, 0:2 * P], c2[:, 2 * P:3 * P]
    token_mask = c2[:, 3 * P:5 * P]
    level_mask = c2[:, 5 * P:(5 + len(LEVELS)) * P].rearrange("p (l n) -> p l n", l=len(LEVELS))
    reset = c2[:, (5 + len(LEVELS)) * P:]
    rwv = at("rwv", [P, 10 * RT_ + 5], F32, B0 + 4 * NC2)
    rwv10 = rwv[:, 0:10 * RT_].rearrange("p (v j) -> p v j", v=10)
    mu_spec, b_forget, gn_eps = rwv[:, 10 * RT_:10 * RT_ + 3], rwv[0:4, 10 * RT_ + 3:10 * RT_ + 4], rwv[:, 10 * RT_ + 4:]
    rv = at("rv", [P, 10, RJ], F32, B0 + 4 * NC2 + 352)
    assert B0 + 4 * NC2 + 352 + 80 <= R0
    mix_t = at("mix_t", [P, GT * T], F32, B0)
    proj2 = at("proj2", [P, PROJ2, T], F32, R0)
    gates = at("gates", [P, 48, T], F32, R0)
    mix = at("mix", [P, GT * T], F32, R0 + 48 * K1)
    yH = at("yH", [P, KT, T], F32R, R0 + 52 * K1)
    yL = at("yL", [P, KT, T], F32R, R0 + 68 * K1)
    vtok2 = at("vtok2", [P, 8, TT, P], F32, SPLIT0)
    prob0 = at("prob0", [P, 2, 4, P], F32, SPLIT0 + 8 * K1)
    prob1 = at("prob1", [P, 2, 4, T], F32, SPLIT0 + 12 * K1)
    qT0 = at("qT0", [P, 4, T], F32, SPLIT0 + 20 * K1)
    qT1 = at("qT1", [P, 4, P], F32, SPLIT0 + 24 * K1)
    soft0 = at("soft0", [P, 4, P], F32, SPLIT0 + 26 * K1)
    soft1 = at("soft1", [P, 4, T], F32, SPLIT0 + 28 * K1)
    cum = at("cum", [4, 4, T], F32, RING0)
    rtop = [RING0]

    def ring(name, shape):
        off = rtop[0]
        rtop[0] += 4 * int(np.prod(shape[1:]))
        assert rtop[0] <= RING0 + 64 * K1
        return at(name, shape, F32, off)

    Bc, Kc = ring("Bc", [P, MATS, 2 * P]), ring("Kc", [P, MATS, 2 * P])
    Xm, Ym, W1 = ring("Xm", [P, MATS, P]), ring("Ym", [P, MATS, P]), ring("W1", [P, MATS, P])
    Lm = ring("Lm", [P, 2, MATS, P])
    AR = [ring(f"AR{h}", [P, RJ, TT, 2, P]) for h in range(2)]
    btok, ktok = ring("btok", [P, 2, TT, RJ, P]), ring("ktok", [P, 2, TT, RJ, P])
    rtok = ring("rtok", [P, TT, RJ, P])
    rhs, uf, ST = ring("rhs", [P, RHEADS * RHEAD]), ring("uf", [P, RHEADS * RHEAD]), ring("ST", [P, RJ, P])
    lw = ring("lw", [P, 3, RJ * P])
    BT, KTt = ring("BT", [P, RJ, T]), ring("KT", [P, RJ, T])
    rr, rk, rvv, d0, d1, d2, sg, aa, gg, cs, Gd, Gi = (
        at(n, [P, RJ, T], F32, R0 + 2 * K1 * j) for j, n in enumerate(
            ("rr", "rk", "rvv", "d0", "d1", "d2", "sg", "aa", "gg", "cs", "Gd", "Gi")))
    at_spec = at("spec_d", [P, 3, T], F32, RING0 + 60 * K1)
    kk, nrm, k2, Gp, ka, rkk, bonus, yb, ysq = d0, d1, d2, cs, sg, aa, d0, rr, rk

    ps = nc.alloc_psum_tensor("ps", [P, 8, 512], F32)

    def flat(ap):
        return ap.rearrange("p a b -> p (a b)")

    def bank2(b):
        return flat(ps[:, b:b + 2, :])

    with ExitStack() as ctx:
        def sem(name):
            return ctx.enter_context(nc.semaphore(name))

        raw_in = [sem(f"raw_in{s}") for s in range(RAW)]
        wh_ready, wl_ready, step_done = sem("wh_ready"), sem("wl_ready"), sem("step_done")
        ada_done, evacuated = sem("ada_done"), sem("evacuated")
        consts_in, x_in, c1_in = sem("consts_in"), sem("x_in"), sem("c1_in")
        csig_ready, csilu_ready, mod_ready = sem("csig_ready"), sem("csilu_ready"), sem("mod_ready")
        sq_ready, ssum_ready, std_ready = sem("sq_ready"), sem("ssum_ready"), sem("std_ready")
        y_ready, h_ready, act_ready, x_ready = sem("y_ready"), sem("h_ready"), sem("act_ready"), sem("x_ready")
        dve_chain, act_chain, pool_chain = sem("dve_chain"), sem("act_chain"), sem("pool_chain")
        gw_in, gw_hi, gw_lo, gate_done, gate_ready = (sem(n) for n in ("gw_in", "gw_hi", "gw_lo", "gate_done", "gate_ready"))
        rotated, rope_cos, rope_used, roped = sem("rotated"), sem("rope_cos"), sem("rope_used"), sem("roped")
        vT_done, vtok_ready = sem("vT_done"), sem("vtok_ready")
        cmp_in, cmp_sum, cmp_sig, cmp_bias, cmp_hid, cmp_kv, cmp_ready = (
            sem(n) for n in ("cmp_in", "cmp_sum", "cmp_sig", "cmp_bias", "cmp_hid", "cmp_kv", "cmp_ready"))
        scores, masked, exped, weight, probs_ready = (
            sem(n) for n in ("scores", "masked", "exped", "weight", "probs_ready"))
        pT_done, pT_ready, pv_done, oH_ready, oL_ready = (
            sem(n) for n in ("pT_done", "pT_ready", "pv_done", "oH_ready", "oL_ready"))
        sqr_ready, hidH_ready, hidL_ready, relu_done = (
            sem(n) for n in ("sqr_ready", "hidH_ready", "hidL_ready", "relu_done"))
        out_sem = sem("out_stored")
        c2_in, lw_in, branch_in = sem("c2_in"), sem("lw_in"), sem("branch_in")
        yn_ready, hn_ready = sem("yn_ready"), sem("hn_ready")
        v2T_done, v2_ready, f_log, cum_ready = sem("v2T_done"), sem("v2_ready"), sem("f_log"), sem("cum_ready")
        s2_done, s2_masked, s2_soft, s2_sub, s2_exp, s2_weight, s2_probs = (
            sem(n) for n in ("s2_done", "s2_masked", "s2_soft", "s2_sub", "s2_exp", "s2_weight", "s2_probs"))
        t2_done, t2_ready, o2_done, y2H_ready, y2L_ready = (
            sem(n) for n in ("t2_done", "t2_ready", "o2_done", "y2H_ready", "y2L_ready"))
        spec_mixed, spec_ready, zeroed, turn_done = sem("spec_mixed"), sem("spec_ready"), sem("zeroed"), sem("turn_done")
        shifted_z, mixed, lora_done, sig_ready, kk_ready, kksq, kksum, nrm_ready = (
            sem(n) for n in ("shifted_z", "mixed", "lora_done", "sig_ready", "kk_ready", "kksq", "kksum", "nrm_ready"))
        cs_ready, gexp, csp_ready, gp_ready, k2_ready, kkn_ready, a_ready, b_ready = (
            sem(n) for n in ("cs_ready", "gexp", "csp_ready", "gp_ready", "k2_ready", "kkn_ready", "a_ready", "b_ready"))
        rk_ready, rk_scaled, bonus_sum, bonus_ready, tok_done, tok_ready = (
            sem(n) for n in ("rk_ready", "rk_scaled", "bonus_sum", "bonus_ready", "tok_done", "tok_ready"))
        mat_done, mat_masked, y1_ready, x1_done, x1_ready, lm_ready = (
            sem(n) for n in ("mat_done", "mat_masked", "y1_ready", "x1_done", "x1_ready", "lm_ready"))
        w1_done, w1_ready, dx_done, level_ready = (sem(n) for n in ("w1_done", "w1_ready", "dx_done", "level_ready"))
        rhs_done, rhs_ready, u_done, u_ready, s_done, st_ready, ysum_done = (
            sem(n) for n in ("rhs_done", "rhs_ready", "u_done", "u_ready", "s_done", "st_ready", "ysum_done"))
        r_ready = sem("r_ready")
        yb_ready, mean_done, yc_ready, ysq_ready, var_done, gstd_ready, yc_out, ycH_ready = (
            sem(n) for n in ("yb_ready", "mean_done", "yc_ready", "ysq_ready", "var_done", "gstd_ready", "yc_out", "ycH_ready"))
        mix_ready, mixH_ready, mixL_ready, branch_used = (
            sem(n) for n in ("mix_ready", "mixH_ready", "mixL_ready", "branch_used"))
        NB = 4 * (1 in blocks)
        UB = 16 * (1 in blocks)
        XB = 2 * (1 in blocks)

        class Chain:

            def __init__(self, eng, s):
                self.eng, self.s, self.n, self.off = eng, s, 0, 0

            def __call__(self, ins):
                self.n += 1
                ins.then_inc(self.s, 1)
                self.eng.wait_ge(self.s, self.off + self.n)

        def over_groups(eng, name, first, body):
            U, n = L.unroll(name), L[name]["groups"]
            for r in range(first):
                body(0, r)
            turns = (n - first) // U
            if turns > 1:
                with eng.Fori(0, turns) as i:
                    for r in range(U):
                        body(i, first + r)
            elif turns:
                for r in range(U):
                    body(0, first + r)
            for r in range(n - first - turns * U):
                body(turns, first + r)

        def raw_loads(name, i, r, s):
            l, U = L[name], L.unroll(name)
            j = r * l["spg"] + s
            return j % RAW, 16 * (l["t0"] // RAW + j // RAW + 1) + i * (16 * U * l["spg"] // RAW)

        def lin(name, i, r, s=0):
            l, U = L[name], L.unroll(name)
            return l["l0"] + r * l["spg"] + s + i * (U * l["spg"])

        def grp(name, i, r):
            return L[name]["g0"] + r + i * L.unroll(name)

        def done(name):
            l = L[name]
            return SPLIT + l["l0"] + l["groups"] * l["spg"]

        def emptied(name):
            return 2 + L[name]["g0"] + L[name]["groups"]

        def acc(name, r):
            return 2 * ((L[name]["g0"] + r) % 2)

        subs = []
        for g in range(GROUPS):
            q = QN + 4 * g
            subs += [("full", q, [KS + g] * 4, [0 + g] * 4, 1, True, False),
                     ("full", q, [KW + g] * 4, [2 + g] * 4, 2, False, False),
                     ("cmp", q, g, None, 0, False, True)]
        for m in range(2):
            subs.append(("full", QM + 4 * m, [KM + 4 * m + h for h in range(4)], [4 + 4 * m + h for h in range(4)],
                         None, True, True))
        out_of = [g for g, n in ((0, 3), (1, 3), (2, 1), (3, 1)) for _ in range(n)]
        NSUB = len(subs)
        rope_pairs = [QN, QN + 2, QN + 4, QN + 6, KC, KS, KW] + list(range(QM, VM, 2))
        v_pairs = [VS, VW] + list(range(VM, PROJ1, 2))

        up_groups_before = {}
        seen_up = 0
        for name in L.order:
            if name.startswith("up"):
                up_groups_before[name] = L[name]["g0"] - seen_up
                seen_up += L[name]["groups"]

        block = ctx.enter_context(nc.Block())

        @block.sync
        def _(sp):
            sp.dma_start(cvec[:, :], a["c"]).then_inc(consts_in, 16)
            sp.dma_start(common[:, :], a["common"]).then_inc(consts_in, 16)
            sp.dma_start(vecs[:, :, :], a["vecs"]).then_inc(consts_in, 16)
            sp.dma_start(b_ada[:, :, :], a["b_ada"]).then_inc(consts_in, 16)
            sp.dma_start(x[:, :, :], matrix(a["x"])).then_inc(x_in, 16)

            def stream(name):
                l, U = L[name], L.unroll(name)
                w, k0, n0 = weights[name]

                def body(i, r):
                    for s in range(l["spg"]):
                        slot, _ = raw_loads(name, i, r, s)
                        if l["kind"] == "ada":
                            sp.wait_ge(ada_done, l["a0"] + r * 4 + s + 1 + i * 4)
                        else:
                            sp.wait_ge(wl_ready, lin(name, i, r, s) + 1)
                        sp.dma_start(raw[:, slot, :, :],
                                     w[:, k0 + s * STEP_K:k0 + (s + 1) * STEP_K, bass.ds(n0 + r * GC + i * (U * GC), GC)]
                                     ).then_inc(raw_in[slot], 16)

                if l["kind"] == "ada":
                    if l["l0"]:
                        sp.wait_ge(wl_ready, RAW + l["l0"])
                elif l["a0"]:
                    sp.wait_ge(ada_done, RAW + l["a0"])
                over_groups(sp, name, 0, body)

            if 1 in blocks:
                stream("ada_a")
                sp.dma_start(c1[:, :], a["c1"]).then_inc(c1_in, 16)
                sp.dma_start(gw[:, :, :], matrix(a["w_gate"])).then_inc(gw_in, 16)
                stream("w_in")
                sp.wait_ge(step_done, done("w_in"))
                sp.wait_ge(gate_done, 1)
                sp.dma_start(cw1[:, 0, :, :], a["cmp_k_w1"].rearrange("(l d) h -> d l h", d=P)).then_inc(cmp_in, 16)
                sp.dma_start(cw1[:, 1, :, :], a["cmp_v_w1"].rearrange("(l d) h -> d l h", d=P)).then_inc(cmp_in, 16)
                sp.dma_start(posk[:, :, :], a["pos"]).then_inc(cmp_in, 16)
                sp.dma_start(cw2[:, 0, :], a["cmp_k_w2"]).then_inc(cmp_in, 16)
                sp.dma_start(cw2[:, 1, :], a["cmp_v_w2"]).then_inc(cmp_in, 16)
                for name in ("ada_b", "w_o", "up_0", "down_0", "up_1", "down_1"):
                    stream(name)
            if 2 in blocks:
                if 1 in blocks:
                    sp.wait_ge(roped, len(rope_pairs))
                    sp.wait_ge(oL_ready, 4)
                sp.dma_start(c2[:, :], a["c2"]).then_inc(c2_in, 16)
                sp.dma_start(rwv[:, :], a["rwv"]).then_inc(c2_in, 16)
                stream("w_in2")
                sp.wait_ge(zeroed, 1)
                with sp.Fori(0, RTURNS) as i:
                    sp.wait_ge(turn_done, i + 1)
                    for part, src in ((slice(0, 64), "rwkv_w_up_2"), (slice(64, P), "rwkv_a_up_2")):
                        sp.dma_start(lw[part, 0, :], a[src][:, bass.ds(i * (RJ * P), RJ * P)]).then_inc(lw_in, 16)
                    sp.dma_start(lw[:, 1, :], a["rwkv_g_up_2"][0:P, bass.ds(i * (RJ * P), RJ * P)]).then_inc(lw_in, 16)
                    sp.dma_start(lw[96:P, 2, :], a["rwkv_g_up_2"][P:P + 32, bass.ds(i * (RJ * P), RJ * P)]).then_inc(lw_in, 16)
                sp.wait_ge(turn_done, RTURNS + 1)
                stream("gates2")
                wa, wb, wc = (matrix(a[f"w_branch_{n}_2"]) for n in "abc")

                def branch_loads(i, r):
                    for s, (w, k) in enumerate(((wa, 0), (wb, 0), (wc, 0), (wc, STEP_K))):
                        slot, _ = raw_loads("branch", i, r, s)
                        sp.wait_ge(wl_ready, lin("branch", i, r, s) + 1)
                        sp.dma_start(raw[:, slot, :, :], w[:, k:k + STEP_K, bass.ds(r * GC + i * (2 * GC), GC)]
                                     ).then_inc(raw_in[slot], 16)

                over_groups(sp, "branch", 0, branch_loads)
                for name in ("w_out2", "up2_0", "down2_0", "up2_1", "down2_1"):
                    stream(name)
            sp.wait_ge(x_ready, 2 * len(blocks))
            sp.dma_start(matrix(a["out"]), x[:, :, :]).then_inc(out_sem, 16)
            sp.wait_ge(out_sem, 16)

        @block.scalar
        def _(act):
            chain = Chain(act, act_chain)

            def split(name, i, r, s):
                slot, count = raw_loads(name, i, r, s)
                act.wait_ge(raw_in[slot], count)
                act.wait_ge(step_done, lin(name, i, r, s) + 1)
                nc.scalar.activation(wH[:, s % SPLIT if L[name]["spg"] > 1 else r % SPLIT, :, :], raw[:, slot, :, :],
                                     ACT.Copy).then_inc(wh_ready, 1)

            def layer(name, evac=None):
                spg = L[name]["spg"]

                def body(i, r):
                    for s in range(spg):
                        split(name, i, r, s)
                        if evac and s == min(1, spg - 1) and not (isinstance(i, int) and i == 0 and r == 0):
                            evac(name, i, r - 1)

                over_groups(act, name, 1, body)
                if evac:
                    last(name, evac)

            def last(name, evac):
                n, U = L[name]["groups"], L.unroll(name)
                i = (n - 1 - 1) // U
                evac(name, i, n - 1 - i * U)

            def copy_to(dst, func=ACT.Copy):
                def evac(name, i, r):
                    act.wait_ge(step_done, SPLIT + lin(name, i, r, L[name]["spg"] - 1) + 1)
                    nc.scalar.activation(flat(dst[:, bass.ds(GT * r + i * (GT * L.unroll(name)), GT), :]),
                                         bank2(acc(name, r)), func).then_inc(evacuated, 1)
                return evac

            def square_relu(half):
                def evac(name, i, r):
                    act.wait_ge(step_done, SPLIT + lin(name, i, r, L[name]["spg"] - 1) + 1)
                    g = grp(name, i, r) - up_groups_before[name] + 1
                    act.wait_ge(hidL_ready, g)
                    nc.scalar.activation(hid[:, :], bank2(acc(name, r)), ACT.Relu).then_inc(evacuated, 1)
                    act.wait_ge(evacuated, 2 + grp(name, i, r) + 1)
                    nc.scalar.activation(hid[:, :], hid[:, :], ACT.Square).then_inc(sqr_ready, 1)
                    act.wait_ge(sqr_ready, g)
                    nc.scalar.activation(flat(hidH[:, bass.ds(GT * r + i * (GT * L.unroll(name)), GT), :]), hid[:, :],
                                         ACT.Copy).then_inc(hidH_ready, 1)
                return evac

            def norm(n, src, wait):
                wait()
                nc.scalar.activation(flat(sq[:, :, :]), flat(src[:, :, :]), ACT.Square).then_inc(sq_ready, 1)
                act.wait_ge(ssum_ready, n + 1)
                nc.scalar.activation(std[:, :], ps[:, 4, 0:T], ACT.Sqrt, bias=eps, scale=1.0 / D
                                     ).then_inc(std_ready, 1)

            def shifted(m, shift):
                for k in range(KT):
                    act.wait_ge(y_ready, KT * m + k + 1)
                    nc.scalar.activation(actH[:, k, :], sq[:, k, :], ACT.Identity, bias=mod[:, shift, k:k + 1]
                                         ).then_inc(h_ready, 1)

            if 1 in blocks:
                act.wait_ge(consts_in, 64)
                nc.scalar.activation(csig[:, :], cvec[:, :], ACT.Sigmoid).then_inc(csig_ready, 1)
                norm(0, x, lambda: act.wait_ge(x_in, 16))
                act.wait_ge(mod_ready, 1)
                shifted(0, 0)
                act.wait_ge(gw_in, 16)
                nc.scalar.activation(gwH[:, :, :], gw[:, :, :], ACT.Copy).then_inc(gw_hi, 1)
                layer("w_in", copy_to(proj))
                act.wait_ge(gate_done, 1)
                nc.scalar.activation(gate[:, :, :], ps[:, 5, 0:TT * GATES].rearrange("p (t g) -> p t g", t=TT),
                                     ACT.Sigmoid).then_inc(gate_ready, 1)
                for n in range(len(v_pairs)):
                    act.wait_ge(vT_done, n + 1)
                    nc.scalar.activation(vtok[:, 2 * n:2 * n + 2, :, :].rearrange("p a t d -> p (a t d)"),
                                         ps[:, 4 + n % 2, :], ACT.Copy).then_inc(vtok_ready, 1)
                act.wait_ge(cmp_bias, 1)
                for n in range(2):
                    nc.scalar.activation(chid[:, n, :], ps[:, 6, n * 32:n * 32 + GROUPS * NCMP], ACT.Sigmoid,
                                         bias=cbias[:, n:n + 1]).then_inc(cmp_sig, 1)
                act.wait_ge(cmp_kv, 1)
                nc.scalar.activation(kcT[:, :], ps[:, 7, 0:GROUPS * NCMP], ACT.Copy)
                for g in range(GROUPS):
                    nc.scalar.activation(vc[:, g, :], ps[0:NCMP, 7, 64 + g * P:64 + (g + 1) * P], ACT.Copy
                                         ).then_inc(cmp_ready, 1)

                def exps(b):
                    kind = subs[b][0]
                    act.wait_ge(masked, b + 1)
                    for t in range(TT):
                        for h in range(4):
                            p = pcmp[:, t, h, :] if kind == "cmp" else (probs0, probs1)[t][:, b % 2, h, :]
                            bias = nmx[:, b % 2, t, h:h + 1]
                            if kind == "cmp":
                                ins = nc.scalar.activation(p, p, ACT.Exp, bias=bias, scale=SCALE)
                            else:
                                ins = nc.scalar.activation(p, p, ACT.Exp, bias=bias, scale=SCALE,
                                                           accum_out=rsum[:, b % 2, t, h:h + 1])
                    ins.then_inc(exped, 1)

                def take_pT(b):
                    act.wait_ge(pT_done, 2 * b + 1)
                    if b:
                        act.wait_ge(pv_done, b)
                    if subs[b][0] == "cmp":
                        nc.scalar.activation(flat(pcT[:, :, :]), flat(ps[0:NCMP, 4:6, :]), ACT.Copy).then_inc(pT_ready, 2)
                        return
                    nc.scalar.activation(flat(pT0[:, :, :]), bank2(4), ACT.Copy).then_inc(pT_ready, 1)
                    act.wait_ge(pT_done, 2 * b + 2)
                    nc.scalar.activation(flat(pT1[:, :, :]), ps[:, 1, :], ACT.Copy).then_inc(pT_ready, 1)

                exps(0)
                for b in range(NSUB):
                    if b + 1 < NSUB:
                        exps(b + 1)
                    take_pT(b)
                    if subs[b][6]:
                        act.wait_ge(pv_done, b + 1)
                        g = out_of[b]
                        nc.scalar.activation(flat(actH[:, 4 * g:4 * g + 4, :]), bank2(6), ACT.Copy).then_inc(oH_ready, 1)
                layer("w_o", copy_to(o))
                norm(1, o, lambda: act.wait_ge(evacuated, emptied("w_o")))
                norm(2, x, lambda: act.wait_ge(x_ready, 1))
                shifted(1, 3)
                for h in range(2):
                    layer(f"up_{h}", square_relu(h))
                    layer(f"down_{h}")
                norm(3, o, lambda: act.wait_ge(evacuated, emptied("down_1")))

            def plain_high(m):
                act.wait_ge(yn_ready, m + 1)
                nc.scalar.activation(flat(actH[:, :, :]), flat(sq[:, :, :]), ACT.Copy).then_inc(hn_ready, 1)

            def rwkv_turn(i):
                def wait(s, per, j):
                    act.wait_ge(s, j + i * per)
                wait(lora_done, 1, 1)
                wait(mixed, 1, 1)
                for j in range(RJ):
                    nc.scalar.activation(sg[:, j, :], ps[:, 0, j * T:(j + 1) * T], ACT.Sigmoid, bias=rv[:, W0, j:j + 1])
                for j in range(RJ):
                    nc.scalar.activation(aa[:, j, :], ps[:, 1, j * T:(j + 1) * T], ACT.Sigmoid, bias=rv[:, A0, j:j + 1])
                nc.scalar.activation(flat(gg[:, :, :]), ps[:, 2, :], ACT.Copy).then_inc(sig_ready, 1)
                wait(kk_ready, 1, 1)
                nc.scalar.activation(flat(nrm[:, :, :]), flat(kk[:, :, :]), ACT.Square).then_inc(kksq, 1)
                wait(kksum, 1, 1)
                nc.scalar.activation(flat(nrm[:, :, :]), ps[:, 3, :], ACT.Sqrt, scale=float(RHEAD)).then_inc(nrm_ready, 1)
                wait(cs_ready, 1, 1)
                nc.scalar.activation(flat(Gd[:, :, :]), flat(cs[:, :, :]), ACT.Exp, scale=-DECAY)
                nc.scalar.activation(flat(Gi[:, :, :]), flat(cs[:, :, :]), ACT.Exp, scale=DECAY).then_inc(gexp, 1)
                wait(csp_ready, 1, 1)
                nc.scalar.activation(flat(Gp[:, :, :]), flat(cs[:, :, :]), ACT.Exp, scale=-DECAY).then_inc(gp_ready, 1)
                wait(tok_done, 3, 1)
                nc.scalar.activation(rtok[:, :, :, :].rearrange("p i j d -> p (i j d)"), ps[:, 4, :], ACT.Copy).then_inc(tok_ready, 1)
                for n, dst in enumerate((btok, ktok)):
                    wait(tok_done, 3, n + 2)
                    for c in range(2):
                        rows = slice(c * CHUNK, (c + 1) * CHUNK)
                        ins = nc.scalar.activation(dst[rows, c, :, :, :].rearrange("p i j d -> p (i j d)"), ps[rows, 5 + n, :],
                                                   ACT.Copy)
                    ins.then_inc(tok_ready, 1)
                wait(x1_done, 1, 1)
                nc.scalar.activation(flat(Xm[:, :, :]), bank2(0), ACT.Copy).then_inc(x1_ready, 1)
                for v in range(1, len(LEVELS)):
                    wait(w1_done, 5, v)
                    nc.scalar.activation(flat(W1[:, :, :]), bank2(0), ACT.Copy).then_inc(w1_ready, 1)
                for c in range(TT * 2):
                    wait(rhs_done, 4, c + 1)
                    nc.scalar.activation(rhs[:, :], ps[:, 0, 0:RHEADS * RHEAD], ACT.Copy).then_inc(rhs_ready, 1)
                    wait(u_done, 4, c + 1)
                    if c == 2:
                        wait(ysum_done, 2, 1)
                    rows = slice(c % 2 * CHUNK, (c % 2 + 1) * CHUNK)
                    nc.scalar.activation(uf[rows, :], ps[rows, 1, 0:RHEADS * RHEAD], ACT.Copy).then_inc(u_ready, 1)
                wait(ysum_done, 2, 2)
                nc.scalar.activation(flat(yb[:, :, :]), ps[:, 6, :], ACT.Copy).then_inc(yb_ready, 1)
                wait(yc_ready, 1, 1)
                nc.scalar.activation(flat(ysq[:, :, :]), flat(yb[:, :, :]), ACT.Square).then_inc(ysq_ready, 1)
                wait(var_done, 1, 1)
                nc.scalar.activation(flat(nrm[:, :, :]), ps[:, 7, :], ACT.Sqrt, bias=gn_eps).then_inc(gstd_ready, 1)
                wait(yc_out, 1, 1)
                nc.scalar.activation(flat(yH[:, bass.ds(2 * 4 + i * RJ, RJ), :]), flat(yb[:, :, :]), ACT.Copy).then_inc(ycH_ready, 1)

            if 2 in blocks:
                if 1 not in blocks:
                    act.wait_ge(consts_in, 64)
                norm(NB, x, lambda: act.wait_ge(x_ready, XB) if XB else act.wait_ge(x_in, 16))
                plain_high(0)
                layer("w_in2", copy_to(proj2))
                act.wait_ge(evacuated, emptied("w_in2"))
                act.wait_ge(c2_in, 32)
                u, e = cum[:, 0, :], cum[:, 1, :]
                chain(nc.scalar.activation(u, proj2[0:4, SPEC + 3, :], ACT.Identity, bias=b_forget))
                chain(nc.scalar.activation(e, u, ACT.Abs))
                chain(nc.scalar.activation(e, e, ACT.Exp, scale=-1.0))
                nc.scalar.activation(e, e, ACT.Ln, bias=ones[0:4, 0:1]).then_inc(f_log, 1)
                for n in range(4):
                    act.wait_ge(v2T_done, n + 1)
                    nc.scalar.activation(vtok2[:, 2 * n:2 * n + 2, :, :].rearrange("p a t d -> p (a t d)"), ps[:, 4 + n % 2, :],
                                         ACT.Copy).then_inc(v2_ready, 1)
                act.wait_ge(s2_masked, 1)
                for so, pr in ((soft0, prob0), (soft1, prob1)):
                    z, so_ = flat(pr[:, 0, :, :]), flat(so[:, :, :])
                    chain(nc.scalar.activation(so_, z, ACT.Abs, scale=SCALE))
                    chain(nc.scalar.activation(so_, so_, ACT.Exp, scale=-1.0))
                    chain(nc.scalar.activation(so_, so_, ACT.Ln, bias=ones[:, 0:1]))
                    nc.scalar.activation(flat(pr[:, 1, :, :]), z, ACT.Relu, scale=SCALE).then_inc(s2_soft, 1)
                act.wait_ge(s2_sub, 1)
                nc.scalar.activation(flat(prob0[:, 0, :, :]), flat(prob0[:, 0, :, :]), ACT.Exp)
                nc.scalar.activation(flat(prob1[:, 0, :, :]), flat(prob1[:, 0, :, :]), ACT.Exp).then_inc(s2_exp, 1)

                def take_t2(b):
                    act.wait_ge(t2_done, 2 * b + 1)
                    if b:
                        act.wait_ge(o2_done, b)
                    nc.scalar.activation(flat(qT0[:, :, :]), bank2(4), ACT.Copy).then_inc(t2_ready, 1)
                    act.wait_ge(t2_done, 2 * b + 2)
                    nc.scalar.activation(flat(qT1[:, :, :]), ps[:, 1, :], ACT.Copy).then_inc(t2_ready, 1)
                    act.wait_ge(o2_done, b + 1)
                    nc.scalar.activation(flat(yH[:, 4 * b:4 * b + 4, :]), bank2(6), ACT.Copy).then_inc(y2H_ready, 1)

                take_t2(0)
                act.wait_ge(s2_masked, 2)
                for t in range(TT):
                    for h in range(4):
                        p = (prob0, prob1)[t][:, 0, h, :]
                        ins = nc.scalar.activation(p, p, ACT.Exp, bias=nmx[:, 0, t, h:h + 1], scale=SCALE,
                                                   accum_out=rsum[:, 0, t, h:h + 1])
                ins.then_inc(s2_exp, 1)
                take_t2(1)
                act.wait_ge(spec_mixed, 1)
                nc.scalar.activation(proj2[0:64, SPEC, :], proj2[0:64, SPEC, :], ACT.Tanh)
                nc.scalar.activation(proj2[:, SPEC + 1, :], proj2[:, SPEC + 1, :], ACT.Sigmoid)
                nc.scalar.activation(proj2[96:P, SPEC + 2, :], proj2[96:P, SPEC + 2, :], ACT.Sigmoid).then_inc(spec_ready, 1)
                act.wait_ge(zeroed, 1)
                with act.Fori(0, RTURNS) as i:
                    act.wait_ge(turn_done, i + 1)
                    rwkv_turn(i)
                act.wait_ge(turn_done, RTURNS + 1)
                layer("gates2", copy_to(gates, ACT.Sigmoid))

                def mix_high(name, i, r):
                    act.wait_ge(mix_ready, 1 + r + i * 2)
                    nc.scalar.activation(flat(actH[:, bass.ds(GT * r + i * (2 * GT), GT), :]), mix[:, :], ACT.Copy
                                         ).then_inc(mixH_ready, 1)

                layer("branch", mix_high)
                layer("w_out2", copy_to(o))
                norm(NB + 1, o, lambda: act.wait_ge(evacuated, emptied("w_out2")))
                norm(NB + 2, x, lambda: act.wait_ge(x_ready, XB + 1))
                plain_high(1)
                for h in range(2):
                    layer(f"up2_{h}", square_relu(h))
                    layer(f"down2_{h}")
                norm(NB + 3, o, lambda: act.wait_ge(evacuated, emptied("down2_1")))

        @block.vector
        def _(dve):
            link = Chain(dve, dve_chain)
            dve.sem_inc(wl_ready, RAW)
            dve.sem_inc(hidL_ready, 1)

            def split(name, i, r, s):
                slot, _ = raw_loads(name, i, r, s)
                l = lin(name, i, r, s)
                b = s % SPLIT if L[name]["spg"] > 1 else r % SPLIT
                dve.wait_ge(wh_ready, l + 1)
                dve.wait_ge(step_done, l + 1)
                nc.vector.tensor_tensor(wL[:, b, :, :], raw[:, slot, :, :], wH[:, b, :, :].bitcast(F32),
                                        ALU.subtract).then_inc(wl_ready, 1)

            def layer(name, evac=None):
                spg = L[name]["spg"]

                def body(i, r):
                    for s in range(spg):
                        split(name, i, r, s)
                        if evac and s == min(2, spg - 1) and not (isinstance(i, int) and i == 0 and r == 0):
                            evac(name, i, r - 1)

                over_groups(dve, name, 1, body)
                if evac:
                    n, U = L[name]["groups"], L.unroll(name)
                    i = (n - 2) // U
                    evac(name, i, n - 1 - i * U)

            def add_to(dst):
                def evac(name, i, r):
                    dve.wait_ge(step_done, SPLIT + lin(name, i, r, L[name]["spg"] - 1) + 1)
                    d = flat(dst[:, bass.ds(GT * r + i * (GT * L.unroll(name)), GT), :])
                    nc.vector.tensor_tensor(d, bank2(acc(name, r)), d, ALU.add).then_inc(evacuated, 1)
                return evac

            def hidden_low(name, i, r):
                dve.wait_ge(hidH_ready, grp(name, i, r) - up_groups_before[name] + 1)
                at_ = bass.ds(GT * r + i * (GT * L.unroll(name)), GT)
                nc.vector.tensor_tensor(flat(hidL[:, at_, :]), hid[:, :], flat(hidH[:, at_, :]).bitcast(F32),
                                        ALU.subtract).then_inc(hidL_ready, 1)

            def scaled(n, src, dst, c, sig=None):
                dve.wait_ge(std_ready, n + 1)
                link(nc.vector.reciprocal(std[:, :], std[:, :]))
                for k in range(KT):
                    ins = nc.vector.scalar_tensor_tensor(dst[:, k, :], src[:, k, :], coef[:, c, k:k + 1], std[:, :],
                                                         ALU.mult, ALU.mult)
                    if sig is not None:
                        ins.then_inc(sig, 1)
                    elif k == KT - 1:
                        link(ins)

            def shifted_low(m, shift):
                for k in range(KT):
                    dve.wait_ge(h_ready, KT * m + k + 1)
                    ins = nc.vector.scalar_tensor_tensor(actL[:, k, :], sq[:, k, :], mod[:, shift, k:k + 1],
                                                         actH[:, k, :].bitcast(F32), ALU.add, ALU.subtract)
                ins.then_inc(act_ready, 1)

            def residual():
                nc.vector.tensor_tensor(flat(x[:, :, :]), flat(x[:, :, :]), flat(o[:, :, :]), ALU.add).then_inc(x_ready, 1)

            if 1 in blocks:
                dve.wait_ge(csig_ready, 1)
                nc.vector.tensor_tensor(csig[:, :], csig[:, :], cvec[:, :], ALU.mult).then_inc(csilu_ready, 1)
                dve.wait_ge(ada_done, RAW + 32)
                psm = ps[:, 0, 0:6 * KT].rearrange("p (j k) -> p j k", k=KT)
                ins = nc.vector.tensor_tensor(mod[:, 0:2, :], psm[:, 0:2, :], b_ada[:, 0:2, :], ALU.add)
                link(ins)
                dve.sem_inc(mod_ready, 1)
                link(nc.vector.scalar_tensor_tensor(coef[:, 0, :], mod[:, 1, :], 1.0, vecs[:, 0, :], ALU.add, ALU.mult))
                scaled(0, x, sq, 0, y_ready)
                shifted_low(0, 0)
                dve.wait_ge(gw_hi, 1)
                nc.vector.tensor_tensor(gwL[:, :, :], gw[:, :, :], gwH[:, :, :].bitcast(F32), ALU.subtract
                                        ).then_inc(gw_lo, 1)
                layer("w_in")
                for n, p in enumerate(rope_pairs):
                    dve.wait_ge(rotated, n + 1)
                    link(nc.vector.tensor_tensor(rope_s[:, n % 2, :, :], ps[:, n % 2, :].rearrange("p (a t) -> p a t", a=2),
                                                 sin.unsqueeze(1).to_broadcast([P, 2, T]), ALU.mult))
                    dve.wait_ge(rope_cos, n + 1)
                    nc.vector.tensor_tensor(proj[:, p:p + 2, :], rope_s[:, n % 2, :, :], rope_c[:, n % 2, :, :],
                                            ALU.add).then_inc(roped, 1)
                dve.wait_ge(cmp_sum, 1)
                link(nc.vector.tensor_copy(cbias[:, :], ps[:, 6, 64:66]))
                dve.sem_inc(cmp_bias, 1)
                dve.wait_ge(cmp_sig, 2)
                for n in range(2):
                    nc.vector.scalar_tensor_tensor(chid[:, n, :], ps[:, 6, n * 32:n * 32 + GROUPS * NCMP], cbias[:, n:n + 1],
                                                   chid[:, n, :], ALU.add, ALU.mult).then_inc(cmp_hid, 1)

                def mask_max(b):
                    dve.wait_ge(scores, b + 1)
                    if b >= 2:
                        dve.wait_ge(pT_done, 2 * (b - 1))
                    if subs[b][0] == "cmp":
                        s = ps[:, 1, 0:TT * 4 * NCMP].rearrange("p (t h n) -> p t h n", t=TT, h=4)
                        for t in range(TT):
                            ins = nc.vector.tensor_tensor(pcmp[:, t, :, :], s[:, t, :, :],
                                                          unseen[:, t, :].unsqueeze(1).to_broadcast([P, 4, NCMP]), ALU.add)
                        link(ins)
                        for t in range(TT):
                            ins = nc.vector.tensor_reduce(nmx[:, b % 2, t, :], pcmp[:, t, :, :], AX.X, ALU.max)
                    else:
                        nc.vector.tensor_tensor(probs0[:, b % 2, :, :], ps[:, 1, :].rearrange("p (h n) -> p h n", h=4),
                                                causal[:, P:2 * P].unsqueeze(1).to_broadcast([P, 4, P]), ALU.add)
                        link(nc.vector.tensor_tensor(probs1[:, b % 2, :, :], bank2(2).rearrange("p (h n) -> p h n", h=4),
                                                     causal.unsqueeze(1).to_broadcast([P, 4, T]), ALU.add))
                        nc.vector.tensor_reduce(nmx[:, b % 2, 0, :], probs0[:, b % 2, :, :], AX.X, ALU.max)
                        ins = nc.vector.tensor_reduce(nmx[:, b % 2, 1, :], probs1[:, b % 2, :, :], AX.X, ALU.max)
                    link(ins)
                    nc.vector.tensor_scalar(nmx[:, b % 2, :, :], nmx[:, b % 2, :, :], -SCALE, None, ALU.mult
                                            ).then_inc(masked, 1)

                def weights_of(b):
                    kind, q, _, _, gk, _, _ = subs[b]
                    dve.wait_ge(exped, b + 1)
                    if kind == "cmp":
                        for t in range(TT):
                            ins = nc.vector.tensor_tensor(pcmp[:, t, :, :], pcmp[:, t, :, :],
                                                          seen[:, t, :].unsqueeze(1).to_broadcast([P, 4, NCMP]), ALU.mult)
                        link(ins)
                        for t in range(TT):
                            ins = nc.vector.tensor_reduce(rsum[:, b % 2, t, :], pcmp[:, t, :, :], AX.X, ALU.add)
                        link(ins)
                    r = rsum[:, b % 2, :, :]
                    link(nc.vector.tensor_scalar(r, r, 1e-30, None, ALU.max))
                    ins = nc.vector.reciprocal(r, r)
                    if gk is not None:
                        link(ins)
                        gt = gate[:, :, :].rearrange("p t (h c) -> p t h c", c=3)[:, :, q:q + 4, gk]
                        ins = nc.vector.tensor_tensor(r, r, gt, ALU.mult)
                    ins.then_inc(weight, 1)

                dve.wait_ge(gate_ready, 1)
                mask_max(0)
                for b in range(NSUB):
                    if b + 1 < NSUB:
                        mask_max(b + 1)
                    weights_of(b)
                    if subs[b][6]:
                        g = out_of[b]
                        dve.wait_ge(oH_ready, g + 1)
                        nc.vector.tensor_tensor(flat(actL[:, 4 * g:4 * g + 4, :]), bank2(6),
                                                flat(actH[:, 4 * g:4 * g + 4, :]).bitcast(F32), ALU.subtract
                                                ).then_inc(oL_ready, 1)
                dve.wait_ge(ada_done, RAW + 96)
                link(nc.vector.tensor_tensor(mod[:, 2:6, :], psm[:, 2:6, :], b_ada[:, 2:6, :], ALU.add))
                dve.sem_inc(mod_ready, 1)
                nc.vector.tensor_tensor(coef[:, 1, :], mod[:, 2, :], vecs[:, 1, :], ALU.mult)
                nc.vector.scalar_tensor_tensor(coef[:, 2, :], mod[:, 4, :], 1.0, vecs[:, 2, :], ALU.add, ALU.mult)
                link(nc.vector.tensor_tensor(coef[:, 3, :], mod[:, 5, :], vecs[:, 3, :], ALU.mult))
                layer("w_o")
                scaled(1, o, o, 1)
                residual()
                scaled(2, x, sq, 2, y_ready)
                shifted_low(1, 3)
                link(nc.vector.memset(flat(o[:, :, :]), 0.0))
                for h in range(2):
                    layer(f"up_{h}", hidden_low)
                    layer(f"down_{h}", add_to(o))
                scaled(3, o, o, 3)
                residual()

            def plain_low(m):
                dve.sem_inc(yn_ready, 1)
                dve.wait_ge(hn_ready, m + 1)
                nc.vector.tensor_tensor(flat(actL[:, :, :]), flat(sq[:, :, :]), flat(actH[:, :, :]).bitcast(F32), ALU.subtract
                                        ).then_inc(act_ready, 1)

            def rwkv_turn(i):
                def wait(s, per, j):
                    dve.wait_ge(s, j + i * per)
                half = [slice(0, RHEAD), slice(RHEAD, P)]
                link(nc.vector.tensor_copy(rv[:, :, :], rwv10[:, :, bass.ds(i * RJ, RJ)]))
                link(nc.vector.memset(flat(ST[:, :, :]), 0.0))
                wait(shifted_z, 1, 1)
                for dst, d, m, base in ((rr, d0, MU_R, RR), (rk, d1, MU_K, RK), (rvv, d2, MU_V, RV)):
                    for j in range(RJ):
                        ins = nc.vector.scalar_tensor_tensor(dst[:, j, :], d[:, j, :], rv[:, m, j:j + 1],
                                                             proj2[:, bass.ds(base + j + i * RJ, 1), :].rearrange("p a t -> p (a t)"),
                                                             ALU.mult, ALU.add)
                link(ins)
                dve.sem_inc(mixed, 1)
                for j in range(RJ):
                    ins = nc.vector.tensor_scalar(kk[:, j, :], rk[:, j, :], rv[:, K_K, j:j + 1], None, ALU.mult)
                link(ins)
                dve.sem_inc(kk_ready, 1)
                wait(sig_ready, 1, 1)
                for j in range(RJ):
                    ins = nc.vector.tensor_tensor_scan(cs[:, j, :], reset, sg[:, j, :], 0.0, ALU.mult, ALU.add)
                link(ins)
                dve.sem_inc(cs_ready, 1)
                for j in range(RJ):
                    ins = nc.vector.tensor_scalar(k2[:, j, :], aa[:, j, :], 1.0, rv[:, K_A, j:j + 1], ALU.subtract, ALU.mult)
                link(ins)
                link(nc.vector.scalar_tensor_tensor(flat(k2[:, :, :]), flat(k2[:, :, :]), 1.0, flat(rk[:, :, :]), ALU.add, ALU.mult))
                dve.sem_inc(k2_ready, 1)
                wait(gexp, 1, 1)
                link(nc.vector.tensor_tensor(flat(cs[:, :, :]), flat(cs[:, :, :]), flat(sg[:, :, :]), ALU.subtract))
                dve.sem_inc(csp_ready, 1)
                wait(nrm_ready, 1, 1)
                link(nc.vector.tensor_scalar(flat(nrm[:, :, :]), flat(nrm[:, :, :]), 1e-12, None, ALU.max))
                link(nc.vector.reciprocal(flat(nrm[:, :, :]), flat(nrm[:, :, :])))
                link(nc.vector.tensor_tensor(flat(kk[:, :, :]), flat(kk[:, :, :]), flat(nrm[:, :, :]), ALU.mult))
                dve.sem_inc(kkn_ready, 1)
                link(nc.vector.tensor_tensor(flat(KTt[:, :, :]), flat(k2[:, :, :]), flat(Gi[:, :, :]), ALU.mult))
                wait(gp_ready, 1, 1)
                for h, part in enumerate(half):
                    ins = nc.vector.scalar_tensor_tensor(AR[h][part, :, :, 0, :].rearrange("p j i t -> p (j i) t"),
                                                         kk[part, :, :].rearrange("p j (i t) -> p (j i) t", i=TT), -1.0,
                                                         Gp[part, :, :].rearrange("p j (i t) -> p (j i) t", i=TT), ALU.mult, ALU.mult)
                link(ins)
                dve.sem_inc(a_ready, 1)
                wait(rk_ready, 1, 1)
                for j in range(RJ):
                    ins = nc.vector.tensor_scalar(rkk[:, j, :], rkk[:, j, :], rv[:, R_K, j:j + 1], None, ALU.mult)
                link(ins)
                dve.sem_inc(rk_scaled, 1)
                wait(bonus_sum, 1, 1)
                link(nc.vector.scalar_tensor_tensor(flat(bonus[:, :, :]), ps[:, 7, :], float(RHEAD), flat(rvv[:, :, :]),
                                                    ALU.mult, ALU.mult))
                dve.sem_inc(bonus_ready, 1)
                for n, dst in enumerate((Bc, Kc)):
                    for h in range(RHEADS):
                        wait(mat_done, 8, 4 * n + h + 1)
                        nc.vector.tensor_tensor(dst[:, 2 * h:2 * h + 2, :], ps[:, 4 * n + h, :].rearrange("p (i c) -> p i c", i=TT),
                                                token_mask.unsqueeze(1).to_broadcast([P, TT, 2 * P]), ALU.mult).then_inc(mat_masked, 1)
                wait(mat_masked, 8, 8)
                lab = Bc[:, :, 0:P]
                link(nc.vector.tensor_tensor(Ym[:, :, :], lab, level_mask[:, 0, :].unsqueeze(1).to_broadcast([P, MATS, P]), ALU.mult))
                link(nc.vector.tensor_tensor(Ym[:, :, :], Ym[:, :, :], ident.unsqueeze(1).to_broadcast([P, MATS, P]), ALU.add))
                dve.sem_inc(y1_ready, 1)
                for v in range(1, len(LEVELS)):
                    wait(dx_done, 5, v)
                    if v < len(LEVELS) - 1:
                        nc.vector.tensor_tensor(flat(Xm[:, :, :]), flat(Xm[:, :, :]), bank2(2), ALU.add)
                    nc.vector.tensor_tensor(flat(Ym[:, :, :]), flat(Ym[:, :, :]), bank2(4), ALU.add).then_inc(level_ready, 1)
                for c in range(TT * 2):
                    wait(s_done, 4, c + 1)
                    link(nc.vector.tensor_tensor(flat(ST[:, :, :]), flat(ST[:, :, :]), ps[:, 2, 0:RJ * P], ALU.add))
                    end = (c + 1) * CHUNK - 1
                    link(nc.vector.tensor_tensor(ST[:, :, :], ST[:, :, :], Gd[:, :, end:end + 1].to_broadcast([P, RJ, P]), ALU.mult))
                    dve.sem_inc(st_ready, 1)
                wait(mean_done, 1, 1)
                link(nc.vector.tensor_tensor(flat(yb[:, :, :]), flat(yb[:, :, :]), ps[:, 7, :], ALU.subtract))
                dve.sem_inc(yc_ready, 1)
                wait(gstd_ready, 1, 1)
                link(nc.vector.reciprocal(flat(nrm[:, :, :]), flat(nrm[:, :, :])))
                link(nc.vector.tensor_tensor(flat(yb[:, :, :]), flat(yb[:, :, :]), flat(nrm[:, :, :]), ALU.mult))
                for j in range(RJ):
                    ins = nc.vector.tensor_scalar(yb[:, j, :], yb[:, j, :], rv[:, LN_W, j:j + 1], rv[:, LN_B, j:j + 1],
                                                  ALU.mult, ALU.add)
                link(ins)
                link(nc.vector.tensor_tensor(flat(yb[:, :, :]), flat(yb[:, :, :]), flat(bonus[:, :, :]), ALU.add))
                link(nc.vector.tensor_tensor(flat(yb[:, :, :]), flat(yb[:, :, :]), flat(gg[:, :, :]), ALU.mult))
                dve.sem_inc(yc_out, 1)
                wait(ycH_ready, 1, 1)
                at_ = bass.ds(2 * 4 + i * RJ, RJ)
                link(nc.vector.tensor_tensor(flat(yL[:, at_, :]), flat(yb[:, :, :]), flat(yH[:, at_, :]).bitcast(F32), ALU.subtract))
                dve.sem_inc(turn_done, 1)

            if 2 in blocks:
                if 1 not in blocks:
                    dve.wait_ge(consts_in, 64)
                nc.vector.tensor_copy(coef[:, 4:8, :], vecs[:, 4:8, :])
                scaled(NB, x, sq, 4)
                plain_low(0)
                layer("w_in2")
                u, e, up, dn = (cum[:, n, :] for n in range(4))
                dve.wait_ge(f_log, 1)
                link(nc.vector.tensor_scalar(u, u, -1.0, 0.0, ALU.mult, ALU.max))
                link(nc.vector.tensor_tensor(e, e, u, ALU.add))
                link(nc.vector.tensor_tensor_scan(u, ones[0:4, 0:1].to_broadcast([4, T]), e, 0.0, ALU.mult, ALU.add))
                nc.vector.tensor_scalar(up, u, 1.0 / SCALE, None, ALU.mult)
                link(nc.vector.tensor_scalar(dn, u, -1.0 / SCALE, None, ALU.mult))
                dve.sem_inc(cum_ready, 1)

                def masked2(b, mask):
                    dve.wait_ge(s2_done, b + 1)
                    nc.vector.tensor_tensor(prob0[:, 0, :, :], ps[:, 1, :].rearrange("p (h n) -> p h n", h=4),
                                            mask[:, P:2 * P].unsqueeze(1).to_broadcast([P, 4, P]), ALU.add)
                    link(nc.vector.tensor_tensor(prob1[:, 0, :, :], bank2(2).rearrange("p (h n) -> p h n", h=4),
                                                 mask.unsqueeze(1).to_broadcast([P, 4, T]), ALU.add))

                masked2(0, strict)
                dve.sem_inc(s2_masked, 1)
                for n, (so, pr, w) in enumerate(((soft0, prob0, P), (soft1, prob1, T))):
                    dve.wait_ge(s2_soft, n + 1)
                    link(nc.vector.tensor_tensor(flat(pr[:, 1, :, :]), flat(pr[:, 1, :, :]), flat(so[:, :, :]), ALU.add))
                    for h in range(4):
                        ins = nc.vector.tensor_tensor_scan(so[:, h, ::-1], ones[:, 0:1].to_broadcast([P, w]), pr[:, 1, h, ::-1], 0.0,
                                                           ALU.mult, ALU.add)
                    link(ins)
                    link(nc.vector.scalar_tensor_tensor(flat(pr[:, 0, :, :]), flat(pr[:, 0, :, :]), SCALE, flat(so[:, :, :]),
                                                        ALU.mult, ALU.subtract))
                dve.sem_inc(s2_sub, 1)

                def y_low(b):
                    dve.wait_ge(y2H_ready, b + 1)
                    nc.vector.tensor_tensor(flat(yL[:, 4 * b:4 * b + 4, :]), bank2(6), flat(yH[:, 4 * b:4 * b + 4, :]).bitcast(F32),
                                            ALU.subtract).then_inc(y2L_ready, 1)

                y_low(0)
                masked2(1, causal)
                nc.vector.tensor_reduce(nmx[:, 0, 0, :], prob0[:, 0, :, :], AX.X, ALU.max)
                link(nc.vector.tensor_reduce(nmx[:, 0, 1, :], prob1[:, 0, :, :], AX.X, ALU.max))
                link(nc.vector.tensor_scalar(nmx[:, 0, :, :], nmx[:, 0, :, :], -SCALE, None, ALU.mult))
                dve.sem_inc(s2_masked, 1)
                dve.wait_ge(s2_exp, 2)
                link(nc.vector.reciprocal(rsum[:, 0, :, :], rsum[:, 0, :, :]))
                dve.sem_inc(s2_weight, 1)
                y_low(1)
                dve.wait_ge(y2L_ready, 2)
                z = proj2[:, SPEC:SPEC + 3, :]
                d = at_spec[:, :, :]
                nc.vector.tensor_tensor(d[:, :, 1:T], z[:, :, 0:T - 1], z[:, :, 1:T], ALU.subtract)
                link(nc.vector.tensor_scalar(d[:, :, 0:1], z[:, :, 0:1], -1.0, None, ALU.mult))
                for j in range(3):
                    ins = nc.vector.scalar_tensor_tensor(z[:, j, :], d[:, j, :], mu_spec[:, j:j + 1], z[:, j, :], ALU.mult, ALU.add)
                link(ins)
                dve.sem_inc(spec_mixed, 1)
                for t_ in (AR[0], AR[1], btok, ktok):
                    ins = nc.vector.memset(t_[:, :, :, :, :], 0.0)
                link(nc.vector.memset(uf[:, :], 0.0))
                dve.sem_inc(zeroed, 1)
                dve.sem_inc(turn_done, 1)
                n0, K = link.n, RWKV_LINKS
                with dve.Fori(0, RTURNS) as i:
                    link.off = i * K
                    rwkv_turn(i)
                assert link.n - n0 == K, link.n - n0
                link.n, link.off = n0 + RTURNS * K, 0
                dve.wait_ge(turn_done, RTURNS + 1)
                layer("gates2")

                def gated(n, name, i, r):
                    dve.wait_ge(step_done, SPLIT + lin(name, i, r, (0, 1, 3)[n]) + 1)
                    g = flat(gates[:, bass.ds(16 * n + GT * r + i * (2 * GT), GT), :])
                    if n == 0:
                        nc.vector.tensor_tensor(mix[:, :], bank2(0), g, ALU.mult).then_inc(branch_used, 1)
                        return
                    nc.vector.tensor_tensor(mix_t[:, :], bank2(2 * n), g, ALU.mult).then_inc(branch_used, 1)
                    dve.wait_ge(branch_used, 3 * r + n + 1 + i * 6)
                    ins = nc.vector.tensor_tensor(mix[:, :], mix[:, :], mix_t[:, :], ALU.add)
                    if n == 1:
                        ins.then_inc(mixL_ready, 1)
                        dve.wait_ge(mixL_ready, 2 * r + 1 + i * 4)
                        return
                    ins.then_inc(mix_ready, 1)
                    dve.wait_ge(mixH_ready, r + 1 + i * 2)
                    at_ = bass.ds(GT * r + i * (2 * GT), GT)
                    nc.vector.tensor_tensor(flat(actL[:, at_, :]), mix[:, :], flat(actH[:, at_, :]).bitcast(F32), ALU.subtract
                                            ).then_inc(mixL_ready, 1)
                    dve.wait_ge(mixL_ready, 2 * r + 2 + i * 4)
                    dve.sem_inc(evacuated, 1)

                dve.wait_ge(evacuated, emptied("gates2"))

                def branch(i, r):
                    split("branch", i, r, 0)
                    split("branch", i, r, 1)
                    if not (isinstance(i, int) and i == 0 and r == 0):
                        gated(2, "branch", i, r - 1)
                    split("branch", i, r, 2)
                    gated(0, "branch", i, r)
                    split("branch", i, r, 3)
                    gated(1, "branch", i, r)

                over_groups(dve, "branch", 1, branch)
                gated(2, "branch", 1, 1)
                layer("w_out2")
                scaled(NB + 1, o, o, 5)
                residual()
                scaled(NB + 2, x, sq, 6)
                plain_low(1)
                link(nc.vector.memset(flat(o[:, :, :]), 0.0))
                for h in range(2):
                    layer(f"up2_{h}", hidden_low)
                    layer(f"down2_{h}", add_to(o))
                scaled(NB + 3, o, o, 7)
                residual()

        @block.gpsimd
        def _(pool):
            if 1 in blocks:
                pool.wait_ge(c1_in, 16)
                pool.wait_ge(evacuated, emptied("w_in"))
                for n, p in enumerate(rope_pairs):
                    if n >= 2:
                        pool.wait_ge(roped, n - 1)
                    nc.gpsimd.tensor_tensor(rope_c[:, n % 2, :, :], proj[:, p:p + 2, :],
                                            cos.unsqueeze(1).to_broadcast([P, 2, T]), ALU.mult).then_inc(rope_cos, 1)
                for b in range(NSUB):
                    pool.wait_ge(weight, b + 1)
                    for t in range(TT):
                        p = pcmp[:, t, :, :] if subs[b][0] == "cmp" else (probs0, probs1)[t][:, b % 2, :, :]
                        ins = nc.gpsimd.tensor_tensor(p, p, rsum[:, b % 2, t, :].unsqueeze(2).to_broadcast(list(p.shape)),
                                                      ALU.mult)
                    ins.then_inc(probs_ready, 1)
            if 2 in blocks:
                pool.wait_ge(s2_weight, 1)
                for t in range(TT):
                    p = (prob0, prob1)[t][:, 0, :, :]
                    ins = nc.gpsimd.tensor_tensor(p, p, rsum[:, 0, t, :].unsqueeze(2).to_broadcast(list(p.shape)), ALU.mult)
                ins.then_inc(s2_probs, 1)
                pool.wait_ge(zeroed, 1)
                half = [slice(0, RHEAD), slice(RHEAD, P)]
                with pool.Fori(0, RTURNS) as i:
                    pool.wait_ge(turn_done, i + 1)
                    for d, base in ((d0, RR), (d1, RK), (d2, RV)):
                        z = proj2[:, bass.ds(base + i * RJ, RJ), :]
                        nc.gpsimd.tensor_tensor(d[:, :, 0:1], causal[:, 0:RJ].unsqueeze(2), z[:, :, 0:1], ALU.subtract)
                        ins = nc.gpsimd.tensor_tensor(d[:, :, 1:T], z[:, :, 0:T - 1], z[:, :, 1:T], ALU.subtract)
                    ins.then_inc(shifted_z, 1)
                    pool.wait_ge(mixed, 1 + i)
                    pool.wait_ge(gexp, 1 + i)
                    for h, part in enumerate(half):
                        for j in range(RJ):
                            nc.gpsimd.tensor_tensor(AR[h][part, j, :, 1, :], rr[part, j, :].rearrange("p (i t) -> p i t", i=TT),
                                                    Gd[part, j, :].rearrange("p (i t) -> p i t", i=TT), ALU.mult
                                                    ).then_inc(r_ready, 1)
                    pool.wait_ge(r_ready, 2 * RJ + i * (2 * RJ))
                    pool.wait_ge(kkn_ready, 1 + i)
                    pool.wait_ge(csp_ready, 1 + i)
                    nc.gpsimd.tensor_tensor(flat(ka[:, :, :]), flat(kk[:, :, :]), flat(aa[:, :, :]), ALU.mult).then_inc(pool_chain, 1)
                    pool.wait_ge(pool_chain, 1 + i)
                    nc.gpsimd.tensor_tensor(flat(BT[:, :, :]), flat(ka[:, :, :]), flat(Gi[:, :, :]), ALU.mult).then_inc(b_ready, 1)
                    pool.wait_ge(k2_ready, 1 + i)
                    nc.gpsimd.tensor_tensor(flat(rkk[:, :, :]), flat(rr[:, :, :]), flat(k2[:, :, :]), ALU.mult).then_inc(rk_ready, 1)
                    pool.wait_ge(mat_masked, 4 + i * 8)
                    for v in range(1, len(LEVELS)):
                        if v > 2:
                            pool.wait_ge(w1_done, v - 2 + i * 5)
                        nc.gpsimd.tensor_tensor(Lm[:, v % 2, :, :], Bc[:, :, 0:P],
                                                level_mask[:, v, :].unsqueeze(1).to_broadcast([P, MATS, P]), ALU.mult
                                                ).then_inc(lm_ready, 1)

        @block.tensor
        def _(pe):
            pe.sem_inc(step_done, SPLIT)
            pe.sem_inc(evacuated, 2)
            pe.sem_inc(ada_done, RAW)

            def norm(n):
                pe.wait_ge(sq_ready, n + 1)
                for k in range(KT):
                    ins = nc.tensor.matmul(ps[:, 4, 0:T], ones, sq[:, k, :], start=(k == 0), stop=(k == KT - 1))
                ins.then_inc(ssum_ready, 1)

            def ada(name, g_from, g_to):
                l = L[name]

                def body(i):
                    for s in range(4):
                        slot, count = s, 16 * (l["t0"] // RAW + 1) + i * 16
                        pe.wait_ge(raw_in[slot], count)
                        for k in range(STEP_K):
                            for n in range(GT):
                                col = L["ada_a"]["groups"] * GT * (name == "ada_b") + n + i * GT
                                ins = nc.tensor.matmul(ps[:, 0, bass.ds(col, 1)], raw[:, slot, k, n * P:(n + 1) * P],
                                                       csig[:, s * STEP_K + k:s * STEP_K + k + 1],
                                                       start=(s == 0 and k == 0 and n == 0), stop=(s == 3 and k == STEP_K - 1),
                                                       skip_group_check=True)
                        ins.then_inc(ada_done, 1)

                with pe.Fori(g_from, g_to) as i:
                    body(i)

            def layer(name, xH, xL, k0=0):
                spg = L[name]["spg"]
                pe.wait_ge(evacuated, 2 + L[name]["g0"])

                def body(i, r):
                    pe.wait_ge(evacuated, grp(name, i, r) + 1)
                    for s in range(spg):
                        pe.wait_ge(wl_ready, RAW + lin(name, i, r, s) + 1)
                        b = s % SPLIT if spg > 1 else r % SPLIT
                        for k in range(STEP_K):
                            kk = s * STEP_K + k
                            for n in range(GT):
                                out = ps[:, acc(name, r) + n // 2, (n % 2) * T:(n % 2 + 1) * T]
                                cols = slice(n * P, (n + 1) * P)
                                for j, (w, v) in enumerate(((wH, xH), (wH, xL), (wL, xH))):
                                    ins = nc.tensor.matmul(out, w[:, b, k, cols], v[:, k0 + kk, :],
                                                           start=(kk == 0 and j == 0 and n % 2 == 0),
                                                           stop=(kk == STEP_K * spg - 1 and j == 2), skip_group_check=True)
                        ins.then_inc(step_done, 1)

                over_groups(pe, name, 0, body)

            if 1 in blocks:
                pe.wait_ge(consts_in, 64)
                norm(0)
                pe.wait_ge(csilu_ready, 1)
                ada("ada_a", 0, 8)
                pe.wait_ge(act_ready, 1)
                layer("w_in", actH, actL)
                pe.wait_ge(gw_lo, 1)
                for t in range(TT):
                    for k in range(KT):
                        for j, (v, w) in enumerate(((actH, gwH), (actL, gwH), (actH, gwL))):
                            ins = nc.tensor.matmul(ps[:, 5, t * GATES:(t + 1) * GATES], v[:, k, t * P:(t + 1) * P], w[:, k, :],
                                                   start=(t == 0 and k == 0 and j == 0), stop=(k == KT - 1 and j == 2),
                                                   skip_group_check=True)
                ins.then_inc(gate_done, 1)
                pe.wait_ge(evacuated, emptied("w_in"))
                pe.wait_ge(c1_in, 16)
                for n, p in enumerate(rope_pairs):
                    if n >= 2:
                        pe.wait_ge(roped, n - 1)
                    nc.tensor.matmul(ps[:, n % 2, :], rot, flat(proj[:, p:p + 2, :]), start=True, stop=True
                                     ).then_inc(rotated, 1)
                pe.wait_ge(gate_ready, 1)
                for n, p in enumerate(v_pairs):
                    if n >= 2:
                        pe.wait_ge(vtok_ready, n - 1)
                    for j in range(2):
                        for t in range(TT):
                            c = (2 * j + t) * P
                            ins = nc.tensor.transpose(ps[:, 4 + n % 2, c:c + P], proj[:, p + j, t * P:(t + 1) * P], ident)
                    ins.then_inc(vT_done, 1)
                pe.wait_ge(roped, 5)
                pe.wait_ge(cmp_in, 80)
                first = True
                for n, p in enumerate((KC, VC)):
                    for l in range(CMP_LEN):
                        blocks_ = proj[:, p:p + 2, l:l + CMP_STRIDE * (NCMP - 1) + 1:CMP_STRIDE]
                        nc.tensor.matmul(ps[:, 6, n * 32:n * 32 + GROUPS * NCMP], cw1[:, n, l, :], blocks_,
                                         start=first, stop=(l == CMP_LEN - 1), skip_group_check=True)
                        first = False
                        ins = nc.tensor.matmul(ps[:, 6, 64 + n:65 + n], cw1[:, n, l, :], posk[:, n, l:l + 1],
                                               start=False, stop=(l == CMP_LEN - 1), skip_group_check=True)
                ins.then_inc(cmp_sum, 1)
                pe.wait_ge(cmp_hid, 2)
                nc.tensor.matmul(ps[:, 7, 0:GROUPS * NCMP], cw2[:, 0, :], chid[:, 0, :], start=True, stop=True,
                                 skip_group_check=True)
                for g in range(GROUPS):
                    ins = nc.tensor.matmul(ps[0:NCMP, 7, 64 + g * P:64 + (g + 1) * P], chid[:, 1, g * NCMP:(g + 1) * NCMP],
                                           cw2[:, 1, :], start=False, stop=True, skip_group_check=True)
                ins.then_inc(cmp_kv, 1)

                def score(b):
                    kind, q, kt, _, _, _, _ = subs[b]
                    if b >= 1:
                        pe.wait_ge(masked, b)
                    if b >= 2:
                        pe.wait_ge(pT_ready, 2 * (b - 1))
                    if kind == "cmp":
                        for t in range(TT):
                            for h in range(4):
                                c = (t * 4 + h) * NCMP
                                ins = nc.tensor.matmul(ps[:, 1, c:c + NCMP], proj[:, q + h, t * P:(t + 1) * P],
                                                       kcT[:, kt * NCMP:(kt + 1) * NCMP], start=(t == 0 and h == 0), stop=True,
                                                       skip_group_check=True)
                    else:
                        for h in range(4):
                            nc.tensor.matmul(ps[:, 1, h * P:(h + 1) * P], proj[:, q + h, 0:P], proj[:, kt[h], 0:P],
                                             start=(h == 0), stop=True, skip_group_check=True)
                        for h in range(4):
                            ins = nc.tensor.matmul(ps[:, 2 + h // 2, (h % 2) * T:(h % 2 + 1) * T], proj[:, q + h, P:T],
                                                   proj[:, kt[h], :], start=(h % 2 == 0), stop=True, skip_group_check=True)
                    ins.then_inc(scores, 1)

                def transposes(b):
                    kind = subs[b][0]
                    pe.wait_ge(probs_ready, b + 1)
                    if kind == "cmp":
                        for h in range(4):
                            for t in range(TT):
                                c = (h % 2) * T + t * P
                                ins = nc.tensor.transpose(ps[0:NCMP, 4 + h // 2, c:c + P], pcmp[:, t, h, :], ident)
                        ins.then_inc(pT_done, 2)
                        return
                    for h in range(4):
                        c = (h % 2) * T
                        nc.tensor.transpose(ps[:, 4 + h // 2, c:c + P], probs0[:, b % 2, h, :], ident)
                        ins = nc.tensor.transpose(ps[:, 4 + h // 2, c + P:c + T], probs1[:, b % 2, h, 0:P], ident)
                    ins.then_inc(pT_done, 1)
                    if b + 1 < NSUB:
                        pe.wait_ge(masked, b + 2)
                    for h in range(4):
                        ins = nc.tensor.transpose(ps[:, 1, h * P:(h + 1) * P], probs1[:, b % 2, h, P:T], ident)
                    ins.then_inc(pT_done, 1)

                def values(b):
                    kind, _, g, vs, _, first, last = subs[b]
                    if first and out_of[b]:
                        pe.wait_ge(oL_ready, out_of[b])
                    pe.wait_ge(pT_ready, 2 * b + 2)
                    for h in range(4):
                        out = ps[:, 6 + h // 2, (h % 2) * T:(h % 2 + 1) * T]
                        if kind == "cmp":
                            ins = nc.tensor.matmul(out, vc[:, g, :], pcT[:, h, :], start=False, stop=last, skip_group_check=True)
                        else:
                            nc.tensor.matmul(out, vtok[:, vs[h], 0, :], pT0[:, h, :], start=(first and h % 2 == 0), stop=False,
                                             skip_group_check=True)
                            ins = nc.tensor.matmul(out[:, P:T], vtok[:, vs[h], 1, :], pT1[:, h, :], start=False, stop=last,
                                                   skip_group_check=True)
                    ins.then_inc(pv_done, 1)

                pe.wait_ge(cmp_ready, GROUPS)
                pe.wait_ge(vtok_ready, len(v_pairs))
                pe.wait_ge(roped, len(rope_pairs))
                score(0)
                for b in range(NSUB):
                    if b + 1 < NSUB:
                        score(b + 1)
                    ada("ada_b", 2 * b, 2 * b + 2)
                    transposes(b)
                    values(b)
                pe.wait_ge(oL_ready, 4)
                pe.wait_ge(mod_ready, 2)
                layer("w_o", actH, actL)
                norm(1)
                norm(2)
                pe.wait_ge(act_ready, 2)
                for h in range(2):
                    layer(f"up_{h}", actH, actL)
                    pe.wait_ge(hidL_ready, 1 + 8 * (h + 1))
                    layer(f"down_{h}", hidH, hidL)
                norm(3)

            def rwkv_turn(i):
                def wait(s, per, j):
                    pe.wait_ge(s, j + i * per)
                hs = [(h // 2, h % 2) for h in range(RHEADS)]
                wait(lw_in, 64, 64)
                for j in range(RJ):
                    c = slice(j * P, (j + 1) * P)
                    t = slice(j * T, (j + 1) * T)
                    nc.tensor.matmul(ps[:, 0, t], lw[0:64, 0, c], proj2[0:64, SPEC, :], start=(j == 0), stop=True, skip_group_check=True)
                for j in range(RJ):
                    c = slice(j * P, (j + 1) * P)
                    t = slice(j * T, (j + 1) * T)
                    nc.tensor.matmul(ps[:, 1, t], lw[64:P, 0, c], proj2[64:P, SPEC, :], start=(j == 0), stop=True, skip_group_check=True)
                for j in range(RJ):
                    c = slice(j * P, (j + 1) * P)
                    t = slice(j * T, (j + 1) * T)
                    nc.tensor.matmul(ps[:, 2, t], lw[:, 1, c], proj2[:, SPEC + 1, :], start=(j == 0), stop=False, skip_group_check=True)
                for j in range(RJ):
                    c = slice(j * P, (j + 1) * P)
                    t = slice(j * T, (j + 1) * T)
                    ins = nc.tensor.matmul(ps[:, 2, t], lw[96:P, 2, c], proj2[96:P, SPEC + 2, :], start=False, stop=True,
                                           skip_group_check=True)
                ins.then_inc(lora_done, 1)
                wait(kksq, 1, 1)
                nc.tensor.matmul(ps[:, 3, :], same_head, flat(nrm[:, :, :]), start=True, stop=True).then_inc(kksum, 1)
                wait(mixed, 1, 1)
                for n, src in enumerate((rvv, BT, KTt)):
                    if n == 1:
                        wait(b_ready, 1, 1)
                    if n == 2:
                        wait(a_ready, 1, 1)
                    for t in range(TT):
                        for j in range(RJ):
                            c = (t * RJ + j) * P
                            ins = nc.tensor.transpose(ps[:, 4 + n, c:c + P], src[:, j, t * P:(t + 1) * P], ident)
                    ins.then_inc(tok_done, 1)
                wait(rk_scaled, 1, 1)
                nc.tensor.matmul(ps[:, 7, :], same_head, flat(rkk[:, :, :]), start=True, stop=True).then_inc(bonus_sum, 1)
                wait(sig_ready, 1, 1)
                wait(nrm_ready, 1, 1)
                wait(rk_ready, 1, 1)
                for n, src in enumerate((BT, KTt)):
                    if n:
                        wait(tok_ready, 3, 3)
                        wait(bonus_ready, 1, 1)
                    for h, (j, hh) in enumerate(hs):
                        for t in range(TT):
                            ins = nc.tensor.matmul(ps[:, 4 * n + h, t * 2 * P:(t + 1) * 2 * P], src[:, j, t * P:(t + 1) * P],
                                                   AR[hh][:, j, t, :, :].rearrange("p a t -> p (a t)"), start=(t == 0), stop=True,
                                                   skip_group_check=True)
                        ins.then_inc(mat_done, 1)
                wait(y1_ready, 1, 1)
                for m in range(MATS):
                    ins = nc.tensor.transpose(ps[:, m // 4, m % 4 * P:(m % 4 + 1) * P], Ym[:, m, :], ident)
                ins.then_inc(x1_done, 1)
                wait(x1_ready, 1, 1)
                for v in range(1, len(LEVELS)):
                    wait(lm_ready, 5, v)
                    if v > 1:
                        wait(level_ready, 5, v - 1)
                    for m in range(MATS):
                        ins = nc.tensor.matmul(ps[:, m // 4, m % 4 * P:(m % 4 + 1) * P], Lm[:, v % 2, m, :], Xm[:, m, :],
                                               start=(m % 4 == 0), stop=True, skip_group_check=True)
                    ins.then_inc(w1_done, 1)
                    wait(w1_ready, 5, v)
                    if v < len(LEVELS) - 1:
                        for m in range(MATS):
                            nc.tensor.matmul(ps[:, 2 + m // 4, m % 4 * P:(m % 4 + 1) * P], Ym[:, m, :], W1[:, m, :],
                                             start=(m % 4 == 0), stop=True, skip_group_check=True)
                    for m in range(MATS):
                        ins = nc.tensor.matmul(ps[:, 4 + m // 4, m % 4 * P:(m % 4 + 1) * P], W1[:, m, :], Ym[:, m, :],
                                               start=(m % 4 == 0), stop=True, skip_group_check=True)
                    ins.then_inc(dx_done, 1)
                wait(level_ready, 5, 5)
                for c in range(TT * 2):
                    t, o_ = c // 2, c % 2 * CHUNK
                    if c:
                        wait(st_ready, 4, c)
                    for h, (j, hh) in enumerate(hs):
                        out = ps[:, 0, h * RHEAD:(h + 1) * RHEAD]
                        nc.tensor.matmul(out, AR[hh][:, j, t, 0, :], ST[:, j, hh * RHEAD:(hh + 1) * RHEAD], start=(h == 0), stop=False,
                                         skip_group_check=True)
                        ins = nc.tensor.matmul(out, Kc[:, 2 * h + t, 0:P], rtok[:, t, j, hh * RHEAD:(hh + 1) * RHEAD], start=False,
                                               stop=True, skip_group_check=True)
                    ins.then_inc(rhs_done, 1)
                    for h, (j, hh) in enumerate(hs):
                        part = slice(hh * RHEAD, (hh + 1) * RHEAD)
                        nc.tensor.matmul(ps[part, 6, j * T + c * CHUNK:j * T + (c + 1) * CHUNK], ST[:, j, part],
                                         AR[hh][:, j, t, 1, o_:o_ + CHUNK], start=(c == 0 and j == 0), stop=False, skip_group_check=True)
                    wait(rhs_ready, 4, c + 1)
                    for h in range(RHEADS):
                        ins = nc.tensor.matmul(ps[:, 1, h * RHEAD:(h + 1) * RHEAD], Ym[:, 2 * h + t, :], rhs[:, h * RHEAD:(h + 1) * RHEAD],
                                               start=(h == 0), stop=True, skip_group_check=True)
                    ins.then_inc(u_done, 1)
                    wait(u_ready, 4, c + 1)
                    for j in range(RJ):
                        out = ps[:, 2, j * P:(j + 1) * P]
                        nc.tensor.matmul(out, btok[:, c % 2, t, j, :], uf[:, j * P:(j + 1) * P], start=(j == 0), stop=False,
                                         skip_group_check=True)
                        ins = nc.tensor.matmul(out, ktok[:, c % 2, t, j, :], rtok[:, t, j, :], start=False, stop=True,
                                               skip_group_check=True)
                    ins.then_inc(s_done, 1)
                    if c % 2:
                        for h, (j, hh) in enumerate(hs):
                            part = slice(hh * RHEAD, (hh + 1) * RHEAD)
                            out = ps[part, 6, j * T + t * P:j * T + (t + 1) * P]
                            nc.tensor.matmul(out, uf[:, h * RHEAD:(h + 1) * RHEAD], Bc[:, 2 * h + t, P:2 * P], start=False, stop=False,
                                             skip_group_check=True)
                            ins = nc.tensor.matmul(out, rtok[:, t, j, part], Kc[:, 2 * h + t, P:2 * P], start=False, stop=True,
                                                   skip_group_check=True)
                        ins.then_inc(ysum_done, 1)
                wait(yb_ready, 1, 1)
                nc.tensor.matmul(ps[:, 7, :], same_head, flat(yb[:, :, :]), start=True, stop=True).then_inc(mean_done, 1)
                wait(ysq_ready, 1, 1)
                nc.tensor.matmul(ps[:, 7, :], same_head, flat(ysq[:, :, :]), start=True, stop=True).then_inc(var_done, 1)

            if 2 in blocks:
                if 1 not in blocks:
                    pe.wait_ge(consts_in, 64)
                norm(NB)
                pe.wait_ge(act_ready, XB + 1)
                layer("w_in2", actH, actL)
                pe.wait_ge(evacuated, emptied("w_in2"))
                for n, p in enumerate((SBV, SBV + 2, FXV, FXV + 2)):
                    if n >= 2:
                        pe.wait_ge(v2_ready, n - 1)
                    for j in range(2):
                        for t in range(TT):
                            c = (2 * j + t) * P
                            ins = nc.tensor.transpose(ps[:, 4 + n % 2, c:c + P], proj2[:, p + j, t * P:(t + 1) * P], ident)
                    ins.then_inc(v2T_done, 1)

                def score2(q, k, forget):
                    for t in range(TT):
                        w = P * (t + 1)
                        for h in range(4):
                            out = ps[:, 1, h * P:(h + 1) * P] if t == 0 else ps[:, 2 + h // 2, (h % 2) * T:(h % 2 + 1) * T]
                            ts = slice(t * P, (t + 1) * P)
                            ins = nc.tensor.matmul(out, proj2[:, q + h, ts], proj2[:, k + h, 0:w],
                                                   start=(h % (4, 2)[t] == 0), stop=not forget, skip_group_check=True)
                            if forget:
                                pick = ident[0:4, h:h + 1]
                                nc.tensor.matmul(out, cum[:, 3, ts], pick.to_broadcast([4, w]), start=False, stop=False,
                                                 skip_group_check=True)
                                ins = nc.tensor.matmul(out, pick.to_broadcast([4, P]), cum[:, 2, 0:w], start=False, stop=True,
                                                       skip_group_check=True)
                    ins.then_inc(s2_done, 1)

                def outputs2(b):
                    for h in range(4):
                        c = (h % 2) * T
                        nc.tensor.transpose(ps[:, 4 + h // 2, c:c + P], prob0[:, 0, h, :], ident)
                        ins = nc.tensor.transpose(ps[:, 4 + h // 2, c + P:c + T], prob1[:, 0, h, 0:P], ident)
                    ins.then_inc(t2_done, 1)
                    for h in range(4):
                        ins = nc.tensor.transpose(ps[:, 1, h * P:(h + 1) * P], prob1[:, 0, h, P:T], ident)
                    ins.then_inc(t2_done, 1)
                    pe.wait_ge(t2_ready, 2 * b + 2)
                    if b:
                        pe.wait_ge(y2L_ready, b)
                    for h in range(4):
                        out = ps[:, 6 + h // 2, (h % 2) * T:(h % 2 + 1) * T]
                        nc.tensor.matmul(out, vtok2[:, 4 * b + h, 0, :], qT0[:, h, :], start=(h % 2 == 0), stop=False,
                                         skip_group_check=True)
                        ins = nc.tensor.matmul(out[:, P:T], vtok2[:, 4 * b + h, 1, :], qT1[:, h, :], start=False, stop=True,
                                               skip_group_check=True)
                    ins.then_inc(o2_done, 1)

                score2(SBQ, SBK, False)
                pe.wait_ge(v2_ready, 4)
                pe.wait_ge(s2_exp, 1)
                outputs2(0)
                pe.wait_ge(cum_ready, 1)
                score2(FXQ, FXK, True)
                pe.wait_ge(s2_probs, 1)
                outputs2(1)
                pe.wait_ge(y2L_ready, 2)
                pe.wait_ge(spec_ready, 1)
                pe.wait_ge(zeroed, 1)
                with pe.Fori(0, RTURNS) as i:
                    pe.wait_ge(turn_done, i + 1)
                    rwkv_turn(i)
                pe.wait_ge(turn_done, RTURNS + 1)
                layer("gates2", actH, actL)
                pe.wait_ge(evacuated, emptied("gates2"))

                def branch(i, r):
                    for s, (n, k0, start, stop) in enumerate(((0, 0, True, True), (1, 4, True, True), (2, 8, True, False), (2, 12, False, True))):
                        pe.wait_ge(wl_ready, RAW + lin("branch", i, r, s) + 1)
                        if start and not (isinstance(i, int) and i == 0 and r == 0):
                            pe.wait_ge(branch_used, 3 * (r - 1) + n + 1 + i * 6)
                        b = s % SPLIT
                        for k in range(STEP_K):
                            for m in range(GT):
                                out = ps[:, 2 * n + m // 2, (m % 2) * T:(m % 2 + 1) * T]
                                cols = slice(m * P, (m + 1) * P)
                                for j, (w, v) in enumerate(((wH, yH), (wH, yL), (wL, yH))):
                                    ins = nc.tensor.matmul(out, w[:, b, k, cols], v[:, k0 + k, :],
                                                           start=(start and k == 0 and j == 0 and m % 2 == 0),
                                                           stop=(stop and k == STEP_K - 1 and j == 2), skip_group_check=True)
                        ins.then_inc(step_done, 1)

                over_groups(pe, "branch", 1, branch)
                layer("w_out2", actH, actL)
                norm(NB + 1)
                norm(NB + 2)
                pe.wait_ge(act_ready, XB + 2)
                for h in range(2):
                    layer(f"up2_{h}", actH, actL)
                    pe.wait_ge(hidL_ready, 1 + UB + 8 * (h + 1))
                    layer(f"down2_{h}", hidH, hidL)
                norm(NB + 3)


def host_layout(inputs):
    given = {n: np.asarray(v) for n, v in inputs.items()}

    def own(n):
        return given[n][0]

    def col(v):
        return v.reshape(-1, P).T

    d = {"x": own("x").T, "c": col(given["c"]), "common": common_consts(), "c1": first_consts(), "c2": second_consts(),
         "vecs": np.stack([col(own(n)) for n in VECS], 1), "b_ada": col(own("b_ada")).reshape(P, 6, KT),
         "pos": np.stack([own("cmp_k_pos").T, own("cmp_v_pos").T], 1)}
    for n in ("w_ada", "w_o", "w_up", "w_down", "cmp_k_w1", "cmp_k_w2", "cmp_v_w1", "cmp_v_w2", "rwkv_w_up_2", "rwkv_a_up_2",
              "rwkv_g_up_2", "w_branch_a_2", "w_branch_b_2", "w_branch_c_2", "w_out_2", "w_mlp_up_2", "w_mlp_down_2"):
        d[n] = own(n)
    w, g0 = own("w_in"), QM * P
    d["w_in"], d["w_gate"] = np.concatenate([w[:, :g0], w[:, g0 + GATES:]], 1), w[:, g0:g0 + GATES]
    w = own("w_in_2")
    f0 = RR * P
    r0 = f0 + FORGET_H
    n0 = r0 + 3 * RW
    end = n0 + P + GATE_RANK
    d["w_in_2"] = np.concatenate([w[:, :f0], w[:, r0:n0], w[:, n0:n0 + 2 * P], w[:, end - P:end], w[:, f0:f0 + P]], 1)
    d["w_gates_2"] = w[:, end:]
    mu, m0 = own("rwkv_mu_2"), 3 * RW
    forget = np.zeros((P, 1), np.float32)
    forget[:FORGET_H, 0] = own("b_forget_2")
    d["rwv"] = np.concatenate(
        [col(mu[:m0]), *[col(own(f"rwkv_{n}_2")) for n in ("w0", "a0", "k_k", "k_a", "r_k", "ln_w", "ln_b")],
         col(mu[m0:m0 + P]), col(mu[m0 + P:m0 + 2 * P]), col(mu[-P:]), forget, np.full((P, 1), GN_EPS, np.float32)], 1)
    return {n: np.ascontiguousarray(v) for n, v in d.items()}


def kernel(**inputs):
    import concourse.bacc as bacc
    from concourse.bass_utils import run_bass_kernel_spmd

    nc = bacc.Bacc("TRN2", target_bir_lowering=False, num_devices=1)
    arrays = host_layout(inputs)
    args = {n: nc.dram_tensor(n, v.shape, F32, kind="ExternalInput").ap() for n, v in arrays.items()}
    args["out"] = nc.dram_tensor("out", (D, T), F32, kind="ExternalOutput").ap()
    build_program(nc, args)
    r = run_bass_kernel_spmd(nc, [arrays], core_ids=[0])
    return np.ascontiguousarray(r.results[0]["out"].T)[None]
```

```python
from contextlib import ExitStack

import numpy as np

import concourse.bass as bass
from concourse import mybir

F32 = mybir.dt.float32
F32R = mybir.dt.float32r
ACT = mybir.ActivationFunctionType
ALU = mybir.AluOpType
AX = mybir.AxisListType

P = 128
D = 2048
T = 256
KT = D // P
TT = T // P
DH = 128
D_FF = 4 * D
HT = D_FF // 2 // P
EPS = 1e-6
SCALE = DH ** -0.5
NEG = -1e30

STEP_K = 4
GC = 512
GT = GC // P
RAW, SPLIT = 4, 2
SIDE = 5

CMP_LEN, CMP_STRIDE = 32, 16
NCMP = (T - CMP_LEN) // CMP_STRIDE + 1
NSA_H, GROUPS = 8, 2

QN, KC, VC, KS, VS, KW, VW, QM, KM, VM = 0, 8, 10, 12, 14, 16, 18, 20, 28, 36
PROJ1 = 44
GATES = 3 * NSA_H

SBQ, SBK, SBV, FXQ, FXK, FXV, RR, RK, RV, SPEC = 0, 4, 8, 12, 16, 20, 24, 32, 40, 48
PROJ2 = 52
RW = 1024
RT_ = RW // P
CHUNK = 64
LEVELS = [1, 2, 4, 8, 16, 32]
RHEAD = 64
RJ = 2
RTURNS = RT_ // RJ
RHEADS = 2 * RJ
HALVES = slice(0, RHEADS), slice(RHEADS, 2 * RHEADS)
MATS = RHEADS * TT
GN_EPS = 64e-5
FORGET_H, GATE_RANK = 4, 160
DECAY = float(np.exp(-0.5))
MU_R, MU_K, MU_V, W0, A0, K_K, K_A, R_K, LN_W, LN_B = range(10)


RWKV_LINKS = 32


class Layers:

    def __init__(self, layers):
        self.at = {}
        t = lin = ada = g = 0
        for name, kind, groups, spg in layers:
            self.at[name] = dict(kind=kind, groups=groups, spg=spg, t0=t, l0=lin, a0=ada, g0=g)
            assert t % RAW == 0
            n = groups * spg
            t += n * (kind != "side")
            if kind == "lin":
                lin += n
                g += groups
            else:
                ada += n
        self.order = [x[0] for x in layers]

    def __getitem__(self, name):
        return self.at[name]

    def unroll(self, name):
        L = self.at[name]
        return 1 if L["kind"] == "ada" else max(2, RAW // L["spg"])


def first_consts():
    pos = np.arange(T, dtype=np.float32)
    inv = (np.float32(10000.0) ** (-np.arange(0, DH, 2, dtype=np.float32) / np.float32(DH))).astype(np.float32)
    ang = inv[:, None] * pos[None, :]
    cos, sin = np.cos(ang).astype(np.float32), np.sin(ang).astype(np.float32)
    h = DH // 2
    rot = np.zeros((P, P), np.float32)
    rot[np.arange(h) + h, np.arange(h)] = -1
    rot[np.arange(h), np.arange(h) + h] = 1
    cend = np.arange(NCMP) * CMP_STRIDE + CMP_LEN - 1
    tok = np.arange(T).reshape(TT, P).T
    seen = (cend[None, None, :] <= tok[:, :, None]).astype(np.float32)
    return np.concatenate([rot, np.tile(cos, (2, 1)), np.tile(sin, (2, 1)), seen.reshape(P, -1),
                           ((1 - seen) * np.float32(NEG)).reshape(P, -1)], axis=1)


def common_consts():
    i = np.arange(P)
    causal = np.where(i[None, :] <= i[:, None], 0, NEG).astype(np.float32)
    return np.concatenate([np.eye(P, dtype=np.float32), np.ones((P, P), np.float32), np.zeros((P, P), np.float32),
                           causal, np.full((P, 1), EPS, np.float32)], axis=1)


def second_consts():
    i = np.arange(P)
    strict = np.where(i[None, :] < i[:, None], 0, NEG).astype(np.float32)
    same_head = (i[:, None] // RHEAD == i[None, :] // RHEAD).astype(np.float32) / np.float32(RHEAD)
    same = i[:, None] // CHUNK == i[None, :] // CHUNK
    before = same & (i[:, None] < i[None, :])
    upto = same & (i[:, None] <= i[None, :])
    levels = [(i[:, None] // (2 * b) == i[None, :] // (2 * b)) & (i[:, None] // b % 2 == 0) & (i[None, :] // b % 2 == 1)
              for b in LEVELS]
    reset = np.tile((np.arange(T) % CHUNK != 0), (P, 1))
    return np.concatenate([np.zeros((P, P)), strict, same_head, before, upto, *levels, reset], axis=1).astype(np.float32)


VECS = ["pre_norm_mix", "post_norm_mix", "pre_norm_ffn", "post_norm_ffn",
        "norm_mix_pre_2", "norm_mix_post_2", "norm_mlp_pre_2", "norm_mlp_post_2"]


def build_program(nc, a, blocks=(1, 2)):
    layers = []
    if 1 in blocks:
        layers += [("ada_a", "ada", 8, 4), ("w_in", "lin", PROJ1 // GT, 4), ("ada_w", "side", SIDE, 4),
                   ("ada_b", "ada", 16 - SIDE, 4), ("w_o", "lin", 4, 4),
                   ("up_0", "lin", 8, 4), ("down_0", "lin", 4, 8), ("up_1", "lin", 8, 4), ("down_1", "lin", 4, 8)]
    if 2 in blocks:
        layers += [("w_in2", "lin", PROJ2 // GT, 4), ("gates2", "lin", 12, 4), ("branch", "lin", 4, 4), ("w_out2", "lin", 4, 4),
                   ("up2_0", "lin", 8, 4), ("down2_0", "lin", 4, 8), ("up2_1", "lin", 8, 4), ("down2_1", "lin", 4, 8)]
    L = Layers(layers)

    def matrix(ap):
        return ap.rearrange("(k p) n -> p k n", p=P)

    weights = {}
    if 1 in blocks:
        w_ada, w_up, w_down = matrix(a["w_ada"]), matrix(a["w_up"]), matrix(a["w_down"])
        weights |= {"ada_a": (w_ada, 0, 0), "ada_b": (w_ada, 0, (8 + SIDE) * GC), "w_in": (matrix(a["w_in"]), 0, 0),
                    "w_o": (matrix(a["w_o"]), 0, 0), "up_0": (w_up, 0, 0), "up_1": (w_up, 0, D_FF // 2),
                    "down_0": (w_down, 0, 0), "down_1": (w_down, HT, 0)}

    if 2 in blocks:
        w_up2, w_down2 = matrix(a["w_mlp_up_2"]), matrix(a["w_mlp_down_2"])
        weights |= {"w_in2": (matrix(a["w_in_2"]), 0, 0), "gates2": (matrix(a["w_gates_2"]), 0, 0),
                    "w_out2": (matrix(a["w_out_2"]), 0, 0), "up2_0": (w_up2, 0, 0), "up2_1": (w_up2, 0, D_FF // 2),
                    "down2_0": (w_down2, 0, 0), "down2_1": (w_down2, HT, 0)}

    top = [16512]
    made = {}

    def at(name, shape, dt, offset):
        made[name] = nc.alloc_sbuf_tensor_at(name, shape, dt, offset=offset)
        return made[name]

    def new(name, shape, dt=F32):
        off = top[0]
        n = 4 * int(np.prod(shape[1:]))
        top[0] = (off + n + 31) // 32 * 32
        return at(name, shape, dt, off)

    x = new("x", [P, KT, T])
    ACT0 = top[0]
    actH = new("actH", [P, KT, T], F32R)
    actL = new("actL", [P, KT, T], F32R)
    RING0 = top[0]
    raw = new("raw", [P, RAW, STEP_K, GC])
    SPLIT0 = top[0]
    wH = new("wH", [P, SPLIT, STEP_K, GC], F32R)
    wL = new("wL", [P, SPLIT, STEP_K, GC], F32R)
    ada_acc = at("ada_acc", [P, 2, 2, GC], F32, SPLIT0 + 4 * SPLIT * STEP_K * GC)
    common = new("common", [P, 4 * P + 1])
    ident, ones = common[:, 0:P], common[:, P:2 * P]
    eps = common[:, 4 * P:]
    causal = common[:, 2 * P:4 * P]
    vecs = new("vecs", [P, len(VECS), KT])
    mod = new("mod", [P, 6, KT])
    b_ada = new("b_ada", [P, 6, KT])
    cvec = new("cvec", [P, KT])
    csig = new("csig", [P, KT])
    coef = new("coef", [P, 8, KT])
    nmx = new("nmx", [P, 2, TT, 4])
    rsum = new("rsum", [P, 2, TT, 4])
    B0 = top[0]
    R0 = 229368 // 32 * 32 - 84 * 1024 - 512
    std = at("std", [P, T], F32, R0 + 83 * 1024)
    NC1 = P + 2 * T + 2 * TT * NCMP
    c1 = at("c1", [P, NC1], F32, B0)
    rot, cos, sin = c1[:, 0:P], c1[:, P:P + T], c1[:, P + T:P + 2 * T]
    seen = c1[:, P + 2 * T:P + 2 * T + TT * NCMP].rearrange("p (t n) -> p t n", t=TT)
    unseen = c1[:, P + 2 * T + TT * NCMP:].rearrange("p (t n) -> p t n", t=TT)
    assert B0 + 4 * NC1 <= R0, (B0 + 4 * NC1, R0)

    hidH = at("hidH", [P, HT, T], F32R, R0)
    hidL = at("hidL", [P, HT, T], F32R, R0 + 32 * 1024)
    o = at("o", [P, KT, T], F32, R0 + 64 * 1024)
    hid = at("hid_sq", [P, GT * T], F32, R0 + 80 * 1024)
    sq = at("sq", [P, KT, T], F32, R0)
    sq4 = at("sq4", [P, GT, T], F32, R0 + 80 * 1024)
    K1 = 1024
    proj = at("proj", [P, PROJ1, T], F32, R0)
    vtok = at("vtok", [P, 12, TT, P], F32, R0 + 44 * K1)
    probs0 = at("probs0", [P, 2, 4, P], F32, R0 + 56 * K1)
    probs1 = at("probs1", [P, 2, 4, T], F32, R0 + 60 * K1)
    pT0 = at("pT0", [P, 4, T], F32, R0 + 68 * K1)
    pT1 = at("pT1", [P, 4, P], F32, R0 + 72 * K1)
    rope_c = at("rope_c", [P, 2, 2, T], F32, SPLIT0)
    rope_s = at("rope_s", [P, 2, 2, T], F32, SPLIT0 + 4 * K1)
    xc = at("xc", [P, 2, CMP_LEN, GROUPS * NCMP], F32, SPLIT0 + 8 * K1)
    GW0 = (B0 + 4 * NC1 + 31) // 32 * 32
    gw = at("gw", [P, KT, GATES], F32, GW0)
    gwH = at("gwH", [P, KT, GATES], F32R, GW0 + 4 * KT * GATES)
    assert GW0 + 8 * KT * GATES <= R0
    gwL = at("gwL", [P, KT, GATES], F32R, R0 + 76 * K1)
    chtok = at("chtok", [GROUPS * NCMP, 2, P], F32, R0 + 78 * K1)
    gate = at("gate", [P, TT, GATES], F32, R0 + 80 * K1)
    posk = at("posk", [P, 2, CMP_LEN], F32, R0 + 80 * K1 + 256)
    cw2 = at("cw2", [P, 2, P], F32, R0 + 80 * K1 + 512)
    chid = at("chid", [P, 2, GROUPS * NCMP], F32, R0 + 80 * K1 + 1568)
    kcT = at("kcT", [P, GROUPS * NCMP], F32, R0 + 80 * K1 + 1824)
    vc = at("vc", [NCMP, GROUPS, P], F32, R0 + 80 * K1 + 1952)
    pcmp = at("pcmp", [P, TT, 4, NCMP], F32, R0 + 74 * K1)
    pcT = at("pcT", [NCMP, 4, T], F32, R0 + 75 * K1)
    cw1 = at("cw1", [P, 2, CMP_LEN, P], F32, ACT0)
    side = at("side", [P, 4, STEP_K, GC], F32, R0 + 44 * K1)
    side_acc = at("side_acc", [P, 2, GC], F32, R0 + 78 * K1)

    NC2 = 5 * P + len(LEVELS) * P + T
    c2 = at("c2", [P, NC2], F32, B0)
    strict, same_head = c2[:, 0:2 * P], c2[:, 2 * P:3 * P]
    token_mask = c2[:, 3 * P:5 * P]
    level_mask = c2[:, 5 * P:(5 + len(LEVELS)) * P].rearrange("p (l n) -> p l n", l=len(LEVELS))
    reset = c2[:, (5 + len(LEVELS)) * P:]
    rwv = at("rwv", [P, 10 * RT_ + 5], F32, B0 + 4 * NC2)
    rwv10 = rwv[:, 0:10 * RT_].rearrange("p (v j) -> p v j", v=10)
    mu_spec, b_forget, gn_eps = rwv[:, 10 * RT_:10 * RT_ + 3], rwv[0:4, 10 * RT_ + 3:10 * RT_ + 4], rwv[:, 10 * RT_ + 4:]
    rv = at("rv", [P, 10, RJ], F32, B0 + 4 * NC2 + 352)
    assert B0 + 4 * NC2 + 352 + 80 <= R0
    mix_t = at("mix_t", [P, GT * T], F32, B0)
    proj2 = at("proj2", [P, PROJ2, T], F32, R0)
    gates = at("gates", [P, 48, T], F32, R0)
    mix = at("mix", [P, GT * T], F32, R0 + 48 * K1)
    yH = at("yH", [P, KT, T], F32R, R0 + 52 * K1)
    yL = at("yL", [P, KT, T], F32R, R0 + 68 * K1)
    vtok2 = at("vtok2", [P, 8, TT, P], F32, SPLIT0)
    prob0 = at("prob0", [P, 2, 4, P], F32, SPLIT0 + 8 * K1)
    prob1 = at("prob1", [P, 2, 4, T], F32, SPLIT0 + 12 * K1)
    qT0 = at("qT0", [P, 4, T], F32, SPLIT0 + 20 * K1)
    qT1 = at("qT1", [P, 4, P], F32, SPLIT0 + 24 * K1)
    soft0 = at("soft0", [P, 4, P], F32, SPLIT0 + 26 * K1)
    soft1 = at("soft1", [P, 4, T], F32, SPLIT0 + 28 * K1)
    cum = at("cum", [4, 4, T], F32, RING0)
    forget0 = at("forget0", [P, 4, P], F32, RING0 + 4 * K1)
    forget1 = at("forget1", [P, 4, T], F32, RING0 + 6 * K1)
    rtop = [RING0]

    def ring(name, shape):
        off = rtop[0]
        rtop[0] += 4 * int(np.prod(shape[1:]))
        assert rtop[0] <= RING0 + 64 * K1
        return at(name, shape, F32, off)

    Bc, Kc = ring("Bc", [P, MATS, 2 * P]), ring("Kc", [P, MATS, 2 * P])
    Xm, Ym, W1 = ring("Xm", [P, MATS, P]), ring("Ym", [P, MATS, P]), ring("W1", [P, MATS, P])
    Lm = ring("Lm", [P, 2, MATS, P])
    AR = [ring(f"AR{h}", [P, RJ, TT, 2, P]) for h in range(2)]
    btok, ktok = ring("btok", [P, 2, TT, RJ, P]), ring("ktok", [P, 2, TT, RJ, P])
    rtok = ring("rtok", [P, TT, RJ, P])
    rhs, uf, ST = ring("rhs", [P, RHEADS * RHEAD]), ring("uf", [P, RHEADS * RHEAD]), ring("ST", [P, RJ, P])
    lw = ring("lw", [P, 3, RJ * P])
    BT, KTt = ring("BT", [P, RJ, T]), ring("KT", [P, RJ, T])
    rr, rk, rvv, d0, d1, d2, sg, aa, gg, cs, Gd, Gi = (
        at(n, [P, RJ, T], F32, R0 + 2 * K1 * j) for j, n in enumerate(
            ("rr", "rk", "rvv", "d0", "d1", "d2", "sg", "aa", "gg", "cs", "Gd", "Gi")))
    at_spec = at("spec_d", [P, 3, T], F32, RING0 + 60 * K1)
    kk, nrm, k2, Gp, ka, rkk, bonus, yb, ysq = d0, d1, d2, cs, sg, aa, d0, rr, rk

    ps = nc.alloc_psum_tensor("ps", [P, 8, 512], F32)

    def flat(ap):
        return ap.rearrange("p a b -> p (a b)")

    def bank2(b):
        return flat(ps[:, b:b + 2, :])

    with ExitStack() as ctx:
        def sem(name):
            return ctx.enter_context(nc.semaphore(name))

        raw_in = [sem(f"raw_in{s}") for s in range(RAW)]
        wh_ready, wl_ready, step_done = sem("wh_ready"), sem("wl_ready"), sem("step_done")
        ada_sum, ada_rows, evacuated = sem("ada_sum"), sem("ada_rows"), sem("evacuated")
        consts_in, x_in, c1_in = sem("consts_in"), sem("x_in"), sem("c1_in")
        side_in = [sem(f"side_in{n}") for n in range(4)]
        csig_ready, mod_ready = sem("csig_ready"), sem("mod_ready")
        sq_ready, ssum_ready, std_ready = sem("sq_ready"), sem("ssum_ready"), sem("std_ready")
        y_ready, h_ready, act_ready, x_ready = sem("y_ready"), sem("h_ready"), sem("act_ready"), sem("x_ready")
        o_scaled = sem("o_scaled")
        dve_chain, act_chain, pool_chain = sem("dve_chain"), sem("act_chain"), sem("pool_chain")
        gw_in, gw_hi, gw_lo, gate_done, gate_ready = (sem(n) for n in ("gw_in", "gw_hi", "gw_lo", "gate_done", "gate_ready"))
        rotated, rope_cos, rope_used, roped = sem("rotated"), sem("rope_cos"), sem("rope_used"), sem("roped")
        vT_done, vtok_ready = sem("vT_done"), sem("vtok_ready")
        cmp_in, xc_ready, cmp_sum, cmp_sig, cmp_hid, cmp_T, cmp_hidT, cmp_kv, cmp_ready = (
            sem(n) for n in ("cmp_in", "xc_ready", "cmp_sum", "cmp_sig", "cmp_hid", "cmp_T", "cmp_hidT", "cmp_kv", "cmp_ready"))
        scores, masked, exped, weight, probs_ready = (
            sem(n) for n in ("scores", "masked", "exped", "weight", "probs_ready"))
        pT_done, pT_ready, pv_done, oH_ready, oL_ready = (
            sem(n) for n in ("pT_done", "pT_ready", "pv_done", "oH_ready", "oL_ready"))
        sqr_ready, hidH_ready, hidL_ready, relu_done = (
            sem(n) for n in ("sqr_ready", "hidH_ready", "hidL_ready", "relu_done"))
        out_sem = sem("out_stored")
        c2_in, lw_in, branch_in = sem("c2_in"), sem("lw_in"), sem("branch_in")
        v2T_done, v2_ready, f_log, cum_ready = sem("v2T_done"), sem("v2_ready"), sem("f_log"), sem("cum_ready")
        s2_done, s2_masked, s2_soft, s2_sub, s2_exp, s2_weight, s2_probs = (
            sem(n) for n in ("s2_done", "s2_masked", "s2_soft", "s2_sub", "s2_exp", "s2_weight", "s2_probs"))
        t2_done, t2_ready, o2_done, y2H_ready, y2L_ready = (
            sem(n) for n in ("t2_done", "t2_ready", "o2_done", "y2H_ready", "y2L_ready"))
        spec_mixed, spec_ready, zeroed, turn_done = sem("spec_mixed"), sem("spec_ready"), sem("zeroed"), sem("turn_done")
        shifted_z, mixed, lora_done, sig_ready, kk_ready, kksq, kksum, nrm_ready = (
            sem(n) for n in ("shifted_z", "mixed", "lora_done", "sig_ready", "kk_ready", "kksq", "kksum", "nrm_ready"))
        cs_ready, gexp, csp_ready, gp_ready, k2_ready, kkn_ready, a_ready, b_ready = (
            sem(n) for n in ("cs_ready", "gexp", "csp_ready", "gp_ready", "k2_ready", "kkn_ready", "a_ready", "b_ready"))
        rk_ready, rk_scaled, bonus_sum, bonus_ready, tok_done, tok_ready = (
            sem(n) for n in ("rk_ready", "rk_scaled", "bonus_sum", "bonus_ready", "tok_done", "tok_ready"))
        mat_done, mat_masked, y1_ready, x1_done, x1_ready, lm_ready = (
            sem(n) for n in ("mat_done", "mat_masked", "y1_ready", "x1_done", "x1_ready", "lm_ready"))
        w1_done, w1_ready, dx_done, level_ready = (sem(n) for n in ("w1_done", "w1_ready", "dx_done", "level_ready"))
        rhs_done, rhs_ready, u_done, u_ready, s_done, st_ready, ysum_done = (
            sem(n) for n in ("rhs_done", "rhs_ready", "u_done", "u_ready", "s_done", "st_ready", "ysum_done"))
        r_ready = sem("r_ready")
        yb_ready, mean_done, yc_ready, ysq_ready, var_done, gstd_ready, yc_out, ycH_ready = (
            sem(n) for n in ("yb_ready", "mean_done", "yc_ready", "ysq_ready", "var_done", "gstd_ready", "yc_out", "ycH_ready"))
        mix_ready, mixH_ready, mixL_ready, branch_used = (
            sem(n) for n in ("mix_ready", "mixH_ready", "mixL_ready", "branch_used"))
        NB = 4 * (1 in blocks)
        UB = 16 * (1 in blocks)
        XB = 2 * (1 in blocks)

        class Chain:

            def __init__(self, eng, s):
                self.eng, self.s, self.n, self.off = eng, s, 0, 0

            def __call__(self, ins):
                self.n += 1
                ins.then_inc(self.s, 1)
                self.eng.wait_ge(self.s, self.off + self.n)

        def over_groups(eng, name, first, body):
            U, n = L.unroll(name), L[name]["groups"]
            for r in range(first):
                body(0, r)
            turns = (n - first) // U
            if turns > 1:
                with eng.Fori(0, turns) as i:
                    for r in range(U):
                        body(i, first + r)
            elif turns:
                for r in range(U):
                    body(0, first + r)
            for r in range(n - first - turns * U):
                body(turns, first + r)

        def raw_loads(name, i, r, s):
            l, U = L[name], L.unroll(name)
            j = r * l["spg"] + s
            return j % RAW, 16 * (l["t0"] // RAW + j // RAW + 1) + i * (16 * U * l["spg"] // RAW)

        def lin(name, i, r, s=0):
            l, U = L[name], L.unroll(name)
            return l["l0"] + r * l["spg"] + s + i * (U * l["spg"])

        def grp(name, i, r):
            return L[name]["g0"] + r + i * L.unroll(name)

        def done(name):
            l = L[name]
            return SPLIT + l["l0"] + l["groups"] * l["spg"]

        def emptied(name):
            return 2 + L[name]["g0"] + L[name]["groups"]

        def acc(name, r):
            return 2 * ((L[name]["g0"] + r) % 2)

        subs = []
        for g in range(GROUPS):
            q = QN + 4 * g
            subs += [("full", q, [KS + g] * 4, [0 + g] * 4, 1, True, False),
                     ("full", q, [KW + g] * 4, [2 + g] * 4, 2, False, False),
                     ("cmp", q, g, None, 0, False, True)]
        for m in range(2):
            subs.append(("full", QM + 4 * m, [KM + 4 * m + h for h in range(4)], [4 + 4 * m + h for h in range(4)],
                         None, True, True))
        out_of = [g for g, n in ((0, 3), (1, 3), (2, 1), (3, 1)) for _ in range(n)]
        NSUB = len(subs)
        ADA_BESIDE = [1, 1, 1, 1, 1, 1, 1, 0]
        assert len(ADA_BESIDE) == NSUB and 4 + sum(ADA_BESIDE) == L["ada_b"]["groups"] if 1 in blocks else True
        rope_pairs = [QN, QN + 2, QN + 4, QN + 6, KC, KS, KW] + list(range(QM, VM, 2))
        v_pairs = [VS, VW] + list(range(VM, PROJ1, 2))

        up_groups_before = {}
        seen_up = 0
        for name in L.order:
            if name.startswith("up"):
                up_groups_before[name] = L[name]["g0"] - seen_up
                seen_up += L[name]["groups"]

        block = ctx.enter_context(nc.Block())

        @block.sync
        def _(sp):
            sp.dma_start(cvec[:, :], a["c"]).then_inc(consts_in, 16)
            sp.dma_start(common[:, :], a["common"]).then_inc(consts_in, 16)
            sp.dma_start(vecs[:, :, :], a["vecs"]).then_inc(consts_in, 16)
            sp.dma_start(b_ada[:, :, :], a["b_ada"]).then_inc(consts_in, 16)
            sp.dma_start(x[:, :, :], matrix(a["x"])).then_inc(x_in, 16)

            def stream(name):
                l, U = L[name], L.unroll(name)
                w, k0, n0 = weights[name]

                def body(i, r):
                    for s in range(l["spg"]):
                        slot, _ = raw_loads(name, i, r, s)
                        if l["kind"] == "ada":
                            sp.wait_ge(ada_sum, STEP_K * (l["a0"] + r * 4 + s + 1) + i * (STEP_K * 4))
                        else:
                            sp.wait_ge(wl_ready, lin(name, i, r, s) + 1)
                        sp.dma_start(raw[:, slot, :, :],
                                     w[:, k0 + s * STEP_K:k0 + (s + 1) * STEP_K, bass.ds(n0 + r * GC + i * (U * GC), GC)]
                                     ).then_inc(raw_in[slot], 16)
                        if name == "w_in" and r == 1:
                            side_g = L["ada_a"]["groups"]
                            sp.wait_ge(ada_sum, STEP_K * (4 * side_g + s + 1) + i * (4 * STEP_K))
                            sp.dma_start(side[:, s, :, :], w_ada[:, s * STEP_K:(s + 1) * STEP_K,
                                                                 bass.ds(side_g * GC + i * GC, GC)]).then_inc(side_in[s], 16)

                if l["kind"] == "ada":
                    if l["l0"]:
                        sp.wait_ge(wl_ready, RAW + l["l0"])
                elif l["a0"]:
                    sp.wait_ge(ada_sum, STEP_K * (RAW + l["a0"]))
                over_groups(sp, name, 0, body)

            if 1 in blocks:
                stream("ada_a")
                sp.dma_start(c1[:, :], a["c1"]).then_inc(c1_in, 16)
                sp.dma_start(gw[:, :, :], matrix(a["w_gate"])).then_inc(gw_in, 16)
                stream("w_in")
                for name in ("ada_b", "w_o", "up_0", "down_0", "up_1", "down_1"):
                    stream(name)
            if 2 in blocks:
                if 1 in blocks:
                    sp.wait_ge(roped, len(rope_pairs))
                    sp.wait_ge(oL_ready, 4)
                sp.dma_start(c2[:, :], a["c2"]).then_inc(c2_in, 16)
                sp.dma_start(rwv[:, :], a["rwv"]).then_inc(c2_in, 16)
                stream("w_in2")
                sp.wait_ge(zeroed, 1)
                with sp.Fori(0, RTURNS) as i:
                    sp.wait_ge(turn_done, i + 1)
                    for part, src in ((slice(0, 64), "rwkv_w_up_2"), (slice(64, P), "rwkv_a_up_2")):
                        sp.dma_start(lw[part, 0, :], a[src][:, bass.ds(i * (RJ * P), RJ * P)]).then_inc(lw_in, 16)
                    sp.dma_start(lw[:, 1, :], a["rwkv_g_up_2"][0:P, bass.ds(i * (RJ * P), RJ * P)]).then_inc(lw_in, 16)
                    sp.dma_start(lw[96:P, 2, :], a["rwkv_g_up_2"][P:P + 32, bass.ds(i * (RJ * P), RJ * P)]).then_inc(lw_in, 16)
                sp.wait_ge(turn_done, RTURNS + 1)
                stream("gates2")
                wa, wb, wc = (matrix(a[f"w_branch_{n}_2"]) for n in "abc")

                def branch_loads(i, r):
                    for s, (w, k) in enumerate(((wa, 0), (wb, 0), (wc, 0), (wc, STEP_K))):
                        slot, _ = raw_loads("branch", i, r, s)
                        sp.wait_ge(wl_ready, lin("branch", i, r, s) + 1)
                        sp.dma_start(raw[:, slot, :, :], w[:, k:k + STEP_K, bass.ds(r * GC + i * (2 * GC), GC)]
                                     ).then_inc(raw_in[slot], 16)

                over_groups(sp, "branch", 0, branch_loads)
                for name in ("w_out2", "up2_0", "down2_0", "up2_1", "down2_1"):
                    stream(name)
            for c in range(KT // GT):
                sp.wait_ge(x_ready, 4 * (2 * len(blocks) - 1) + c + 1)
                sp.dma_start(matrix(a["out"])[:, GT * c:GT * (c + 1), :], x[:, GT * c:GT * (c + 1), :]).then_inc(out_sem, 16)
            sp.wait_ge(out_sem, 16 * (KT // GT))

        @block.scalar
        def _(act):
            chain = Chain(act, act_chain)

            def split(name, i, r, s):
                slot, count = raw_loads(name, i, r, s)
                act.wait_ge(raw_in[slot], count)
                act.wait_ge(step_done, lin(name, i, r, s) + 1)
                nc.scalar.activation(wH[:, s % SPLIT if L[name]["spg"] > 1 else r % SPLIT, :, :], raw[:, slot, :, :],
                                     ACT.Copy).then_inc(wh_ready, 1)

            carry = []

            def layer(name, evac=None, done=0, when=1):
                spg = L[name]["spg"]

                def body(i, r):
                    peeled = isinstance(i, int) and i == 0 and r == 0
                    for s in range(spg):
                        if not (peeled and s < done):
                            split(name, i, r, s)
                        if peeled and s == min(1, spg - 1):
                            flush()
                        if evac and s == min(when, spg - 1) and not peeled:
                            evac(name, i, r - 1)

                over_groups(act, name, 1, body)
                if evac:
                    n, U = L[name]["groups"], L.unroll(name)
                    i = (n - 1 - 1) // U
                    carry.append(lambda: evac(name, i, n - 1 - i * U))

            def flush():
                while carry:
                    carry.pop()()

            def copy_to(dst, func=ACT.Copy):
                def evac(name, i, r):
                    act.wait_ge(step_done, SPLIT + lin(name, i, r, L[name]["spg"] - 1) + 1)
                    nc.scalar.activation(flat(dst[:, bass.ds(GT * r + i * (GT * L.unroll(name)), GT), :]),
                                         bank2(acc(name, r)), func).then_inc(evacuated, 1)
                return evac

            def square_relu(name, i, r):
                act.wait_ge(step_done, SPLIT + lin(name, i, r, L[name]["spg"] - 1) + 1)
                g = grp(name, i, r) - up_groups_before[name] + 1
                act.wait_ge(hidL_ready, g)
                nc.scalar.activation(hid[:, :], bank2(acc(name, r)), ACT.Relu).then_inc(evacuated, 1)
                act.wait_ge(evacuated, 2 + grp(name, i, r) + 1)
                nc.scalar.activation(hid[:, :], hid[:, :], ACT.Square).then_inc(sqr_ready, 1)
                act.wait_ge(sqr_ready, g)
                nc.scalar.activation(flat(hidH[:, bass.ds(GT * r + i * (GT * L.unroll(name)), GT), :]), hid[:, :],
                                     ACT.Copy).then_inc(hidH_ready, 1)

            def squares(n, c, src, dst):
                nc.scalar.activation(flat(dst[:, :, :]), flat(src[:, GT * c:GT * (c + 1), :]), ACT.Square).then_inc(sq_ready, 1)

            def copy_square(n):
                def evac(name, i, r):
                    c = r + i * L.unroll(name)
                    copy_to(o)(name, i, r)
                    act.wait_ge(evacuated, 2 + grp(name, i, r) + 1)
                    square_of(n)(name, i, r)
                return evac

            def square_of(n):
                def evac(name, i, r):
                    c = r + i * L.unroll(name)
                    act.wait_ge(evacuated, 2 + grp(name, i, r) + 1)
                    if c:
                        act.wait_ge(ssum_ready, 4 * n + c)
                    squares(n, c, o, sq4)
                return evac

            def root(n):
                act.wait_ge(ssum_ready, 4 * (n + 1))
                nc.scalar.activation(std[:, :], ps[:, 4, 0:T], ACT.Sqrt, bias=eps, scale=1.0 / D).then_inc(std_ready, 1)

            def pre_norm(n, update):
                for c in range(KT // GT):
                    if update:
                        act.wait_ge(x_ready, 4 * (update - 1) + c + 1)
                    elif c == 0:
                        act.wait_ge(x_in, 16)
                    squares(n, c, x, sq[:, GT * c:GT * (c + 1), :])
                root(n)

            def inputs_high(m, shift=None):
                for c in range(KT // GT):
                    act.wait_ge(y_ready, 4 * m + c + 1)
                    if shift is None:
                        ins = nc.scalar.activation(flat(actH[:, GT * c:GT * (c + 1), :]), flat(sq[:, GT * c:GT * (c + 1), :]), ACT.Copy)
                    else:
                        for k in range(GT * c, GT * (c + 1)):
                            ins = nc.scalar.activation(actH[:, k, :], sq[:, k, :], ACT.Identity, bias=mod[:, shift, k:k + 1])
                    ins.then_inc(h_ready, 1)

            def between(n, name):
                split(name, 0, 0, 0)
                flush()
                split(name, 0, 0, 1)
                root(n)
                pre_norm(n + 1, (n + 1) // 2)

            if 1 in blocks:
                act.wait_ge(consts_in, 64)
                nc.scalar.activation(csig[:, :], cvec[:, :], ACT.Sigmoid).then_inc(csig_ready, 1)
                pre_norm(0, 0)
                for s in range(2):
                    split("w_in", 0, 0, s)
                act.wait_ge(mod_ready, 1)
                inputs_high(0, 0)
                act.wait_ge(gw_in, 16)
                nc.scalar.activation(gwH[:, :, :], gw[:, :, :], ACT.Copy).then_inc(gw_hi, 1)
                layer("w_in", copy_to(proj), 2)
                flush()
                act.wait_ge(gate_done, 1)
                nc.scalar.activation(gate[:, :, :], ps[:, 5, 0:TT * GATES].rearrange("p (t g) -> p t g", t=TT),
                                     ACT.Sigmoid).then_inc(gate_ready, 1)
                act.dma_start(cw1[:, 0, :, :], a["cmp_k_w1"].rearrange("(l d) h -> d l h", d=P)).then_inc(cmp_in, 16)
                act.dma_start(cw1[:, 1, :, :], a["cmp_v_w1"].rearrange("(l d) h -> d l h", d=P)).then_inc(cmp_in, 16)
                act.dma_start(posk[:, :, :], a["pos"]).then_inc(cmp_in, 16)
                act.dma_start(cw2[:, 0, :], a["cmp_k_w2"]).then_inc(cmp_in, 16)
                act.dma_start(cw2[:, 1, :], a["cmp_v_w2"]).then_inc(cmp_in, 16)
                for n in range(len(v_pairs)):
                    act.wait_ge(vT_done, n + 1)
                    nc.scalar.activation(vtok[:, 2 * n:2 * n + 2, :, :].rearrange("p a t d -> p (a t d)"),
                                         ps[:, 4 + n % 2, :], ACT.Copy).then_inc(vtok_ready, 1)
                act.wait_ge(cmp_sum, 1)
                nc.scalar.activation(flat(chtok[:, :, :]), ps[0:GROUPS * NCMP, 6, 0:2 * P], ACT.Sigmoid).then_inc(cmp_sig, 1)
                act.wait_ge(cmp_T, 1)
                nc.scalar.activation(flat(chid[:, :, :]), ps[:, 6, 0:2 * GROUPS * NCMP], ACT.Copy).then_inc(cmp_hidT, 1)
                act.wait_ge(cmp_kv, 1)
                nc.scalar.activation(kcT[:, :], ps[:, 7, 0:GROUPS * NCMP], ACT.Copy)
                for g in range(GROUPS):
                    nc.scalar.activation(vc[:, g, :], ps[0:NCMP, 7, 64 + g * P:64 + (g + 1) * P], ACT.Copy
                                         ).then_inc(cmp_ready, 1)

                def exps(b):
                    kind = subs[b][0]
                    act.wait_ge(masked, b + 1)
                    for t in range(TT):
                        for h in range(4):
                            p = pcmp[:, t, h, :] if kind == "cmp" else (probs0, probs1)[t][:, b % 2, h, :]
                            bias = nmx[:, b % 2, t, h:h + 1]
                            if kind == "cmp":
                                ins = nc.scalar.activation(p, p, ACT.Exp, bias=bias, scale=SCALE)
                            else:
                                ins = nc.scalar.activation(p, p, ACT.Exp, bias=bias, scale=SCALE,
                                                           accum_out=rsum[:, b % 2, t, h:h + 1])
                    ins.then_inc(exped, 1)

                def take_pT(b):
                    act.wait_ge(pT_done, 2 * b + 1)
                    if b:
                        act.wait_ge(pv_done, b)
                    if subs[b][0] == "cmp":
                        nc.scalar.activation(flat(pcT[:, :, :]), flat(ps[0:NCMP, 4:6, :]), ACT.Copy).then_inc(pT_ready, 2)
                        return
                    nc.scalar.activation(flat(pT0[:, :, :]), bank2(4), ACT.Copy).then_inc(pT_ready, 1)
                    act.wait_ge(pT_done, 2 * b + 2)
                    nc.scalar.activation(flat(pT1[:, :, :]), ps[:, 1, :], ACT.Copy).then_inc(pT_ready, 1)

                exps(0)
                for b in range(NSUB):
                    if b + 1 < NSUB:
                        exps(b + 1)
                    take_pT(b)
                    if subs[b][6]:
                        act.wait_ge(pv_done, b + 1)
                        g = out_of[b]
                        nc.scalar.activation(flat(actH[:, 4 * g:4 * g + 4, :]), bank2(6), ACT.Copy).then_inc(oH_ready, 1)
                layer("w_o", copy_square(1))
                between(1, "up_0")
                inputs_high(1, 3)
                layer("up_0", square_relu, 2)
                layer("down_0", copy_to(o))
                layer("up_1", square_relu)
                layer("down_1", square_of(3), when=4)

            def rwkv_turn(i):
                def wait(s, per, j):
                    act.wait_ge(s, j + i * per)
                wait(lora_done, 1, 1)
                wait(mixed, 1, 1)
                for j in range(RJ):
                    nc.scalar.activation(sg[:, j, :], ps[:, 0, j * T:(j + 1) * T], ACT.Sigmoid, bias=rv[:, W0, j:j + 1])
                for j in range(RJ):
                    nc.scalar.activation(aa[:, j, :], ps[:, 1, j * T:(j + 1) * T], ACT.Sigmoid, bias=rv[:, A0, j:j + 1])
                nc.scalar.activation(flat(gg[:, :, :]), ps[:, 2, :], ACT.Copy).then_inc(sig_ready, 1)
                wait(kk_ready, 1, 1)
                nc.scalar.activation(flat(nrm[:, :, :]), flat(kk[:, :, :]), ACT.Square).then_inc(kksq, 1)
                wait(kksum, 1, 1)
                nc.scalar.activation(flat(nrm[:, :, :]), ps[:, 3, :], ACT.Sqrt, scale=float(RHEAD)).then_inc(nrm_ready, 1)
                wait(cs_ready, 1, 1)
                nc.scalar.activation(flat(Gd[:, :, :]), flat(cs[:, :, :]), ACT.Exp, scale=-DECAY)
                nc.scalar.activation(flat(Gi[:, :, :]), flat(cs[:, :, :]), ACT.Exp, scale=DECAY).then_inc(gexp, 1)
                wait(csp_ready, 1, 1)
                nc.scalar.activation(flat(Gp[:, :, :]), flat(cs[:, :, :]), ACT.Exp, scale=-DECAY).then_inc(gp_ready, 1)
                wait(tok_done, 3, 1)
                nc.scalar.activation(rtok[:, :, :, :].rearrange("p i j d -> p (i j d)"), ps[:, 4, :], ACT.Copy).then_inc(tok_ready, 1)
                for n, dst in enumerate((btok, ktok)):
                    wait(tok_done, 3, n + 2)
                    for c in range(2):
                        rows = slice(c * CHUNK, (c + 1) * CHUNK)
                        ins = nc.scalar.activation(dst[rows, c, :, :, :].rearrange("p i j d -> p (i j d)"), ps[rows, 5 + n, :],
                                                   ACT.Copy)
                    ins.then_inc(tok_ready, 1)
                for f, m4 in enumerate(HALVES):
                    wait(x1_done, 2, f + 1)
                    nc.scalar.activation(flat(Xm[:, m4, :]), ps[:, f, :], ACT.Copy).then_inc(x1_ready, 1)
                for v in range(1, len(LEVELS)):
                    for f, m4 in enumerate(HALVES):
                        wait(w1_done, 10, 2 * v - 1 + f)
                        nc.scalar.activation(flat(W1[:, m4, :]), ps[:, f, :], ACT.Copy).then_inc(w1_ready, 1)
                for c in range(TT * 2):
                    wait(rhs_done, 4, c + 1)
                    nc.scalar.activation(rhs[:, :], ps[:, 0, 0:RHEADS * RHEAD], ACT.Copy).then_inc(rhs_ready, 1)
                    wait(u_done, 4, c + 1)
                    if c == 2:
                        wait(ysum_done, 2, 1)
                    rows = slice(c % 2 * CHUNK, (c % 2 + 1) * CHUNK)
                    nc.scalar.activation(uf[rows, :], ps[rows, 1, 0:RHEADS * RHEAD], ACT.Copy).then_inc(u_ready, 1)
                wait(ysum_done, 2, 2)
                nc.scalar.activation(flat(yb[:, :, :]), ps[:, 6, :], ACT.Copy).then_inc(yb_ready, 1)
                wait(yc_ready, 1, 1)
                nc.scalar.activation(flat(ysq[:, :, :]), flat(yb[:, :, :]), ACT.Square).then_inc(ysq_ready, 1)
                wait(var_done, 1, 1)
                nc.scalar.activation(flat(nrm[:, :, :]), ps[:, 7, :], ACT.Sqrt, bias=gn_eps).then_inc(gstd_ready, 1)
                wait(yc_out, 1, 1)
                nc.scalar.activation(flat(yH[:, bass.ds(2 * 4 + i * RJ, RJ), :]), flat(yb[:, :, :]), ACT.Copy).then_inc(ycH_ready, 1)

            if 2 in blocks:
                if 1 not in blocks:
                    act.wait_ge(consts_in, 64)
                if 1 in blocks:
                    between(3, "w_in2")
                else:
                    pre_norm(0, 0)
                    for s in range(2):
                        split("w_in2", 0, 0, s)
                inputs_high(XB)
                layer("w_in2", copy_to(proj2), 2)
                flush()
                act.wait_ge(evacuated, emptied("w_in2"))
                act.wait_ge(c2_in, 32)
                u, e = cum[:, 0, :], cum[:, 1, :]
                chain(nc.scalar.activation(u, proj2[0:4, SPEC + 3, :], ACT.Identity, bias=b_forget))
                chain(nc.scalar.activation(e, u, ACT.Abs))
                chain(nc.scalar.activation(e, e, ACT.Exp, scale=-1.0))
                nc.scalar.activation(e, e, ACT.Ln, bias=ones[0:4, 0:1]).then_inc(f_log, 1)
                for n in range(4):
                    act.wait_ge(v2T_done, n + 1)
                    nc.scalar.activation(vtok2[:, 2 * n:2 * n + 2, :, :].rearrange("p a t d -> p (a t d)"), ps[:, 4 + n % 2, :],
                                         ACT.Copy).then_inc(v2_ready, 1)
                act.wait_ge(s2_masked, 1)
                for so, pr in ((soft0, prob0), (soft1, prob1)):
                    z, so_ = flat(pr[:, 0, :, :]), flat(so[:, :, :])
                    chain(nc.scalar.activation(so_, z, ACT.Abs, scale=SCALE))
                    chain(nc.scalar.activation(so_, so_, ACT.Exp, scale=-1.0))
                    chain(nc.scalar.activation(so_, so_, ACT.Ln, bias=ones[:, 0:1]))
                    nc.scalar.activation(flat(pr[:, 1, :, :]), z, ACT.Relu, scale=SCALE).then_inc(s2_soft, 1)
                act.wait_ge(s2_masked, 2)
                for t in range(TT):
                    for h in range(4):
                        p = (forget0, forget1)[t][:, h, :]
                        ins = nc.scalar.activation(p, p, ACT.Exp, bias=nmx[:, 0, t, h:h + 1], scale=SCALE,
                                                   accum_out=rsum[:, 0, t, h:h + 1])
                ins.then_inc(s2_exp, 1)
                act.wait_ge(s2_sub, 1)
                nc.scalar.activation(flat(prob0[:, 0, :, :]), flat(prob0[:, 0, :, :]), ACT.Exp)
                nc.scalar.activation(flat(prob1[:, 0, :, :]), flat(prob1[:, 0, :, :]), ACT.Exp).then_inc(s2_exp, 1)

                def take_t2(b):
                    act.wait_ge(t2_done, 2 * b + 1)
                    if b:
                        act.wait_ge(o2_done, b)
                    nc.scalar.activation(flat(qT0[:, :, :]), bank2(4), ACT.Copy).then_inc(t2_ready, 1)
                    act.wait_ge(t2_done, 2 * b + 2)
                    nc.scalar.activation(flat(qT1[:, :, :]), ps[:, 1, :], ACT.Copy).then_inc(t2_ready, 1)
                    act.wait_ge(o2_done, b + 1)
                    nc.scalar.activation(flat(yH[:, 4 * b:4 * b + 4, :]), bank2(6), ACT.Copy).then_inc(y2H_ready, 1)

                take_t2(0)
                take_t2(1)
                act.wait_ge(spec_mixed, 1)
                nc.scalar.activation(proj2[0:64, SPEC, :], proj2[0:64, SPEC, :], ACT.Tanh)
                nc.scalar.activation(proj2[:, SPEC + 1, :], proj2[:, SPEC + 1, :], ACT.Sigmoid)
                nc.scalar.activation(proj2[96:P, SPEC + 2, :], proj2[96:P, SPEC + 2, :], ACT.Sigmoid).then_inc(spec_ready, 1)
                act.wait_ge(zeroed, 1)
                with act.Fori(0, RTURNS) as i:
                    act.wait_ge(turn_done, i + 1)
                    rwkv_turn(i)
                act.wait_ge(turn_done, RTURNS + 1)
                layer("gates2", copy_to(gates, ACT.Sigmoid))
                flush()

                def mix_high(name, i, r):
                    act.wait_ge(mix_ready, 1 + r + i * 2)
                    nc.scalar.activation(flat(actH[:, bass.ds(GT * r + i * (2 * GT), GT), :]), mix[:, :], ACT.Copy
                                         ).then_inc(mixH_ready, 1)

                layer("branch", mix_high)
                flush()
                layer("w_out2", copy_square(NB + 1))
                between(NB + 1, "up2_0")
                inputs_high(XB + 1)
                layer("up2_0", square_relu, 2)
                layer("down2_0", copy_to(o))
                layer("up2_1", square_relu)
                layer("down2_1", square_of(NB + 3), when=4)
                flush()
                root(NB + 3)

        @block.vector
        def _(dve):
            link = Chain(dve, dve_chain)
            dve.sem_inc(wl_ready, RAW)
            dve.sem_inc(hidL_ready, 1)
            dve.sem_inc(ada_sum, STEP_K * RAW)
            dve.sem_inc(ada_rows, 2)

            def split(name, i, r, s):
                slot, _ = raw_loads(name, i, r, s)
                l = lin(name, i, r, s)
                b = s % SPLIT if L[name]["spg"] > 1 else r % SPLIT
                dve.wait_ge(wh_ready, l + 1)
                dve.wait_ge(step_done, l + 1)
                nc.vector.tensor_tensor(wL[:, b, :, :], raw[:, slot, :, :], wH[:, b, :, :].bitcast(F32),
                                        ALU.subtract).then_inc(wl_ready, 1)

            carry = []

            def layer(name, evac=None, done=0, beside=None):
                spg = L[name]["spg"]

                def body(i, r):
                    peeled = isinstance(i, int) and i == 0 and r == 0
                    for s in range(spg):
                        if not (peeled and s < done):
                            split(name, i, r, s)
                        if beside and not peeled:
                            beside(i, r, s)
                        if peeled and s == min(2, spg - 1):
                            flush()
                        if evac and s == min(2, spg - 1) and not peeled:
                            evac(name, i, r - 1)

                over_groups(dve, name, 1, body)
                if evac:
                    n, U = L[name]["groups"], L.unroll(name)
                    i = (n - 2) // U
                    carry.append(lambda: evac(name, i, n - 1 - i * U))

            def flush():
                while carry:
                    carry.pop()()

            def add_to(dst):
                def evac(name, i, r):
                    dve.wait_ge(step_done, SPLIT + lin(name, i, r, L[name]["spg"] - 1) + 1)
                    d = flat(dst[:, bass.ds(GT * r + i * (GT * L.unroll(name)), GT), :])
                    nc.vector.tensor_tensor(d, bank2(acc(name, r)), d, ALU.add).then_inc(evacuated, 1)
                return evac

            def hidden_low(name, i, r):
                dve.wait_ge(hidH_ready, grp(name, i, r) - up_groups_before[name] + 1)
                at_ = bass.ds(GT * r + i * (GT * L.unroll(name)), GT)
                nc.vector.tensor_tensor(flat(hidL[:, at_, :]), hid[:, :], flat(hidH[:, at_, :]).bitcast(F32),
                                        ALU.subtract).then_inc(hidL_ready, 1)

            def rstd(n):
                dve.wait_ge(std_ready, n + 1)
                link(nc.vector.reciprocal(std[:, :], std[:, :]))

            def tiles(c):
                return range(GT * c, GT * (c + 1))

            def residual(n, coefficient, update):
                rstd(n)
                for c in range(KT // GT + 1):
                    if c < KT // GT:
                        for k in tiles(c):
                            ins = nc.vector.scalar_tensor_tensor(o[:, k, :], o[:, k, :], coef[:, coefficient, k:k + 1], std[:, :],
                                                                 ALU.mult, ALU.mult)
                        ins.then_inc(o_scaled, 1)
                    if c:
                        dve.wait_ge(o_scaled, 4 * update + c)
                        part = slice(GT * (c - 1), GT * c)
                        nc.vector.tensor_tensor(flat(x[:, part, :]), flat(x[:, part, :]), flat(o[:, part, :]), ALU.add
                                                ).then_inc(x_ready, 1)

            def inputs_low(n, m, coefficient, shift=None):
                rstd(n)
                for c in range(KT // GT + 1):
                    if c < KT // GT:
                        for k in tiles(c):
                            ins = nc.vector.scalar_tensor_tensor(sq[:, k, :], x[:, k, :], coef[:, coefficient, k:k + 1], std[:, :],
                                                                 ALU.mult, ALU.mult)
                        ins.then_inc(y_ready, 1)
                    if c:
                        dve.wait_ge(h_ready, 4 * m + c)
                        if shift is None:
                            part = slice(GT * (c - 1), GT * c)
                            ins = nc.vector.tensor_tensor(flat(actL[:, part, :]), flat(sq[:, part, :]),
                                                          flat(actH[:, part, :]).bitcast(F32), ALU.subtract)
                        else:
                            for k in tiles(c - 1):
                                ins = nc.vector.scalar_tensor_tensor(actL[:, k, :], sq[:, k, :], mod[:, shift, k:k + 1],
                                                                     actH[:, k, :].bitcast(F32), ALU.add, ALU.subtract)
                        ins.then_inc(act_ready, 1)

            def first_splits(name):
                for s in range(2):
                    split(name, 0, 0, s)

            def ada_step(g, s_, w, sums, i=0, per=0):
                for k in range(STEP_K):
                    n = s_ * STEP_K + k
                    if n < 2:
                        ins = nc.vector.tensor_scalar(sums[:, n % 2, :], w[:, k, :], csig[:, n:n + 1], None, ALU.mult)
                    else:
                        dve.wait_ge(ada_sum, STEP_K * RAW + 4 * STEP_K * g + n - 1 + i * (4 * STEP_K * per))
                        ins = nc.vector.scalar_tensor_tensor(sums[:, n % 2, :], w[:, k, :], csig[:, n:n + 1], sums[:, n % 2, :],
                                                             ALU.mult, ALU.add)
                    ins.then_inc(ada_sum, 1)

            def ada(g, i=0, per=0):
                dve.wait_ge(ada_rows, g + 1 + i * per)
                for s_ in range(4):
                    dve.wait_ge(raw_in[s_], ada_raw(g) + i * (16 * per))
                    ada_step(g, s_, raw[:, s_, :, :], ada_acc[:, g % 2, :, :], i, per)

            def beside_w_in(i, r, s):
                s_ = 4 * (r - 1) + s - 2
                if not 0 <= s_ < 4:
                    return
                g = L["ada_a"]["groups"]
                if s_ == 0:
                    dve.wait_ge(ada_rows, 2 + g + i)
                dve.wait_ge(side_in[s_], 16 + i * 16)
                ada_step(g, s_, side[:, s_, :, :], side_acc, i, 1)

            def ada_raw(g):
                n, m = L["ada_a"]["groups"], L["ada_a"]["groups"] + SIDE
                return 16 * (L["ada_a"]["t0"] // RAW + 1 + g) if g < n else 16 * (L["ada_b"]["t0"] // RAW + 1 + g - m)

            if 1 in blocks:
                dve.wait_ge(csig_ready, 1)
                link(nc.vector.tensor_tensor(csig[:, :], csig[:, :], cvec[:, :], ALU.mult))
                with dve.Fori(0, L["ada_a"]["groups"] // 2) as i:
                    for r in range(2):
                        ada(r, i, 2)
                dve.wait_ge(ada_rows, 2 + L["ada_a"]["groups"])
                psm = ps[:, 0, 0:6 * KT].rearrange("p (j k) -> p j k", k=KT)
                ins = nc.vector.tensor_tensor(mod[:, 0:2, :], psm[:, 0:2, :], b_ada[:, 0:2, :], ALU.add)
                link(ins)
                dve.sem_inc(mod_ready, 1)
                link(nc.vector.scalar_tensor_tensor(coef[:, 0, :], mod[:, 1, :], 1.0, vecs[:, 0, :], ALU.add, ALU.mult))
                inputs_low(0, 0, 0, 0)
                first_splits("w_in")
                dve.wait_ge(gw_hi, 1)
                nc.vector.tensor_tensor(gwL[:, :, :], gw[:, :, :], gwH[:, :, :].bitcast(F32), ALU.subtract
                                        ).then_inc(gw_lo, 1)
                layer("w_in", None, 2, beside_w_in)
                ada_next = [L["ada_a"]["groups"] + SIDE]
                c0, c1_ = L["ada_a"]["groups"] * GT, (L["ada_a"]["groups"] + SIDE) * GT
                dve.wait_ge(ada_rows, 2 + L["ada_a"]["groups"] + SIDE)
                nc.vector.tensor_tensor(flat(mod[:, :, :])[:, c0:c1_], ps[:, 6, c0:c1_], flat(b_ada[:, :, :])[:, c0:c1_], ALU.add)

                def ada_groups(n):
                    for _ in range(n):
                        ada(ada_next[0])
                        ada_next[0] += 1

                dve.wait_ge(evacuated, emptied("w_in"))
                ada_groups(2)
                for n, p in enumerate(rope_pairs):
                    dve.wait_ge(rotated, n + 1)
                    link(nc.vector.tensor_tensor(rope_s[:, n % 2, :, :], ps[:, 2 + n % 2, :].rearrange("p (a t) -> p a t", a=2),
                                                 sin.unsqueeze(1).to_broadcast([P, 2, T]), ALU.mult))
                    dve.wait_ge(rope_cos, n + 1)
                    nc.vector.tensor_tensor(proj[:, p:p + 2, :], rope_s[:, n % 2, :, :], rope_c[:, n % 2, :, :],
                                            ALU.add).then_inc(roped, 1)
                dve.wait_ge(cmp_in, 80)
                half_ = CMP_STRIDE
                for n, p in enumerate((KC, VC)):
                    for g in range(GROUPS):
                        for h in range(CMP_LEN // CMP_STRIDE):
                            rows = proj[:, p + g, h * half_:(h + NCMP) * half_].rearrange("p (b r) -> p r b", r=half_)
                            ins = nc.vector.tensor_tensor(xc[:, n, h * half_:(h + 1) * half_, g * NCMP:(g + 1) * NCMP], rows,
                                                          posk[:, n, h * half_:(h + 1) * half_].unsqueeze(2).to_broadcast(
                                                              [P, half_, NCMP]), ALU.add)
                ins.then_inc(xc_ready, 1)
                ada_groups(2)
                dve.wait_ge(cmp_sig, 1)
                nc.vector.tensor_tensor(flat(chtok[:, :, :]), ps[0:GROUPS * NCMP, 6, 0:2 * P], flat(chtok[:, :, :]), ALU.mult
                                        ).then_inc(cmp_hid, 1)

                def mask_max(b):
                    dve.wait_ge(scores, b + 1)
                    if b >= 2:
                        dve.wait_ge(pT_done, 2 * (b - 1))
                    if subs[b][0] == "cmp":
                        s = ps[:, 1, 0:TT * 4 * NCMP].rearrange("p (t h n) -> p t h n", t=TT, h=4)
                        for t in range(TT):
                            ins = nc.vector.tensor_tensor(pcmp[:, t, :, :], s[:, t, :, :],
                                                          unseen[:, t, :].unsqueeze(1).to_broadcast([P, 4, NCMP]), ALU.add)
                        link(ins)
                        for t in range(TT):
                            ins = nc.vector.tensor_reduce(nmx[:, b % 2, t, :], pcmp[:, t, :, :], AX.X, ALU.max)
                    else:
                        nc.vector.tensor_tensor(probs0[:, b % 2, :, :], ps[:, 1, :].rearrange("p (h n) -> p h n", h=4),
                                                causal[:, P:2 * P].unsqueeze(1).to_broadcast([P, 4, P]), ALU.add)
                        link(nc.vector.tensor_tensor(probs1[:, b % 2, :, :], bank2(2).rearrange("p (h n) -> p h n", h=4),
                                                     causal.unsqueeze(1).to_broadcast([P, 4, T]), ALU.add))
                        nc.vector.tensor_reduce(nmx[:, b % 2, 0, :], probs0[:, b % 2, :, :], AX.X, ALU.max)
                        ins = nc.vector.tensor_reduce(nmx[:, b % 2, 1, :], probs1[:, b % 2, :, :], AX.X, ALU.max)
                    link(ins)
                    nc.vector.tensor_scalar(nmx[:, b % 2, :, :], nmx[:, b % 2, :, :], -SCALE, None, ALU.mult
                                            ).then_inc(masked, 1)

                def weights_of(b):
                    kind, q, _, _, gk, _, _ = subs[b]
                    dve.wait_ge(exped, b + 1)
                    if kind == "cmp":
                        for t in range(TT):
                            ins = nc.vector.tensor_tensor(pcmp[:, t, :, :], pcmp[:, t, :, :],
                                                          seen[:, t, :].unsqueeze(1).to_broadcast([P, 4, NCMP]), ALU.mult)
                        link(ins)
                        for t in range(TT):
                            ins = nc.vector.tensor_reduce(rsum[:, b % 2, t, :], pcmp[:, t, :, :], AX.X, ALU.add)
                        link(ins)
                    r = rsum[:, b % 2, :, :]
                    link(nc.vector.tensor_scalar(r, r, 1e-30, None, ALU.max))
                    ins = nc.vector.reciprocal(r, r)
                    if gk is not None:
                        link(ins)
                        gt = gate[:, :, :].rearrange("p t (h c) -> p t h c", c=3)[:, :, q:q + 4, gk]
                        ins = nc.vector.tensor_tensor(r, r, gt, ALU.mult)
                    ins.then_inc(weight, 1)

                dve.wait_ge(gate_ready, 1)
                mask_max(0)
                for b in range(NSUB):
                    if b + 1 < NSUB:
                        mask_max(b + 1)
                    weights_of(b)
                    ada_groups(ADA_BESIDE[b])
                    if subs[b][6]:
                        g = out_of[b]
                        dve.wait_ge(oH_ready, g + 1)
                        nc.vector.tensor_tensor(flat(actL[:, 4 * g:4 * g + 4, :]), bank2(6),
                                                flat(actH[:, 4 * g:4 * g + 4, :]).bitcast(F32), ALU.subtract
                                                ).then_inc(oL_ready, 1)
                dve.wait_ge(ada_rows, 2 + 6 * KT // GT)
                link(nc.vector.tensor_tensor(flat(mod[:, :, :])[:, c1_:], ps[:, 0, c1_:6 * KT], flat(b_ada[:, :, :])[:, c1_:], ALU.add))
                dve.sem_inc(mod_ready, 1)
                nc.vector.tensor_tensor(coef[:, 1, :], mod[:, 2, :], vecs[:, 1, :], ALU.mult)
                nc.vector.scalar_tensor_tensor(coef[:, 2, :], mod[:, 4, :], 1.0, vecs[:, 2, :], ALU.add, ALU.mult)
                link(nc.vector.tensor_tensor(coef[:, 3, :], mod[:, 5, :], vecs[:, 3, :], ALU.mult))
                layer("w_o")
                first_splits("up_0")
                residual(1, 1, 0)
                inputs_low(2, 1, 2, 3)
                layer("up_0", hidden_low, 2)
                layer("down_0")
                layer("up_1", hidden_low)
                layer("down_1", add_to(o))
                flush()
                if 2 in blocks:
                    first_splits("w_in2")
                residual(3, 3, 1)

            def rwkv_turn(i):
                def wait(s, per, j):
                    dve.wait_ge(s, j + i * per)
                half = [slice(0, RHEAD), slice(RHEAD, P)]
                link(nc.vector.tensor_copy(rv[:, :, :], rwv10[:, :, bass.ds(i * RJ, RJ)]))
                link(nc.vector.memset(flat(ST[:, :, :]), 0.0))
                wait(shifted_z, 1, 1)
                for dst, d, m, base in ((rr, d0, MU_R, RR), (rk, d1, MU_K, RK), (rvv, d2, MU_V, RV)):
                    for j in range(RJ):
                        ins = nc.vector.scalar_tensor_tensor(dst[:, j, :], d[:, j, :], rv[:, m, j:j + 1],
                                                             proj2[:, bass.ds(base + j + i * RJ, 1), :].rearrange("p a t -> p (a t)"),
                                                             ALU.mult, ALU.add)
                link(ins)
                dve.sem_inc(mixed, 1)
                for j in range(RJ):
                    ins = nc.vector.tensor_scalar(kk[:, j, :], rk[:, j, :], rv[:, K_K, j:j + 1], None, ALU.mult)
                link(ins)
                dve.sem_inc(kk_ready, 1)
                wait(sig_ready, 1, 1)
                for j in range(RJ):
                    ins = nc.vector.tensor_tensor_scan(cs[:, j, :], reset, sg[:, j, :], 0.0, ALU.mult, ALU.add)
                link(ins)
                dve.sem_inc(cs_ready, 1)
                for j in range(RJ):
                    ins = nc.vector.tensor_scalar(k2[:, j, :], aa[:, j, :], 1.0, rv[:, K_A, j:j + 1], ALU.subtract, ALU.mult)
                link(ins)
                link(nc.vector.scalar_tensor_tensor(flat(k2[:, :, :]), flat(k2[:, :, :]), 1.0, flat(rk[:, :, :]), ALU.add, ALU.mult))
                dve.sem_inc(k2_ready, 1)
                wait(gexp, 1, 1)
                link(nc.vector.tensor_tensor(flat(cs[:, :, :]), flat(cs[:, :, :]), flat(sg[:, :, :]), ALU.subtract))
                dve.sem_inc(csp_ready, 1)
                wait(nrm_ready, 1, 1)
                link(nc.vector.tensor_scalar(flat(nrm[:, :, :]), flat(nrm[:, :, :]), 1e-12, None, ALU.max))
                link(nc.vector.reciprocal(flat(nrm[:, :, :]), flat(nrm[:, :, :])))
                link(nc.vector.tensor_tensor(flat(kk[:, :, :]), flat(kk[:, :, :]), flat(nrm[:, :, :]), ALU.mult))
                dve.sem_inc(kkn_ready, 1)
                link(nc.vector.tensor_tensor(flat(KTt[:, :, :]), flat(k2[:, :, :]), flat(Gi[:, :, :]), ALU.mult))
                wait(gp_ready, 1, 1)
                for h, part in enumerate(half):
                    ins = nc.vector.scalar_tensor_tensor(AR[h][part, :, :, 0, :].rearrange("p j i t -> p (j i) t"),
                                                         kk[part, :, :].rearrange("p j (i t) -> p (j i) t", i=TT), -1.0,
                                                         Gp[part, :, :].rearrange("p j (i t) -> p (j i) t", i=TT), ALU.mult, ALU.mult)
                link(ins)
                dve.sem_inc(a_ready, 1)
                wait(rk_ready, 1, 1)
                for j in range(RJ):
                    ins = nc.vector.tensor_scalar(rkk[:, j, :], rkk[:, j, :], rv[:, R_K, j:j + 1], None, ALU.mult)
                link(ins)
                dve.sem_inc(rk_scaled, 1)
                wait(bonus_sum, 1, 1)
                link(nc.vector.scalar_tensor_tensor(flat(bonus[:, :, :]), ps[:, 7, :], float(RHEAD), flat(rvv[:, :, :]),
                                                    ALU.mult, ALU.mult))
                dve.sem_inc(bonus_ready, 1)
                for n, dst in enumerate((Bc, Kc)):
                    for h in range(RHEADS):
                        wait(mat_done, 8, 4 * n + h + 1)
                        nc.vector.tensor_tensor(dst[:, 2 * h:2 * h + 2, :], ps[:, 4 * n + h, :].rearrange("p (i c) -> p i c", i=TT),
                                                token_mask.unsqueeze(1).to_broadcast([P, TT, 2 * P]), ALU.mult).then_inc(mat_masked, 1)
                wait(mat_masked, 8, 8)
                lab = Bc[:, :, 0:P]
                link(nc.vector.tensor_tensor(Ym[:, :, :], lab, level_mask[:, 0, :].unsqueeze(1).to_broadcast([P, MATS, P]), ALU.mult))
                link(nc.vector.tensor_tensor(Ym[:, :, :], Ym[:, :, :], ident.unsqueeze(1).to_broadcast([P, MATS, P]), ALU.add))
                dve.sem_inc(y1_ready, 1)
                for v in range(1, len(LEVELS)):
                    for f, m4 in enumerate(HALVES):
                        wait(dx_done, 10, 2 * v - 1 + f)
                        if v < len(LEVELS) - 1:
                            nc.vector.tensor_tensor(flat(Xm[:, m4, :]), flat(Xm[:, m4, :]), ps[:, 2 + f, :], ALU.add)
                        nc.vector.tensor_tensor(flat(Ym[:, m4, :]), flat(Ym[:, m4, :]), ps[:, 4 + f, :], ALU.add
                                                ).then_inc(level_ready, 1)
                for c in range(TT * 2):
                    wait(s_done, 4, c + 1)
                    link(nc.vector.tensor_tensor(flat(ST[:, :, :]), flat(ST[:, :, :]), ps[:, 2, 0:RJ * P], ALU.add))
                    end = (c + 1) * CHUNK - 1
                    link(nc.vector.tensor_tensor(ST[:, :, :], ST[:, :, :], Gd[:, :, end:end + 1].to_broadcast([P, RJ, P]), ALU.mult))
                    dve.sem_inc(st_ready, 1)
                wait(mean_done, 1, 1)
                link(nc.vector.tensor_tensor(flat(yb[:, :, :]), flat(yb[:, :, :]), ps[:, 7, :], ALU.subtract))
                dve.sem_inc(yc_ready, 1)
                wait(gstd_ready, 1, 1)
                link(nc.vector.reciprocal(flat(nrm[:, :, :]), flat(nrm[:, :, :])))
                link(nc.vector.tensor_tensor(flat(yb[:, :, :]), flat(yb[:, :, :]), flat(nrm[:, :, :]), ALU.mult))
                for j in range(RJ):
                    ins = nc.vector.tensor_scalar(yb[:, j, :], yb[:, j, :], rv[:, LN_W, j:j + 1], rv[:, LN_B, j:j + 1],
                                                  ALU.mult, ALU.add)
                link(ins)
                link(nc.vector.tensor_tensor(flat(yb[:, :, :]), flat(yb[:, :, :]), flat(bonus[:, :, :]), ALU.add))
                link(nc.vector.tensor_tensor(flat(yb[:, :, :]), flat(yb[:, :, :]), flat(gg[:, :, :]), ALU.mult))
                dve.sem_inc(yc_out, 1)
                wait(ycH_ready, 1, 1)
                at_ = bass.ds(2 * 4 + i * RJ, RJ)
                link(nc.vector.tensor_tensor(flat(yL[:, at_, :]), flat(yb[:, :, :]), flat(yH[:, at_, :]).bitcast(F32), ALU.subtract))
                dve.sem_inc(turn_done, 1)

            if 2 in blocks:
                if 1 not in blocks:
                    dve.wait_ge(consts_in, 64)
                link(nc.vector.tensor_copy(coef[:, 4:8, :], vecs[:, 4:8, :]))
                if 1 not in blocks:
                    first_splits("w_in2")
                inputs_low(NB, XB, 4)
                layer("w_in2", None, 2)
                u, e, up, dn = (cum[:, n, :] for n in range(4))
                dve.wait_ge(f_log, 1)
                link(nc.vector.tensor_scalar(u, u, -1.0, 0.0, ALU.mult, ALU.max))
                link(nc.vector.tensor_tensor(e, e, u, ALU.add))
                link(nc.vector.tensor_tensor_scan(u, ones[0:4, 0:1].to_broadcast([4, T]), e, 0.0, ALU.mult, ALU.add))
                nc.vector.tensor_scalar(up, u, 1.0 / SCALE, None, ALU.mult)
                link(nc.vector.tensor_scalar(dn, u, -1.0 / SCALE, None, ALU.mult))
                dve.sem_inc(cum_ready, 1)

                def masked2(b, mask, first, second):
                    dve.wait_ge(s2_done, b + 1)
                    nc.vector.tensor_tensor(first, ps[:, 1, :].rearrange("p (h n) -> p h n", h=4),
                                            mask[:, P:2 * P].unsqueeze(1).to_broadcast([P, 4, P]), ALU.add)
                    link(nc.vector.tensor_tensor(second, bank2(2).rearrange("p (h n) -> p h n", h=4),
                                                 mask.unsqueeze(1).to_broadcast([P, 4, T]), ALU.add))

                masked2(0, strict, prob0[:, 0, :, :], prob1[:, 0, :, :])
                dve.sem_inc(s2_masked, 1)
                masked2(1, causal, forget0[:, :, :], forget1[:, :, :])
                nc.vector.tensor_reduce(nmx[:, 0, 0, :], forget0[:, :, :], AX.X, ALU.max)
                link(nc.vector.tensor_reduce(nmx[:, 0, 1, :], forget1[:, :, :], AX.X, ALU.max))
                link(nc.vector.tensor_scalar(nmx[:, 0, :, :], nmx[:, 0, :, :], -SCALE, None, ALU.mult))
                dve.sem_inc(s2_masked, 1)
                for n, (so, pr, w) in enumerate(((soft0, prob0, P), (soft1, prob1, T))):
                    dve.wait_ge(s2_soft, n + 1)
                    link(nc.vector.tensor_tensor(flat(pr[:, 1, :, :]), flat(pr[:, 1, :, :]), flat(so[:, :, :]), ALU.add))
                    for h in range(4):
                        ins = nc.vector.tensor_tensor_scan(so[:, h, ::-1], ones[:, 0:1].to_broadcast([P, w]), pr[:, 1, h, ::-1], 0.0,
                                                           ALU.mult, ALU.add)
                    link(ins)
                    link(nc.vector.scalar_tensor_tensor(flat(pr[:, 0, :, :]), flat(pr[:, 0, :, :]), SCALE, flat(so[:, :, :]),
                                                        ALU.mult, ALU.subtract))
                dve.sem_inc(s2_sub, 1)

                def y_low(b):
                    dve.wait_ge(y2H_ready, b + 1)
                    nc.vector.tensor_tensor(flat(yL[:, 4 * b:4 * b + 4, :]), bank2(6), flat(yH[:, 4 * b:4 * b + 4, :]).bitcast(F32),
                                            ALU.subtract).then_inc(y2L_ready, 1)

                dve.wait_ge(s2_exp, 1)
                link(nc.vector.reciprocal(rsum[:, 0, :, :], rsum[:, 0, :, :]))
                dve.sem_inc(s2_weight, 1)
                y_low(0)
                y_low(1)
                dve.wait_ge(y2L_ready, 2)
                z = proj2[:, SPEC:SPEC + 3, :]
                d = at_spec[:, :, :]
                nc.vector.tensor_tensor(d[:, :, 1:T], z[:, :, 0:T - 1], z[:, :, 1:T], ALU.subtract)
                link(nc.vector.tensor_scalar(d[:, :, 0:1], z[:, :, 0:1], -1.0, None, ALU.mult))
                for j in range(3):
                    ins = nc.vector.scalar_tensor_tensor(z[:, j, :], d[:, j, :], mu_spec[:, j:j + 1], z[:, j, :], ALU.mult, ALU.add)
                link(ins)
                dve.sem_inc(spec_mixed, 1)
                for t_ in (AR[0], AR[1], btok, ktok):
                    ins = nc.vector.memset(t_[:, :, :, :, :], 0.0)
                link(nc.vector.memset(uf[:, :], 0.0))
                dve.sem_inc(zeroed, 1)
                dve.sem_inc(turn_done, 1)
                n0, K = link.n, RWKV_LINKS
                with dve.Fori(0, RTURNS) as i:
                    link.off = i * K
                    rwkv_turn(i)
                assert link.n - n0 == K, link.n - n0
                link.n, link.off = n0 + RTURNS * K, 0
                dve.wait_ge(turn_done, RTURNS + 1)
                layer("gates2")

                def gated(n, name, i, r):
                    dve.wait_ge(step_done, SPLIT + lin(name, i, r, (0, 1, 3)[n]) + 1)
                    g = flat(gates[:, bass.ds(16 * n + GT * r + i * (2 * GT), GT), :])
                    if n == 0:
                        nc.vector.tensor_tensor(mix[:, :], bank2(0), g, ALU.mult).then_inc(branch_used, 1)
                        return
                    nc.vector.tensor_tensor(mix_t[:, :], bank2(2 * n), g, ALU.mult).then_inc(branch_used, 1)
                    dve.wait_ge(branch_used, 3 * r + n + 1 + i * 6)
                    ins = nc.vector.tensor_tensor(mix[:, :], mix[:, :], mix_t[:, :], ALU.add)
                    if n == 1:
                        ins.then_inc(mixL_ready, 1)
                        dve.wait_ge(mixL_ready, 2 * r + 1 + i * 4)
                        return
                    ins.then_inc(mix_ready, 1)
                    dve.wait_ge(mixH_ready, r + 1 + i * 2)
                    at_ = bass.ds(GT * r + i * (2 * GT), GT)
                    nc.vector.tensor_tensor(flat(actL[:, at_, :]), mix[:, :], flat(actH[:, at_, :]).bitcast(F32), ALU.subtract
                                            ).then_inc(mixL_ready, 1)
                    dve.wait_ge(mixL_ready, 2 * r + 2 + i * 4)
                    dve.sem_inc(evacuated, 1)

                dve.wait_ge(evacuated, emptied("gates2"))

                def branch(i, r):
                    split("branch", i, r, 0)
                    split("branch", i, r, 1)
                    if not (isinstance(i, int) and i == 0 and r == 0):
                        gated(2, "branch", i, r - 1)
                    split("branch", i, r, 2)
                    gated(0, "branch", i, r)
                    split("branch", i, r, 3)
                    gated(1, "branch", i, r)

                over_groups(dve, "branch", 1, branch)
                gated(2, "branch", 1, 1)
                layer("w_out2")
                first_splits("up2_0")
                residual(NB + 1, 5, XB)
                inputs_low(NB + 2, XB + 1, 6)
                layer("up2_0", hidden_low, 2)
                layer("down2_0")
                layer("up2_1", hidden_low)
                layer("down2_1", add_to(o))
                flush()
                residual(NB + 3, 7, XB + 1)

        @block.gpsimd
        def _(pool):
            if 1 in blocks:
                pool.wait_ge(c1_in, 16)
                pool.wait_ge(evacuated, emptied("w_in"))
                for n, p in enumerate(rope_pairs):
                    if n >= 2:
                        pool.wait_ge(roped, n - 1)
                    nc.gpsimd.tensor_tensor(rope_c[:, n % 2, :, :], proj[:, p:p + 2, :],
                                            cos.unsqueeze(1).to_broadcast([P, 2, T]), ALU.mult).then_inc(rope_cos, 1)
                for b in range(NSUB):
                    pool.wait_ge(weight, b + 1)
                    for t in range(TT):
                        p = pcmp[:, t, :, :] if subs[b][0] == "cmp" else (probs0, probs1)[t][:, b % 2, :, :]
                        ins = nc.gpsimd.tensor_tensor(p, p, rsum[:, b % 2, t, :].unsqueeze(2).to_broadcast(list(p.shape)),
                                                      ALU.mult)
                    ins.then_inc(probs_ready, 1)
            if 2 in blocks:
                pool.wait_ge(s2_weight, 1)
                for t in range(TT):
                    p = (forget0, forget1)[t][:, :, :]
                    ins = nc.gpsimd.tensor_tensor(p, p, rsum[:, 0, t, :].unsqueeze(2).to_broadcast(list(p.shape)), ALU.mult)
                ins.then_inc(s2_probs, 1)
                pool.wait_ge(zeroed, 1)
                half = [slice(0, RHEAD), slice(RHEAD, P)]
                with pool.Fori(0, RTURNS) as i:
                    pool.wait_ge(turn_done, i + 1)
                    for d, base in ((d0, RR), (d1, RK), (d2, RV)):
                        z = proj2[:, bass.ds(base + i * RJ, RJ), :]
                        nc.gpsimd.tensor_tensor(d[:, :, 0:1], causal[:, 0:RJ].unsqueeze(2), z[:, :, 0:1], ALU.subtract)
                        ins = nc.gpsimd.tensor_tensor(d[:, :, 1:T], z[:, :, 0:T - 1], z[:, :, 1:T], ALU.subtract)
                    ins.then_inc(shifted_z, 1)
                    pool.wait_ge(mixed, 1 + i)
                    pool.wait_ge(gexp, 1 + i)
                    for h, part in enumerate(half):
                        for j in range(RJ):
                            nc.gpsimd.tensor_tensor(AR[h][part, j, :, 1, :], rr[part, j, :].rearrange("p (i t) -> p i t", i=TT),
                                                    Gd[part, j, :].rearrange("p (i t) -> p i t", i=TT), ALU.mult
                                                    ).then_inc(r_ready, 1)
                    pool.wait_ge(r_ready, 2 * RJ + i * (2 * RJ))
                    pool.wait_ge(kkn_ready, 1 + i)
                    pool.wait_ge(csp_ready, 1 + i)
                    nc.gpsimd.tensor_tensor(flat(ka[:, :, :]), flat(kk[:, :, :]), flat(aa[:, :, :]), ALU.mult).then_inc(pool_chain, 1)
                    pool.wait_ge(pool_chain, 1 + i)
                    nc.gpsimd.tensor_tensor(flat(BT[:, :, :]), flat(ka[:, :, :]), flat(Gi[:, :, :]), ALU.mult).then_inc(b_ready, 1)
                    pool.wait_ge(k2_ready, 1 + i)
                    nc.gpsimd.tensor_tensor(flat(rkk[:, :, :]), flat(rr[:, :, :]), flat(k2[:, :, :]), ALU.mult).then_inc(rk_ready, 1)
                    pool.wait_ge(mat_masked, 4 + i * 8)
                    for v in range(1, len(LEVELS)):
                        if v > 2:
                            pool.wait_ge(w1_done, 2 * (v - 2) + i * 10)
                        nc.gpsimd.tensor_tensor(Lm[:, v % 2, :, :], Bc[:, :, 0:P],
                                                level_mask[:, v, :].unsqueeze(1).to_broadcast([P, MATS, P]), ALU.mult
                                                ).then_inc(lm_ready, 1)

        @block.tensor
        def _(pe):
            pe.sem_inc(step_done, SPLIT)
            pe.sem_inc(evacuated, 2)

            def norm_part(n, c, src):
                pe.wait_ge(sq_ready, 4 * n + c + 1)
                for k in range(GT):
                    ins = nc.tensor.matmul(ps[:, 4, 0:T], ones, src[:, k, :], start=(c == 0 and k == 0), stop=(c == 3 and k == GT - 1))
                ins.then_inc(ssum_ready, 1)

            def pre_norm(n):
                for c in range(KT // GT):
                    norm_part(n, c, sq[:, GT * c:GT * (c + 1), :])

            def ada_total(g, i=0, per=0, sums=None, bank=0):
                pe.wait_ge(ada_sum, STEP_K * (RAW + 4 * (g + 1)) + i * (STEP_K * 4 * per))
                if sums is None:
                    sums = ada_acc[:, g % 2, :, :]
                for n in range(GT):
                    for j in range(2):
                        ins = nc.tensor.matmul(ps[:, bank, bass.ds(n + g * GT + i * (GT * per), 1)], sums[:, j, n * P:(n + 1) * P],
                                               ones[:, 0:1], start=(n == 0 and j == 0), stop=(j == 1), skip_group_check=True)
                ins.then_inc(ada_rows, 1)

            def layer(name, xH, xL, arrives=None, then_norm=None):
                spg = L[name]["spg"]
                pe.wait_ge(evacuated, 2 + L[name]["g0"])

                def body(i, r):
                    pe.wait_ge(evacuated, grp(name, i, r) + 1)
                    for s in range(spg):
                        if arrives and isinstance(i, int) and i == 0 and r == 0:
                            pe.wait_ge(arrives[0], arrives[1] + s + 1)
                        pe.wait_ge(wl_ready, RAW + lin(name, i, r, s) + 1)
                        b = s % SPLIT if spg > 1 else r % SPLIT
                        for k in range(STEP_K):
                            kk = s * STEP_K + k
                            for n in range(GT):
                                out = ps[:, acc(name, r) + n // 2, (n % 2) * T:(n % 2 + 1) * T]
                                cols = slice(n * P, (n + 1) * P)
                                for j, (w, v) in enumerate(((wH, xH), (wH, xL), (wL, xH))):
                                    ins = nc.tensor.matmul(out, w[:, b, k, cols], v[:, kk, :],
                                                           start=(kk == 0 and j == 0 and n % 2 == 0),
                                                           stop=(kk == STEP_K * spg - 1 and j == 2), skip_group_check=True)
                        ins.then_inc(step_done, 1)
                        if name == "w_in" and r == 2 and s == 2:
                            ada_total(L["ada_a"]["groups"], i, 1, side_acc, 6)
                    if then_norm is not None and r + i * L.unroll(name) > 0:
                        norm_part(then_norm, r + i * L.unroll(name) - 1, sq4)

                over_groups(pe, name, 1, body)
                if then_norm is not None:
                    norm_part(then_norm, L[name]["groups"] - 1, sq4)

            if 1 in blocks:
                pe.wait_ge(consts_in, 64)
                pre_norm(0)
                with pe.Fori(0, L["ada_a"]["groups"] // 2) as i:
                    for r in range(2):
                        ada_total(r, i, 2)
                layer("w_in", actH, actL, (act_ready, 0))
                pe.wait_ge(gw_lo, 1)
                for t in range(TT):
                    for k in range(KT):
                        for j, (v, w) in enumerate(((actH, gwH), (actL, gwH), (actH, gwL))):
                            ins = nc.tensor.matmul(ps[:, 5, t * GATES:(t + 1) * GATES], v[:, k, t * P:(t + 1) * P], w[:, k, :],
                                                   start=(t == 0 and k == 0 and j == 0), stop=(k == KT - 1 and j == 2),
                                                   skip_group_check=True)
                ins.then_inc(gate_done, 1)
                pe.wait_ge(evacuated, emptied("w_in"))
                ada_next = [L["ada_a"]["groups"] + SIDE]

                def ada_totals(n):
                    for _ in range(n):
                        ada_total(ada_next[0])
                        ada_next[0] += 1

                pe.wait_ge(c1_in, 16)
                for n, p in enumerate(rope_pairs):
                    if n >= 2:
                        pe.wait_ge(roped, n - 1)
                    nc.tensor.matmul(ps[:, 2 + n % 2, :], rot, flat(proj[:, p:p + 2, :]), start=True, stop=True
                                     ).then_inc(rotated, 1)
                    if n == 0:
                        ada_totals(2)
                pe.wait_ge(xc_ready, 1)
                for n in range(2):
                    for l in range(CMP_LEN):
                        ins = nc.tensor.matmul(ps[0:GROUPS * NCMP, 6, n * P:(n + 1) * P], xc[:, n, l, :], cw1[:, n, l, :],
                                               start=(n == 0 and l == 0), stop=(l == CMP_LEN - 1), skip_group_check=True)
                ins.then_inc(cmp_sum, 1)
                pe.wait_ge(gate_ready, 1)
                for n, p in enumerate(v_pairs):
                    if n >= 2:
                        pe.wait_ge(vtok_ready, n - 1)
                    for j in range(2):
                        for t in range(TT):
                            c = (2 * j + t) * P
                            ins = nc.tensor.transpose(ps[:, 4 + n % 2, c:c + P], proj[:, p + j, t * P:(t + 1) * P], ident)
                    ins.then_inc(vT_done, 1)
                ada_totals(2)
                pe.wait_ge(cmp_hid, 1)
                for n in range(2):
                    ins = nc.tensor.transpose(ps[:, 6, n * GROUPS * NCMP:(n + 1) * GROUPS * NCMP], chtok[:, n, :],
                                              ident[0:GROUPS * NCMP, 0:GROUPS * NCMP])
                ins.then_inc(cmp_T, 1)
                pe.wait_ge(cmp_hidT, 1)
                nc.tensor.matmul(ps[:, 7, 0:GROUPS * NCMP], cw2[:, 0, :], chid[:, 0, :], start=True, stop=True,
                                 skip_group_check=True)
                for g in range(GROUPS):
                    ins = nc.tensor.matmul(ps[0:NCMP, 7, 64 + g * P:64 + (g + 1) * P], chid[:, 1, g * NCMP:(g + 1) * NCMP],
                                           cw2[:, 1, :], start=False, stop=True, skip_group_check=True)
                ins.then_inc(cmp_kv, 1)

                def score(b):
                    kind, q, kt, _, _, _, _ = subs[b]
                    if b >= 1:
                        pe.wait_ge(masked, b)
                    if b >= 2:
                        pe.wait_ge(pT_ready, 2 * (b - 1))
                    if kind == "cmp":
                        for t in range(TT):
                            for h in range(4):
                                c = (t * 4 + h) * NCMP
                                ins = nc.tensor.matmul(ps[:, 1, c:c + NCMP], proj[:, q + h, t * P:(t + 1) * P],
                                                       kcT[:, kt * NCMP:(kt + 1) * NCMP], start=(t == 0 and h == 0), stop=True,
                                                       skip_group_check=True)
                    else:
                        for h in range(4):
                            nc.tensor.matmul(ps[:, 1, h * P:(h + 1) * P], proj[:, q + h, 0:P], proj[:, kt[h], 0:P],
                                             start=(h == 0), stop=True, skip_group_check=True)
                        for h in range(4):
                            ins = nc.tensor.matmul(ps[:, 2 + h // 2, (h % 2) * T:(h % 2 + 1) * T], proj[:, q + h, P:T],
                                                   proj[:, kt[h], :], start=(h % 2 == 0), stop=True, skip_group_check=True)
                    ins.then_inc(scores, 1)

                def transposes(b):
                    kind = subs[b][0]
                    pe.wait_ge(probs_ready, b + 1)
                    if kind == "cmp":
                        for h in range(4):
                            for t in range(TT):
                                c = (h % 2) * T + t * P
                                ins = nc.tensor.transpose(ps[0:NCMP, 4 + h // 2, c:c + P], pcmp[:, t, h, :], ident)
                        ins.then_inc(pT_done, 2)
                        return
                    for h in range(4):
                        c = (h % 2) * T
                        nc.tensor.transpose(ps[:, 4 + h // 2, c:c + P], probs0[:, b % 2, h, :], ident)
                        ins = nc.tensor.transpose(ps[:, 4 + h // 2, c + P:c + T], probs1[:, b % 2, h, 0:P], ident)
                    ins.then_inc(pT_done, 1)
                    if b + 1 < NSUB:
                        pe.wait_ge(masked, b + 2)
                    for h in range(4):
                        ins = nc.tensor.transpose(ps[:, 1, h * P:(h + 1) * P], probs1[:, b % 2, h, P:T], ident)
                    ins.then_inc(pT_done, 1)

                def values(b):
                    kind, _, g, vs, _, first, last = subs[b]
                    if first and out_of[b]:
                        pe.wait_ge(oL_ready, out_of[b])
                    pe.wait_ge(pT_ready, 2 * b + 2)
                    for h in range(4):
                        out = ps[:, 6 + h // 2, (h % 2) * T:(h % 2 + 1) * T]
                        if kind == "cmp":
                            ins = nc.tensor.matmul(out, vc[:, g, :], pcT[:, h, :], start=False, stop=last, skip_group_check=True)
                        else:
                            nc.tensor.matmul(out, vtok[:, vs[h], 0, :], pT0[:, h, :], start=(first and h % 2 == 0), stop=False,
                                             skip_group_check=True)
                            ins = nc.tensor.matmul(out[:, P:T], vtok[:, vs[h], 1, :], pT1[:, h, :], start=False, stop=last,
                                                   skip_group_check=True)
                    ins.then_inc(pv_done, 1)

                pe.wait_ge(cmp_ready, GROUPS)
                pe.wait_ge(vtok_ready, len(v_pairs))
                pe.wait_ge(roped, len(rope_pairs))
                score(0)
                for b in range(NSUB):
                    if b + 1 < NSUB:
                        score(b + 1)
                    if b:
                        ada_totals(ADA_BESIDE[b - 1])
                    transposes(b)
                    values(b)
                ada_totals(ADA_BESIDE[-1])
                pe.wait_ge(oL_ready, 4)
                pe.wait_ge(mod_ready, 2)
                layer("w_o", actH, actL, None, 1)
                pre_norm(2)
                layer("up_0", actH, actL, (act_ready, 4))
                layer("down_0", hidH, hidL, (hidL_ready, 1))
                layer("up_1", actH, actL)
                layer("down_1", hidH, hidL, (hidL_ready, 9), 3)

            def rwkv_turn(i):
                def wait(s, per, j):
                    pe.wait_ge(s, j + i * per)
                hs = [(h // 2, h % 2) for h in range(RHEADS)]
                wait(lw_in, 64, 64)
                for j in range(RJ):
                    c = slice(j * P, (j + 1) * P)
                    t = slice(j * T, (j + 1) * T)
                    nc.tensor.matmul(ps[:, 0, t], lw[0:64, 0, c], proj2[0:64, SPEC, :], start=(j == 0), stop=True, skip_group_check=True)
                for j in range(RJ):
                    c = slice(j * P, (j + 1) * P)
                    t = slice(j * T, (j + 1) * T)
                    nc.tensor.matmul(ps[:, 1, t], lw[64:P, 0, c], proj2[64:P, SPEC, :], start=(j == 0), stop=True, skip_group_check=True)
                for j in range(RJ):
                    c = slice(j * P, (j + 1) * P)
                    t = slice(j * T, (j + 1) * T)
                    nc.tensor.matmul(ps[:, 2, t], lw[:, 1, c], proj2[:, SPEC + 1, :], start=(j == 0), stop=False, skip_group_check=True)
                for j in range(RJ):
                    c = slice(j * P, (j + 1) * P)
                    t = slice(j * T, (j + 1) * T)
                    ins = nc.tensor.matmul(ps[:, 2, t], lw[96:P, 2, c], proj2[96:P, SPEC + 2, :], start=False, stop=True,
                                           skip_group_check=True)
                ins.then_inc(lora_done, 1)
                wait(kksq, 1, 1)
                nc.tensor.matmul(ps[:, 3, :], same_head, flat(nrm[:, :, :]), start=True, stop=True).then_inc(kksum, 1)
                wait(mixed, 1, 1)
                for n, src in enumerate((rvv, BT, KTt)):
                    if n == 1:
                        wait(b_ready, 1, 1)
                    if n == 2:
                        wait(a_ready, 1, 1)
                    for t in range(TT):
                        for j in range(RJ):
                            c = (t * RJ + j) * P
                            ins = nc.tensor.transpose(ps[:, 4 + n, c:c + P], src[:, j, t * P:(t + 1) * P], ident)
                    ins.then_inc(tok_done, 1)
                wait(rk_scaled, 1, 1)
                nc.tensor.matmul(ps[:, 7, :], same_head, flat(rkk[:, :, :]), start=True, stop=True).then_inc(bonus_sum, 1)
                wait(sig_ready, 1, 1)
                wait(nrm_ready, 1, 1)
                wait(rk_ready, 1, 1)
                for n, src in enumerate((BT, KTt)):
                    if n:
                        wait(tok_ready, 3, 3)
                        wait(bonus_ready, 1, 1)
                    for h, (j, hh) in enumerate(hs):
                        for t in range(TT):
                            ins = nc.tensor.matmul(ps[:, 4 * n + h, t * 2 * P:(t + 1) * 2 * P], src[:, j, t * P:(t + 1) * P],
                                                   AR[hh][:, j, t, :, :].rearrange("p a t -> p (a t)"), start=(t == 0), stop=True,
                                                   skip_group_check=True)
                        ins.then_inc(mat_done, 1)
                wait(y1_ready, 1, 1)

                def each(f, out, lhs, rhs_):
                    for m in range(4 * f, 4 * f + 4):
                        ins = nc.tensor.matmul(ps[:, out + f, m % 4 * P:(m % 4 + 1) * P], lhs[:, m, :], rhs_[:, m, :],
                                               start=(m % 4 == 0), stop=True, skip_group_check=True)
                    return ins

                for f in range(2):
                    for m in range(4 * f, 4 * f + 4):
                        ins = nc.tensor.transpose(ps[:, f, m % 4 * P:(m % 4 + 1) * P], Ym[:, m, :], ident)
                    ins.then_inc(x1_done, 1)
                for v in range(1, len(LEVELS)):
                    wait(lm_ready, 5, v)
                    for f in range(2):
                        if v > 1:
                            wait(level_ready, 10, 2 * v - 3 + f)
                        else:
                            wait(x1_ready, 2, f + 1)
                        each(f, 0, Lm[:, v % 2, :, :], Xm).then_inc(w1_done, 1)
                    for f in range(2):
                        wait(w1_ready, 10, 2 * v - 1 + f)
                        if v < len(LEVELS) - 1:
                            each(f, 2, Ym, W1)
                        each(f, 4, W1, Ym).then_inc(dx_done, 1)
                wait(level_ready, 10, 10)
                for c in range(TT * 2):
                    t, o_ = c // 2, c % 2 * CHUNK
                    if c:
                        wait(st_ready, 4, c)
                    for h, (j, hh) in enumerate(hs):
                        out = ps[:, 0, h * RHEAD:(h + 1) * RHEAD]
                        nc.tensor.matmul(out, AR[hh][:, j, t, 0, :], ST[:, j, hh * RHEAD:(hh + 1) * RHEAD], start=(h == 0), stop=False,
                                         skip_group_check=True)
                        ins = nc.tensor.matmul(out, Kc[:, 2 * h + t, 0:P], rtok[:, t, j, hh * RHEAD:(hh + 1) * RHEAD], start=False,
                                               stop=True, skip_group_check=True)
                    ins.then_inc(rhs_done, 1)
                    for h, (j, hh) in enumerate(hs):
                        part = slice(hh * RHEAD, (hh + 1) * RHEAD)
                        nc.tensor.matmul(ps[part, 6, j * T + c * CHUNK:j * T + (c + 1) * CHUNK], ST[:, j, part],
                                         AR[hh][:, j, t, 1, o_:o_ + CHUNK], start=(c == 0 and j == 0), stop=False, skip_group_check=True)
                    wait(rhs_ready, 4, c + 1)
                    for h in range(RHEADS):
                        ins = nc.tensor.matmul(ps[:, 1, h * RHEAD:(h + 1) * RHEAD], Ym[:, 2 * h + t, :], rhs[:, h * RHEAD:(h + 1) * RHEAD],
                                               start=(h == 0), stop=True, skip_group_check=True)
                    ins.then_inc(u_done, 1)
                    wait(u_ready, 4, c + 1)
                    for j in range(RJ):
                        out = ps[:, 2, j * P:(j + 1) * P]
                        nc.tensor.matmul(out, btok[:, c % 2, t, j, :], uf[:, j * P:(j + 1) * P], start=(j == 0), stop=False,
                                         skip_group_check=True)
                        ins = nc.tensor.matmul(out, ktok[:, c % 2, t, j, :], rtok[:, t, j, :], start=False, stop=True,
                                               skip_group_check=True)
                    ins.then_inc(s_done, 1)
                    if c % 2:
                        for h, (j, hh) in enumerate(hs):
                            part = slice(hh * RHEAD, (hh + 1) * RHEAD)
                            out = ps[part, 6, j * T + t * P:j * T + (t + 1) * P]
                            nc.tensor.matmul(out, uf[:, h * RHEAD:(h + 1) * RHEAD], Bc[:, 2 * h + t, P:2 * P], start=False, stop=False,
                                             skip_group_check=True)
                            ins = nc.tensor.matmul(out, rtok[:, t, j, part], Kc[:, 2 * h + t, P:2 * P], start=False, stop=True,
                                                   skip_group_check=True)
                        ins.then_inc(ysum_done, 1)
                wait(yb_ready, 1, 1)
                nc.tensor.matmul(ps[:, 7, :], same_head, flat(yb[:, :, :]), start=True, stop=True).then_inc(mean_done, 1)
                wait(ysq_ready, 1, 1)
                nc.tensor.matmul(ps[:, 7, :], same_head, flat(ysq[:, :, :]), start=True, stop=True).then_inc(var_done, 1)

            if 2 in blocks:
                if 1 not in blocks:
                    pe.wait_ge(consts_in, 64)
                pre_norm(NB)
                layer("w_in2", actH, actL, (act_ready, 4 * XB))
                pe.wait_ge(evacuated, emptied("w_in2"))
                for n, p in enumerate((SBV, SBV + 2, FXV, FXV + 2)):
                    if n >= 2:
                        pe.wait_ge(v2_ready, n - 1)
                    for j in range(2):
                        for t in range(TT):
                            c = (2 * j + t) * P
                            ins = nc.tensor.transpose(ps[:, 4 + n % 2, c:c + P], proj2[:, p + j, t * P:(t + 1) * P], ident)
                    ins.then_inc(v2T_done, 1)

                def score2(q, k, forget):
                    for t in range(TT):
                        w = P * (t + 1)
                        for h in range(4):
                            out = ps[:, 1, h * P:(h + 1) * P] if t == 0 else ps[:, 2 + h // 2, (h % 2) * T:(h % 2 + 1) * T]
                            ts = slice(t * P, (t + 1) * P)
                            ins = nc.tensor.matmul(out, proj2[:, q + h, ts], proj2[:, k + h, 0:w],
                                                   start=(h % (4, 2)[t] == 0), stop=not forget, skip_group_check=True)
                            if forget:
                                pick = ident[0:4, h:h + 1]
                                nc.tensor.matmul(out, cum[:, 3, ts], pick.to_broadcast([4, w]), start=False, stop=False,
                                                 skip_group_check=True)
                                ins = nc.tensor.matmul(out, pick.to_broadcast([4, P]), cum[:, 2, 0:w], start=False, stop=True,
                                                       skip_group_check=True)
                    ins.then_inc(s2_done, 1)

                def outputs2(b, first, second):
                    for h in range(4):
                        c = (h % 2) * T
                        nc.tensor.transpose(ps[:, 4 + h // 2, c:c + P], first[:, h, :], ident)
                        ins = nc.tensor.transpose(ps[:, 4 + h // 2, c + P:c + T], second[:, h, 0:P], ident)
                    ins.then_inc(t2_done, 1)
                    for h in range(4):
                        ins = nc.tensor.transpose(ps[:, 1, h * P:(h + 1) * P], second[:, h, P:T], ident)
                    ins.then_inc(t2_done, 1)
                    pe.wait_ge(t2_ready, 2 * b + 2)
                    if b:
                        pe.wait_ge(y2L_ready, b)
                    for h in range(4):
                        out = ps[:, 6 + h // 2, (h % 2) * T:(h % 2 + 1) * T]
                        nc.tensor.matmul(out, vtok2[:, 4 * b + h, 0, :], qT0[:, h, :], start=(h % 2 == 0), stop=False,
                                         skip_group_check=True)
                        ins = nc.tensor.matmul(out[:, P:T], vtok2[:, 4 * b + h, 1, :], qT1[:, h, :], start=False, stop=True,
                                               skip_group_check=True)
                    ins.then_inc(o2_done, 1)

                score2(SBQ, SBK, False)
                pe.wait_ge(v2_ready, 4)
                pe.wait_ge(cum_ready, 1)
                pe.wait_ge(s2_masked, 1)
                score2(FXQ, FXK, True)
                pe.wait_ge(s2_masked, 2)
                pe.wait_ge(s2_exp, 2)
                outputs2(0, prob0[:, 0, :, :], prob1[:, 0, :, :])
                pe.wait_ge(s2_probs, 1)
                outputs2(1, forget0, forget1)
                pe.wait_ge(y2L_ready, 2)
                pe.wait_ge(spec_ready, 1)
                pe.wait_ge(zeroed, 1)
                with pe.Fori(0, RTURNS) as i:
                    pe.wait_ge(turn_done, i + 1)
                    rwkv_turn(i)
                pe.wait_ge(turn_done, RTURNS + 1)
                layer("gates2", actH, actL)
                pe.wait_ge(evacuated, emptied("gates2"))

                def branch(i, r):
                    for s, (n, k0, start, stop) in enumerate(((0, 0, True, True), (1, 4, True, True), (2, 8, True, False), (2, 12, False, True))):
                        pe.wait_ge(wl_ready, RAW + lin("branch", i, r, s) + 1)
                        if start and not (isinstance(i, int) and i == 0 and r == 0):
                            pe.wait_ge(branch_used, 3 * (r - 1) + n + 1 + i * 6)
                        b = s % SPLIT
                        for k in range(STEP_K):
                            for m in range(GT):
                                out = ps[:, 2 * n + m // 2, (m % 2) * T:(m % 2 + 1) * T]
                                cols = slice(m * P, (m + 1) * P)
                                for j, (w, v) in enumerate(((wH, yH), (wH, yL), (wL, yH))):
                                    ins = nc.tensor.matmul(out, w[:, b, k, cols], v[:, k0 + k, :],
                                                           start=(start and k == 0 and j == 0 and m % 2 == 0),
                                                           stop=(stop and k == STEP_K - 1 and j == 2), skip_group_check=True)
                        ins.then_inc(step_done, 1)

                over_groups(pe, "branch", 1, branch)
                layer("w_out2", actH, actL, None, NB + 1)
                pre_norm(NB + 2)
                layer("up2_0", actH, actL, (act_ready, 4 * XB + 4))
                layer("down2_0", hidH, hidL, (hidL_ready, UB + 1))
                layer("up2_1", actH, actL)
                layer("down2_1", hidH, hidL, (hidL_ready, UB + 9), NB + 3)


def host_layout(inputs):
    given = {n: np.asarray(v) for n, v in inputs.items()}

    def own(n):
        return given[n][0]

    def col(v):
        return v.reshape(-1, P).T

    d = {"x": own("x").T, "c": col(given["c"]), "common": common_consts(), "c1": first_consts(), "c2": second_consts(),
         "vecs": np.stack([col(own(n)) for n in VECS], 1), "b_ada": col(own("b_ada")).reshape(P, 6, KT),
         "pos": np.stack([own("cmp_k_pos").T, own("cmp_v_pos").T], 1)}
    for n in ("w_ada", "w_o", "w_up", "w_down", "cmp_k_w1", "cmp_k_w2", "cmp_v_w1", "cmp_v_w2", "rwkv_w_up_2", "rwkv_a_up_2",
              "rwkv_g_up_2", "w_branch_a_2", "w_branch_b_2", "w_branch_c_2", "w_out_2", "w_mlp_up_2", "w_mlp_down_2"):
        d[n] = own(n)
    w, g0 = own("w_in"), QM * P
    d["w_in"], d["w_gate"] = np.concatenate([w[:, :g0], w[:, g0 + GATES:]], 1), w[:, g0:g0 + GATES]
    w = own("w_in_2")
    f0 = RR * P
    r0 = f0 + FORGET_H
    n0 = r0 + 3 * RW
    end = n0 + P + GATE_RANK
    d["w_in_2"] = np.concatenate([w[:, :f0], w[:, r0:n0], w[:, n0:n0 + 2 * P], w[:, end - P:end], w[:, f0:f0 + P]], 1)
    d["w_gates_2"] = w[:, end:]
    mu, m0 = own("rwkv_mu_2"), 3 * RW
    forget = np.zeros((P, 1), np.float32)
    forget[:FORGET_H, 0] = own("b_forget_2")
    d["rwv"] = np.concatenate(
        [col(mu[:m0]), *[col(own(f"rwkv_{n}_2")) for n in ("w0", "a0", "k_k", "k_a", "r_k", "ln_w", "ln_b")],
         col(mu[m0:m0 + P]), col(mu[m0 + P:m0 + 2 * P]), col(mu[-P:]), forget, np.full((P, 1), GN_EPS, np.float32)], 1)
    return {n: np.ascontiguousarray(v) for n, v in d.items()}


def kernel(**inputs):
    import concourse.bacc as bacc
    from concourse.bass_utils import run_bass_kernel_spmd

    nc = bacc.Bacc("TRN2", target_bir_lowering=False, num_devices=1)
    arrays = host_layout(inputs)
    args = {n: nc.dram_tensor(n, v.shape, F32, kind="ExternalInput").ap() for n, v in arrays.items()}
    args["out"] = nc.dram_tensor("out", (D, T), F32, kind="ExternalOutput").ap()
    build_program(nc, args)
    r = run_bass_kernel_spmd(nc, [arrays], core_ids=[0])
    return np.ascontiguousarray(r.results[0]["out"].T)[None]
```

```python
from contextlib import ExitStack

import numpy as np

import concourse.bass as bass
from concourse import mybir

F32 = mybir.dt.float32
F32R = mybir.dt.float32r
ACT = mybir.ActivationFunctionType
ALU = mybir.AluOpType
AX = mybir.AxisListType

P = 128
D = 2048
T = 256
KT = D // P
TT = T // P
DH = 128
D_FF = 4 * D
HT = D_FF // 2 // P
EPS = 1e-6
SCALE = DH ** -0.5
NEG = -1e30

STEP_K = 4
GC = 512
GT = GC // P
RAW, SPLIT = 4, 2
SIDE = 5

CMP_LEN, CMP_STRIDE = 32, 16
NCMP = (T - CMP_LEN) // CMP_STRIDE + 1
NSA_H, GROUPS = 8, 2

QN, KC, VC, KS, VS, KW, VW, QM, KM, VM = 0, 8, 10, 12, 14, 16, 18, 20, 28, 36
PROJ1 = 44
GATES = 3 * NSA_H

SBQ, SBK, SBV, FXQ, FXK, FXV, RR, RK, RV, SPEC = 0, 4, 8, 12, 16, 20, 24, 32, 40, 48
PROJ2 = 52
RW = 1024
RT_ = RW // P
CHUNK = 64
LEVELS = [1, 2, 4, 8, 16, 32]
RHEAD = 64
RJ = 2
RTURNS = RT_ // RJ
RHEADS = 2 * RJ
HALVES = slice(0, RHEADS), slice(RHEADS, 2 * RHEADS)
MATS = RHEADS * TT
GN_EPS = 64e-5
FORGET_H, GATE_RANK = 4, 160
DECAY = float(np.exp(-0.5))
MU_R, MU_K, MU_V, W0, A0, K_K, K_A, R_K, LN_W, LN_B = range(10)


RWKV_LINKS = 34


class Layers:

    def __init__(self, layers):
        self.at = {}
        t = lin = ada = g = 0
        for name, kind, groups, spg in layers:
            self.at[name] = dict(kind=kind, groups=groups, spg=spg, t0=t, l0=lin, a0=ada, g0=g)
            assert t % RAW == 0
            n = groups * spg
            t += n * (kind != "side")
            if kind == "lin":
                lin += n
                g += groups
            else:
                ada += n
        self.order = [x[0] for x in layers]

    def __getitem__(self, name):
        return self.at[name]

    def unroll(self, name):
        L = self.at[name]
        return 1 if L["kind"] == "ada" else max(2, RAW // L["spg"])


def first_consts():
    pos = np.arange(T, dtype=np.float32)
    inv = (np.float32(10000.0) ** (-np.arange(0, DH, 2, dtype=np.float32) / np.float32(DH))).astype(np.float32)
    ang = inv[:, None] * pos[None, :]
    cos, sin = np.cos(ang).astype(np.float32), np.sin(ang).astype(np.float32)
    h = DH // 2
    rot = np.zeros((P, P), np.float32)
    rot[np.arange(h) + h, np.arange(h)] = -1
    rot[np.arange(h), np.arange(h) + h] = 1
    cend = np.arange(NCMP) * CMP_STRIDE + CMP_LEN - 1
    tok = np.arange(T).reshape(TT, P).T
    seen = (cend[None, None, :] <= tok[:, :, None]).astype(np.float32)
    return np.concatenate([rot, np.tile(cos, (2, 1)), np.tile(sin, (2, 1)), seen.reshape(P, -1),
                           ((1 - seen) * np.float32(NEG)).reshape(P, -1)], axis=1)


def common_consts():
    i = np.arange(P)
    causal = np.where(i[None, :] <= i[:, None], 0, NEG).astype(np.float32)
    return np.concatenate([np.eye(P, dtype=np.float32), np.ones((P, P), np.float32), np.zeros((P, P), np.float32),
                           causal, np.full((P, 1), EPS, np.float32)], axis=1)


def second_consts():
    i = np.arange(P)
    strict = np.where(i[None, :] < i[:, None], 0, NEG).astype(np.float32)
    same_head = (i[:, None] // RHEAD == i[None, :] // RHEAD).astype(np.float32) / np.float32(RHEAD)
    same = i[:, None] // CHUNK == i[None, :] // CHUNK
    before = same & (i[:, None] < i[None, :])
    upto = same & (i[:, None] <= i[None, :])
    levels = [(i[:, None] // (2 * b) == i[None, :] // (2 * b)) & (i[:, None] // b % 2 == 0) & (i[None, :] // b % 2 == 1)
              for b in LEVELS]
    reset = np.tile((np.arange(T) % CHUNK != 0), (P, 1))
    return np.concatenate([np.zeros((P, P)), strict, same_head, before, upto, *levels, reset], axis=1).astype(np.float32)


VECS = ["pre_norm_mix", "post_norm_mix", "pre_norm_ffn", "post_norm_ffn",
        "norm_mix_pre_2", "norm_mix_post_2", "norm_mlp_pre_2", "norm_mlp_post_2"]


def build_program(nc, a):
    layers = [("ada_a", "ada", 8, 4), ("w_in", "lin", PROJ1 // GT, 4), ("ada_w", "side", SIDE, 4),
              ("ada_b", "ada", 16 - SIDE, 4), ("w_o", "lin", 4, 4),
              ("up_0", "lin", 8, 4), ("down_0", "lin", 4, 8), ("up_1", "lin", 8, 4), ("down_1", "lin", 4, 8),
              ("w_in2", "lin", PROJ2 // GT, 4), ("gates2", "lin", 12, 4), ("branch", "lin", 4, 4), ("w_out2", "lin", 4, 4),
              ("up2_0", "lin", 8, 4), ("down2_0", "lin", 4, 8), ("up2_1", "lin", 8, 4), ("down2_1", "lin", 4, 8)]
    L = Layers(layers)

    def matrix(ap):
        return ap.rearrange("(k p) n -> p k n", p=P)

    w_ada, w_up, w_down = matrix(a["w_ada"]), matrix(a["w_up"]), matrix(a["w_down"])
    w_up2, w_down2 = matrix(a["w_mlp_up_2"]), matrix(a["w_mlp_down_2"])
    weights = {"ada_a": (w_ada, 0, 0), "ada_b": (w_ada, 0, (8 + SIDE) * GC), "w_in": (matrix(a["w_in"]), 0, 0),
               "w_o": (matrix(a["w_o"]), 0, 0), "up_0": (w_up, 0, 0), "up_1": (w_up, 0, D_FF // 2),
               "down_0": (w_down, 0, 0), "down_1": (w_down, HT, 0),
               "w_in2": (matrix(a["w_in_2"]), 0, 0), "gates2": (matrix(a["w_gates_2"]), 0, 0),
               "w_out2": (matrix(a["w_out_2"]), 0, 0), "up2_0": (w_up2, 0, 0), "up2_1": (w_up2, 0, D_FF // 2),
               "down2_0": (w_down2, 0, 0), "down2_1": (w_down2, HT, 0)}

    top = [16512]

    def at(name, shape, dt, offset):
        return nc.alloc_sbuf_tensor_at(name, shape, dt, offset=offset)

    def new(name, shape, dt=F32):
        off = top[0]
        n = 4 * int(np.prod(shape[1:]))
        top[0] = (off + n + 31) // 32 * 32
        return at(name, shape, dt, off)

    X0 = top[0]
    x = new("x", [P, KT, T])
    ACT0 = top[0]
    actH = new("actH", [P, KT, T], F32R)
    actL = new("actL", [P, KT, T], F32R)
    RING0 = top[0]
    raw = new("raw", [P, RAW, STEP_K, GC])
    SPLIT0 = top[0]
    wH = new("wH", [P, SPLIT, STEP_K, GC], F32R)
    wL = new("wL", [P, SPLIT, STEP_K, GC], F32R)
    ada_acc = at("ada_acc", [P, 2, 2, GC], F32, SPLIT0 + 4 * SPLIT * STEP_K * GC)
    common = new("common", [P, 4 * P + 1])
    ident, ones = common[:, 0:P], common[:, P:2 * P]
    eps = common[:, 4 * P:]
    causal = common[:, 2 * P:4 * P]
    vecs = new("vecs", [P, len(VECS), KT])
    mod = new("mod", [P, 6, KT])
    b_ada = new("b_ada", [P, 6, KT])
    cvec = new("cvec", [P, KT])
    csig = new("csig", [P, KT])
    coef = new("coef", [P, 8, KT])
    nmx = new("nmx", [P, 2, TT, 4])
    rsum = new("rsum", [P, 2, TT, 4])
    B0 = top[0]
    R0 = 229368 // 32 * 32 - 84 * 1024 - 512
    std = at("std", [P, T], F32, R0 + 83 * 1024)
    NC1 = P + 2 * T + 2 * TT * NCMP
    c1 = at("c1", [P, NC1], F32, B0)
    rot, cos, sin = c1[:, 0:P], c1[:, P:P + T], c1[:, P + T:P + 2 * T]
    seen = c1[:, P + 2 * T:P + 2 * T + TT * NCMP].rearrange("p (t n) -> p t n", t=TT)
    unseen = c1[:, P + 2 * T + TT * NCMP:].rearrange("p (t n) -> p t n", t=TT)
    assert B0 + 4 * NC1 <= R0, (B0 + 4 * NC1, R0)

    hidH = at("hidH", [P, HT, T], F32R, R0)
    hidL = at("hidL", [P, HT, T], F32R, R0 + 32 * 1024)
    o = at("o", [P, KT, T], F32, R0 + 64 * 1024)
    hid = at("hid_sq", [P, GT * T], F32, R0 + 80 * 1024)
    sq = at("sq", [P, KT, T], F32, R0)
    sq4 = at("sq4", [P, GT, T], F32, R0 + 80 * 1024)
    K1 = 1024
    proj = at("proj", [P, PROJ1, T], F32, R0)
    vtok = at("vtok", [P, 12, TT, P], F32, R0 + 44 * K1)
    probs0 = at("probs0", [P, 2, 4, P], F32, R0 + 56 * K1)
    probs1 = at("probs1", [P, 2, 4, T], F32, R0 + 60 * K1)
    pT0 = at("pT0", [P, 4, T], F32, R0 + 68 * K1)
    pT1 = at("pT1", [P, 4, P], F32, R0 + 72 * K1)
    rope_c = at("rope_c", [P, 2, 2, T], F32, SPLIT0)
    rope_s = at("rope_s", [P, 2, 2, T], F32, SPLIT0 + 4 * K1)
    xc = at("xc", [P, 2, CMP_LEN, GROUPS * NCMP], F32, SPLIT0 + 8 * K1)
    GW0 = (B0 + 4 * NC1 + 31) // 32 * 32
    gw = at("gw", [P, KT, GATES], F32, GW0)
    gwH = at("gwH", [P, KT, GATES], F32R, GW0 + 4 * KT * GATES)
    assert GW0 + 8 * KT * GATES <= R0
    gwL = at("gwL", [P, KT, GATES], F32R, R0 + 76 * K1)
    chtok = at("chtok", [GROUPS * NCMP, 2, P], F32, R0 + 78 * K1)
    gate = at("gate", [P, TT, GATES], F32, R0 + 80 * K1)
    posk = at("posk", [P, 2, CMP_LEN], F32, R0 + 80 * K1 + 256)
    cw2 = at("cw2", [P, 2, P], F32, R0 + 80 * K1 + 512)
    chid = at("chid", [P, 2, GROUPS * NCMP], F32, R0 + 80 * K1 + 1568)
    kcT = at("kcT", [P, GROUPS * NCMP], F32, R0 + 80 * K1 + 1824)
    vc = at("vc", [NCMP, GROUPS, P], F32, R0 + 80 * K1 + 1952)
    pcmp = at("pcmp", [P, TT, 4, NCMP], F32, R0 + 74 * K1)
    pcT = at("pcT", [NCMP, 4, T], F32, R0 + 75 * K1)
    cw1 = at("cw1", [P, 2, CMP_LEN, P], F32, ACT0)
    side = at("side", [P, 4, STEP_K, GC], F32, R0 + 44 * K1)
    side_acc = at("side_acc", [P, 2, GC], F32, R0 + 78 * K1)

    NC2 = 5 * P + len(LEVELS) * P + T
    c2 = at("c2", [P, NC2], F32, B0)
    strict, same_head = c2[:, 0:2 * P], c2[:, 2 * P:3 * P]
    token_mask = c2[:, 3 * P:5 * P]
    level_mask = c2[:, 5 * P:(5 + len(LEVELS)) * P].rearrange("p (l n) -> p l n", l=len(LEVELS))
    reset = c2[:, (5 + len(LEVELS)) * P:]
    rwv = at("rwv", [P, 10 * RT_ + 5], F32, B0 + 4 * NC2)
    rwv10 = rwv[:, 0:10 * RT_].rearrange("p (v j) -> p v j", v=10)
    mu_spec, b_forget, gn_eps = rwv[:, 10 * RT_:10 * RT_ + 3], rwv[0:4, 10 * RT_ + 3:10 * RT_ + 4], rwv[:, 10 * RT_ + 4:]
    rv = at("rv", [P, 10, RJ], F32, B0 + 4 * NC2 + 352)
    assert B0 + 4 * NC2 + 352 + 80 <= R0
    mix_t = at("mix_t", [P, GT * T], F32, B0)
    proj2 = at("proj2", [P, PROJ2, T], F32, R0)
    gates = at("gates", [P, 48, T], F32, R0)
    mix = at("mix", [P, GT * T], F32, R0 + 48 * K1)
    yH = at("yH", [P, KT, T], F32R, R0 + 52 * K1)
    yL = at("yL", [P, KT, T], F32R, R0 + 68 * K1)
    vtok2 = at("vtok2", [P, 8, TT, P], F32, SPLIT0)
    prob0 = at("prob0", [P, 2, 4, P], F32, SPLIT0 + 8 * K1)
    prob1 = at("prob1", [P, 2, 4, T], F32, SPLIT0 + 12 * K1)
    qT0 = at("qT0", [P, 4, T], F32, SPLIT0 + 20 * K1)
    qT1 = at("qT1", [P, 4, P], F32, SPLIT0 + 24 * K1)
    soft0 = at("soft0", [P, 4, P], F32, SPLIT0 + 26 * K1)
    soft1 = at("soft1", [P, 4, T], F32, SPLIT0 + 28 * K1)
    cum = at("cum", [4, 4, T], F32, RING0)
    forget0 = at("forget0", [P, 4, P], F32, RING0 + 4 * K1)
    forget1 = at("forget1", [P, 4, T], F32, RING0 + 6 * K1)
    rtop = [RING0]

    def ring(name, shape):
        off = rtop[0]
        rtop[0] += 4 * int(np.prod(shape[1:]))
        assert rtop[0] <= RING0 + 64 * K1
        return at(name, shape, F32, off)

    Bc, Kc = ring("Bc", [P, MATS, 2 * P]), ring("Kc", [P, MATS, 2 * P])
    Xm, Ym, W1 = ring("Xm", [P, MATS, P]), ring("Ym", [P, MATS, P]), ring("W1", [P, MATS, P])
    Lm = ring("Lm", [P, 2, MATS, P])
    AR = [ring(f"AR{h}", [P, RJ, TT, 2, P]) for h in range(2)]
    btok, ktok = ring("btok", [P, 2, TT, RJ, P]), ring("ktok", [P, 2, TT, RJ, P])
    rtok = ring("rtok", [P, TT, RJ, P])
    rhs, uf, ST = ring("rhs", [P, RHEADS * RHEAD]), ring("uf", [P, RHEADS * RHEAD]), ring("ST", [P, RJ, P])
    lw = ring("lw", [P, 3, RJ * P])
    BT, KTt = ring("BT", [P, RJ, T]), ring("KT", [P, RJ, T])
    rr, rk, rvv, d0, d1, d2, sg, aa, gg, cs, Gd, Gi = (
        at(n, [P, RJ, T], F32, R0 + 2 * K1 * j) for j, n in enumerate(
            ("rr", "rk", "rvv", "d0", "d1", "d2", "sg", "aa", "gg", "cs", "Gd", "Gi")))
    at_spec = at("spec_d", [P, 3, T], F32, RING0 + 60 * K1)
    kk, nrm, k2, ka, rkk = d0, d1, d2, sg, d1
    Gp, bonus, gate_now, yb, ysq, spread = (
        at(n, [P, RJ, T], F32, X0 + 2 * K1 * j) for j, n in enumerate(("Gp", "bonus", "gate_now", "yb", "ysq", "spread")))
    Gend = at("Gend", [P, RJ, 2 * TT], F32, X0 + 12 * K1)

    ps = nc.alloc_psum_tensor("ps", [P, 8, 512], F32)

    def flat(ap):
        return ap.rearrange("p a b -> p (a b)")

    def bank2(b):
        return flat(ps[:, b:b + 2, :])

    with ExitStack() as ctx:
        def sem(name):
            return ctx.enter_context(nc.semaphore(name))


        raw_in = [sem(f"raw_in{s}") for s in range(RAW)]
        wh_ready, wl_ready, step_done = sem("wh_ready"), sem("wl_ready"), sem("step_done")
        ada_sum, ada_rows, evacuated = sem("ada_sum"), sem("ada_rows"), sem("evacuated")
        consts_in, x_in, c1_in = sem("consts_in"), sem("x_in"), sem("c1_in")
        side_in = [sem(f"side_in{n}") for n in range(4)]
        csig_ready, mod_ready = sem("csig_ready"), sem("mod_ready")
        sq_ready, ssum_ready, std_ready = sem("sq_ready"), sem("ssum_ready"), sem("std_ready")
        y_ready, h_ready, act_ready, x_ready = sem("y_ready"), sem("h_ready"), sem("act_ready"), sem("x_ready")
        o_scaled = sem("o_scaled")
        dve_chain, act_chain, pool_chain = sem("dve_chain"), sem("act_chain"), sem("pool_chain")
        gw_in, gw_hi, gw_lo, gate_done, gate_ready = (sem(n) for n in ("gw_in", "gw_hi", "gw_lo", "gate_done", "gate_ready"))
        rotated, rope_cos, roped = sem("rotated"), sem("rope_cos"), sem("roped")
        vT_done, vtok_ready = sem("vT_done"), sem("vtok_ready")
        cmp_in, xc_ready, cmp_sum, cmp_sig, cmp_hid, cmp_T, cmp_hidT, cmp_kv, cmp_ready = (
            sem(n) for n in ("cmp_in", "xc_ready", "cmp_sum", "cmp_sig", "cmp_hid", "cmp_T", "cmp_hidT", "cmp_kv", "cmp_ready"))
        scores, masked, exped, weight, probs_ready = (
            sem(n) for n in ("scores", "masked", "exped", "weight", "probs_ready"))
        pT_done, pT_ready, pv_done, oH_ready, oL_ready = (
            sem(n) for n in ("pT_done", "pT_ready", "pv_done", "oH_ready", "oL_ready"))
        sqr_ready, hidH_ready, hidL_ready = sem("sqr_ready"), sem("hidH_ready"), sem("hidL_ready")
        out_sem = sem("out_stored")
        c2_in, lw_in, x_out, x_back = sem("c2_in"), sem("lw_in"), sem("x_out"), sem("x_back")
        v2T_done, v2_ready, f_log, cum_ready = sem("v2T_done"), sem("v2_ready"), sem("f_log"), sem("cum_ready")
        s2_done, s2_masked, s2_soft, s2_sub, s2_exp, s2_weight, s2_probs = (
            sem(n) for n in ("s2_done", "s2_masked", "s2_soft", "s2_sub", "s2_exp", "s2_weight", "s2_probs"))
        t2_done, t2_ready, o2_done, y2H_ready, y2L_ready = (
            sem(n) for n in ("t2_done", "t2_ready", "o2_done", "y2H_ready", "y2L_ready"))
        spec_mixed, spec_ready, zeroed, turn_done = sem("spec_mixed"), sem("spec_ready"), sem("zeroed"), sem("turn_done")
        shifted_z, mixed, lora_done, sig_ready, kk_ready, kksq, kksum, nrm_ready = (
            sem(n) for n in ("shifted_z", "mixed", "lora_done", "sig_ready", "kk_ready", "kksq", "kksum", "nrm_ready"))
        cs_ready, gexp, k2_ready, kkn_ready, a_ready, b_ready = (
            sem(n) for n in ("cs_ready", "gexp", "k2_ready", "kkn_ready", "a_ready", "b_ready"))
        rk_scaled, bonus_sum, bonus_ready, tok_done, tok_ready = (
            sem(n) for n in ("rk_scaled", "bonus_sum", "bonus_ready", "tok_done", "tok_ready"))
        mat_done, mat_masked, y1_ready, x1_done, x1_ready, lm_ready = (
            sem(n) for n in ("mat_done", "mat_masked", "y1_ready", "x1_done", "x1_ready", "lm_ready"))
        w1_done, w1_ready, dx_done, level_ready = (sem(n) for n in ("w1_done", "w1_ready", "dx_done", "level_ready"))
        rhs_done, rhs_ready, u_done, u_ready, s_done, st_ready, ysum_done = (
            sem(n) for n in ("rhs_done", "rhs_ready", "u_done", "u_ready", "s_done", "st_ready", "ysum_done"))
        r_ready = sem("r_ready")
        yb_ready, mean_done, yc_ready, ysq_ready, var_done, gstd_ready, yc_out, ycH_ready = (
            sem(n) for n in ("yb_ready", "mean_done", "yc_ready", "ysq_ready", "var_done", "gstd_ready", "yc_out", "ycH_ready"))
        mix_ready, mixH_ready, mixL_ready, branch_used = (
            sem(n) for n in ("mix_ready", "mixH_ready", "mixL_ready", "branch_used"))
        NB = 4
        UB = 16
        XB = 2

        class Chain:

            def __init__(self, eng, s):
                self.eng, self.s, self.n, self.off = eng, s, 0, 0

            def __call__(self, ins):
                self.n += 1
                ins.then_inc(self.s, 1)
                self.eng.wait_ge(self.s, self.off + self.n)

        def over_groups(eng, name, first, body):
            U, n = L.unroll(name), L[name]["groups"]
            for r in range(first):
                body(0, r)
            turns = (n - first) // U
            if turns > 1:
                with eng.Fori(0, turns) as i:
                    for r in range(U):
                        body(i, first + r)
            elif turns:
                for r in range(U):
                    body(0, first + r)
            for r in range(n - first - turns * U):
                body(turns, first + r)

        def raw_loads(name, i, r, s):
            l, U = L[name], L.unroll(name)
            j = r * l["spg"] + s
            return j % RAW, 16 * (l["t0"] // RAW + j // RAW + 1) + i * (16 * U * l["spg"] // RAW)

        def lin(name, i, r, s=0):
            l, U = L[name], L.unroll(name)
            return l["l0"] + r * l["spg"] + s + i * (U * l["spg"])

        def grp(name, i, r):
            return L[name]["g0"] + r + i * L.unroll(name)

        def done(name):
            l = L[name]
            return SPLIT + l["l0"] + l["groups"] * l["spg"]

        def emptied(name):
            return 2 + L[name]["g0"] + L[name]["groups"]

        def acc(name, r):
            return 2 * ((L[name]["g0"] + r) % 2)

        subs = []
        for g in range(GROUPS):
            q = QN + 4 * g
            subs += [("full", q, [KS + g] * 4, [0 + g] * 4, 1, True, False),
                     ("full", q, [KW + g] * 4, [2 + g] * 4, 2, False, False),
                     ("cmp", q, g, None, 0, False, True)]
        for m in range(2):
            subs.append(("full", QM + 4 * m, [KM + 4 * m + h for h in range(4)], [4 + 4 * m + h for h in range(4)],
                         None, True, True))
        out_of = [g for g, n in ((0, 3), (1, 3), (2, 1), (3, 1)) for _ in range(n)]
        NSUB = len(subs)
        ADA_BEFORE, ADA_BESIDE = (1, 1), (2, 1, 1, 1, 1, 1, 1, 1)
        assert len(ADA_BESIDE) == NSUB and sum(ADA_BEFORE + ADA_BESIDE) == 16 - SIDE
        rope_pairs = [QN, QN + 2, QN + 4, QN + 6, KC, KS, KW] + list(range(QM, VM, 2))
        v_pairs = [VS, VW] + list(range(VM, PROJ1, 2))

        up_groups_before = {}
        seen_up = 0
        for name in L.order:
            if name.startswith("up"):
                up_groups_before[name] = L[name]["g0"] - seen_up
                seen_up += L[name]["groups"]

        block = ctx.enter_context(nc.Block())

        @block.sync
        def _(sp):
            sp.dma_start(cvec[:, :], a["c"]).then_inc(consts_in, 16)
            sp.dma_start(common[:, :], a["common"]).then_inc(consts_in, 16)
            sp.dma_start(vecs[:, :, :], a["vecs"]).then_inc(consts_in, 16)
            sp.dma_start(b_ada[:, :, :], a["b_ada"]).then_inc(consts_in, 16)
            sp.dma_start(x[:, :, :], matrix(a["x"])).then_inc(x_in, 16)

            def stream(name):
                l, U = L[name], L.unroll(name)
                w, k0, n0 = weights[name]

                def body(i, r):
                    for s in range(l["spg"]):
                        slot, _ = raw_loads(name, i, r, s)
                        if l["kind"] == "ada":
                            sp.wait_ge(ada_sum, STEP_K * (l["a0"] + r * 4 + s + 1) + i * (STEP_K * 4))
                        else:
                            sp.wait_ge(wl_ready, lin(name, i, r, s) + 1)
                        sp.dma_start(raw[:, slot, :, :],
                                     w[:, k0 + s * STEP_K:k0 + (s + 1) * STEP_K, bass.ds(n0 + r * GC + i * (U * GC), GC)]
                                     ).then_inc(raw_in[slot], 16)
                        if name == "w_in" and r == 1:
                            side_g = L["ada_a"]["groups"]
                            sp.wait_ge(ada_sum, STEP_K * (4 * side_g + s + 1) + i * (4 * STEP_K))
                            sp.dma_start(side[:, s, :, :], w_ada[:, s * STEP_K:(s + 1) * STEP_K,
                                                                 bass.ds(side_g * GC + i * GC, GC)]).then_inc(side_in[s], 16)

                if l["kind"] == "ada":
                    if l["l0"]:
                        sp.wait_ge(wl_ready, RAW + l["l0"])
                elif l["a0"]:
                    sp.wait_ge(ada_sum, STEP_K * (RAW + l["a0"]))
                over_groups(sp, name, 0, body)

            stream("ada_a")
            sp.dma_start(c1[:, :], a["c1"]).then_inc(c1_in, 16)
            sp.dma_start(gw[:, :, :], matrix(a["w_gate"])).then_inc(gw_in, 16)
            stream("w_in")
            for name in ("ada_b", "w_o", "up_0", "down_0", "up_1", "down_1"):
                stream(name)
            sp.wait_ge(roped, len(rope_pairs))
            sp.wait_ge(oL_ready, 4)
            sp.dma_start(c2[:, :], a["c2"]).then_inc(c2_in, 16)
            sp.dma_start(rwv[:, :], a["rwv"]).then_inc(c2_in, 16)
            stream("w_in2")
            sp.wait_ge(y_ready, 4 * (XB + 1))
            sp.dma_start(matrix(a["out"]), x[:, :, :]).then_inc(x_out, 16)
            sp.wait_ge(zeroed, 1)
            with sp.Fori(0, RTURNS) as i:
                sp.wait_ge(lora_done, 1 + 3 * i)
                for part, src in ((slice(0, 64), "rwkv_w_up_2"), (slice(64, P), "rwkv_a_up_2")):
                    sp.dma_start(lw[part, 0, :], a[src][:, bass.ds(i * (RJ * P), RJ * P)]).then_inc(lw_in, 16)
                sp.dma_start(lw[:, 1, :], a["rwkv_g_up_2"][0:P, bass.ds(i * (RJ * P), RJ * P)]).then_inc(lw_in, 16)
                sp.dma_start(lw[96:P, 2, :], a["rwkv_g_up_2"][P:P + 32, bass.ds(i * (RJ * P), RJ * P)]).then_inc(lw_in, 16)
            sp.wait_ge(turn_done, RTURNS + 1)
            sp.wait_ge(x_out, 16)
            stream("gates2")
            sp.dma_start(x[:, :, :], matrix(a["out"])).then_inc(x_back, 16)
            wa, wb, wc = (matrix(a[f"w_branch_{n}_2"]) for n in "abc")

            def branch_loads(i, r):
                for s, (w, k) in enumerate(((wa, 0), (wb, 0), (wc, 0), (wc, STEP_K))):
                    slot, _ = raw_loads("branch", i, r, s)
                    sp.wait_ge(wl_ready, lin("branch", i, r, s) + 1)
                    sp.dma_start(raw[:, slot, :, :], w[:, k:k + STEP_K, bass.ds(r * GC + i * (2 * GC), GC)]
                                 ).then_inc(raw_in[slot], 16)

            over_groups(sp, "branch", 0, branch_loads)
            for name in ("w_out2", "up2_0", "down2_0", "up2_1", "down2_1"):
                stream(name)
            for c in range(KT // GT):
                sp.wait_ge(x_ready, 4 * (2 * XB - 1) + c + 1)
                sp.dma_start(matrix(a["out"])[:, GT * c:GT * (c + 1), :], x[:, GT * c:GT * (c + 1), :]).then_inc(out_sem, 16)
            sp.wait_ge(out_sem, 16 * (KT // GT))

        @block.scalar
        def _(act):
            act.sem_inc(gstd_ready, 1)
            chain = Chain(act, act_chain)

            def split(name, i, r, s):
                slot, count = raw_loads(name, i, r, s)
                act.wait_ge(raw_in[slot], count)
                act.wait_ge(step_done, lin(name, i, r, s) + 1)
                nc.scalar.activation(wH[:, s % SPLIT if L[name]["spg"] > 1 else r % SPLIT, :, :], raw[:, slot, :, :],
                                     ACT.Copy).then_inc(wh_ready, 1)

            def last_group(name, evac):
                n, U = L[name]["groups"], L.unroll(name)
                i = (n - 2) // U
                evac(name, i, n - 1 - i * U)

            def layer(name, evac=None, done=0, when=1, before=None):
                spg = L[name]["spg"]

                def body(i, r):
                    peeled = isinstance(i, int) and i == 0 and r == 0
                    for s in range(spg):
                        if not (peeled and s < done):
                            split(name, i, r, s)
                        if before and peeled and s == min(1, spg - 1):
                            last_group(*before)
                        if evac and s == min(when, spg - 1) and not peeled:
                            evac(name, i, r - 1)

                over_groups(act, name, 1, body)

            def copy_to(dst, func=ACT.Copy):
                def evac(name, i, r):
                    act.wait_ge(step_done, SPLIT + lin(name, i, r, L[name]["spg"] - 1) + 1)
                    nc.scalar.activation(flat(dst[:, bass.ds(GT * r + i * (GT * L.unroll(name)), GT), :]),
                                         bank2(acc(name, r)), func).then_inc(evacuated, 1)
                return evac

            def square_relu(name, i, r):
                act.wait_ge(step_done, SPLIT + lin(name, i, r, L[name]["spg"] - 1) + 1)
                g = grp(name, i, r) - up_groups_before[name] + 1
                act.wait_ge(hidL_ready, g)
                nc.scalar.activation(hid[:, :], bank2(acc(name, r)), ACT.Relu).then_inc(evacuated, 1)
                act.wait_ge(evacuated, 2 + grp(name, i, r) + 1)
                nc.scalar.activation(hid[:, :], hid[:, :], ACT.Square).then_inc(sqr_ready, 1)
                act.wait_ge(sqr_ready, g)
                nc.scalar.activation(flat(hidH[:, bass.ds(GT * r + i * (GT * L.unroll(name)), GT), :]), hid[:, :],
                                     ACT.Copy).then_inc(hidH_ready, 1)

            def squares(n, c, src, dst):
                nc.scalar.activation(flat(dst[:, :, :]), flat(src[:, GT * c:GT * (c + 1), :]), ACT.Square).then_inc(sq_ready, 1)

            def copy_square(n):
                def evac(name, i, r):
                    c = r + i * L.unroll(name)
                    copy_to(o)(name, i, r)
                    act.wait_ge(evacuated, 2 + grp(name, i, r) + 1)
                    square_of(n)(name, i, r)
                return evac

            def square_of(n):
                def evac(name, i, r):
                    c = r + i * L.unroll(name)
                    act.wait_ge(evacuated, 2 + grp(name, i, r) + 1)
                    if c:
                        act.wait_ge(ssum_ready, 4 * n + c)
                    squares(n, c, o, sq4)
                return evac

            def root(n):
                act.wait_ge(ssum_ready, 4 * (n + 1))
                nc.scalar.activation(std[:, :], ps[:, 4, 0:T], ACT.Sqrt, bias=eps, scale=1.0 / D).then_inc(std_ready, 1)

            def pre_norm(n, update):
                for c in range(KT // GT):
                    if update:
                        act.wait_ge(x_ready, 4 * (update - 1) + c + 1)
                    elif c == 0:
                        act.wait_ge(x_in, 16)
                    squares(n, c, x, sq[:, GT * c:GT * (c + 1), :])
                root(n)

            def inputs_high(m, shift=None):
                for c in range(KT // GT):
                    act.wait_ge(y_ready, 4 * m + c + 1)
                    if shift is None:
                        ins = nc.scalar.activation(flat(actH[:, GT * c:GT * (c + 1), :]), flat(sq[:, GT * c:GT * (c + 1), :]), ACT.Copy)
                    else:
                        for k in range(GT * c, GT * (c + 1)):
                            ins = nc.scalar.activation(actH[:, k, :], sq[:, k, :], ACT.Identity, bias=mod[:, shift, k:k + 1])
                    ins.then_inc(h_ready, 1)

            def between(n, name, last):
                split(name, 0, 0, 0)
                last_group(*last)
                split(name, 0, 0, 1)
                root(n)
                pre_norm(n + 1, (n + 1) // 2)

            act.wait_ge(consts_in, 64)
            nc.scalar.activation(csig[:, :], cvec[:, :], ACT.Sigmoid).then_inc(csig_ready, 1)
            pre_norm(0, 0)
            for s in range(2):
                split("w_in", 0, 0, s)
            act.wait_ge(mod_ready, 1)
            inputs_high(0, 0)
            act.wait_ge(gw_in, 16)
            nc.scalar.activation(gwH[:, :, :], gw[:, :, :], ACT.Copy).then_inc(gw_hi, 1)
            layer("w_in", copy_to(proj), 2)
            last_group("w_in", copy_to(proj))
            act.wait_ge(gate_done, 1)
            nc.scalar.activation(gate[:, :, :], ps[:, 5, 0:TT * GATES].rearrange("p (t g) -> p t g", t=TT),
                                 ACT.Sigmoid).then_inc(gate_ready, 1)
            act.dma_start(cw1[:, 0, :, :], a["cmp_k_w1"].rearrange("(l d) h -> d l h", d=P)).then_inc(cmp_in, 16)
            act.dma_start(cw1[:, 1, :, :], a["cmp_v_w1"].rearrange("(l d) h -> d l h", d=P)).then_inc(cmp_in, 16)
            act.dma_start(posk[:, :, :], a["pos"]).then_inc(cmp_in, 16)
            act.dma_start(cw2[:, 0, :], a["cmp_k_w2"]).then_inc(cmp_in, 16)
            act.dma_start(cw2[:, 1, :], a["cmp_v_w2"]).then_inc(cmp_in, 16)
            for n in range(len(v_pairs)):
                act.wait_ge(vT_done, n + 1)
                nc.scalar.activation(vtok[:, 2 * n:2 * n + 2, :, :].rearrange("p a t d -> p (a t d)"),
                                     ps[:, 4 + n % 2, :], ACT.Copy).then_inc(vtok_ready, 1)
            act.wait_ge(cmp_sum, 1)
            nc.scalar.activation(flat(chtok[:, :, :]), ps[0:GROUPS * NCMP, 6, 0:2 * P], ACT.Sigmoid).then_inc(cmp_sig, 1)
            act.wait_ge(cmp_T, 1)
            nc.scalar.activation(flat(chid[:, :, :]), ps[:, 6, 0:2 * GROUPS * NCMP], ACT.Copy).then_inc(cmp_hidT, 1)
            act.wait_ge(cmp_kv, 1)
            nc.scalar.activation(kcT[:, :], ps[:, 7, 0:GROUPS * NCMP], ACT.Copy)
            for g in range(GROUPS):
                nc.scalar.activation(vc[:, g, :], ps[0:NCMP, 7, 64 + g * P:64 + (g + 1) * P], ACT.Copy
                                     ).then_inc(cmp_ready, 1)

            def exps(b):
                kind = subs[b][0]
                act.wait_ge(masked, b + 1)
                for t in range(TT):
                    for h in range(4):
                        p = pcmp[:, t, h, :] if kind == "cmp" else (probs0, probs1)[t][:, b % 2, h, :]
                        bias = nmx[:, b % 2, t, h:h + 1]
                        if kind == "cmp":
                            ins = nc.scalar.activation(p, p, ACT.Exp, bias=bias, scale=SCALE)
                        else:
                            ins = nc.scalar.activation(p, p, ACT.Exp, bias=bias, scale=SCALE,
                                                       accum_out=rsum[:, b % 2, t, h:h + 1])
                ins.then_inc(exped, 1)

            def take_pT(b):
                act.wait_ge(pT_done, 2 * b + 1)
                if b:
                    act.wait_ge(pv_done, b)
                if subs[b][0] == "cmp":
                    nc.scalar.activation(flat(pcT[:, :, :]), flat(ps[0:NCMP, 4:6, :]), ACT.Copy).then_inc(pT_ready, 2)
                    return
                nc.scalar.activation(flat(pT0[:, :, :]), bank2(4), ACT.Copy).then_inc(pT_ready, 1)
                act.wait_ge(pT_done, 2 * b + 2)
                nc.scalar.activation(flat(pT1[:, :, :]), ps[:, 1, :], ACT.Copy).then_inc(pT_ready, 1)

            exps(0)
            for b in range(NSUB):
                if b + 1 < NSUB:
                    exps(b + 1)
                take_pT(b)
                if subs[b][6]:
                    act.wait_ge(pv_done, b + 1)
                    g = out_of[b]
                    nc.scalar.activation(flat(actH[:, 4 * g:4 * g + 4, :]), bank2(6), ACT.Copy).then_inc(oH_ready, 1)
            layer("w_o", copy_square(1))
            between(1, "up_0", ("w_o", copy_square(1)))
            inputs_high(1, 3)
            layer("up_0", square_relu, 2)
            layer("down_0", copy_to(o), before=("up_0", square_relu))
            layer("up_1", square_relu, before=("down_0", copy_to(o)))
            layer("down_1", square_of(3), when=4, before=("up_1", square_relu))

            def rwkv_early(i, ahead, part):
                def wait(s, per, j):
                    act.wait_ge(s, j + ahead * per + i * per)
                if part == 0:
                    wait(mixed, 1, 1)
                    for n, (dst, v) in enumerate(((sg, W0), (aa, A0))):
                        wait(lora_done, 3, n + 2)
                        for j in range(RJ):
                            ins = nc.scalar.activation(dst[:, j, :], ps[:, 3 + n, j * T:(j + 1) * T], ACT.Sigmoid, bias=rv[:, v, j:j + 1])
                        ins.then_inc(sig_ready, 1)
                if part == 1:
                    wait(lora_done, 3, 4)
                    nc.scalar.activation(flat(gg[:, :, :]), ps[:, 5, :], ACT.Copy).then_inc(sig_ready, 1)
                    wait(kk_ready, 1, 1)
                    nc.scalar.activation(flat(nrm[:, :, :]), flat(kk[:, :, :]), ACT.Square).then_inc(kksq, 1)
                if part == 2:
                    wait(kksum, 1, 1)
                    nc.scalar.activation(flat(nrm[:, :, :]), ps[:, 3, :], ACT.Sqrt, scale=float(RHEAD)).then_inc(nrm_ready, 1)
                if part == 3:
                    wait(cs_ready, 1, 1)
                    nc.scalar.activation(flat(Gd[:, :, :]), flat(cs[:, :, :]), ACT.Exp, scale=-DECAY)
                    nc.scalar.activation(flat(Gi[:, :, :]), flat(cs[:, :, :]), ACT.Exp, scale=DECAY)
                    nc.scalar.activation(flat(Gp[:, :, :]), flat(Gp[:, :, :]), ACT.Exp, scale=-DECAY).then_inc(gexp, 1)

            def rwkv_turn(i, more):
                def wait(s, per, j):
                    act.wait_ge(s, j + i * per)
                wait(tok_done, 3, 1)
                nc.scalar.activation(rtok[:, :, :, :].rearrange("p i j d -> p (i j d)"), ps[:, 4, :], ACT.Copy).then_inc(tok_ready, 1)
                for n, dst in enumerate((btok, ktok)):
                    wait(tok_done, 3, n + 2)
                    for c in range(2):
                        rows = slice(c * CHUNK, (c + 1) * CHUNK)
                        ins = nc.scalar.activation(dst[rows, c, :, :, :].rearrange("p i j d -> p (i j d)"), ps[rows, 5 + n, :],
                                                   ACT.Copy)
                    ins.then_inc(tok_ready, 1)
                wait(turn_done, 1, 1)
                wait(sig_ready, 3, 3)
                nc.scalar.activation(flat(gate_now[:, :, :]), flat(gg[:, :, :]), ACT.Copy)
                for f, m4 in enumerate(HALVES):
                    wait(x1_done, 2, f + 1)
                    nc.scalar.activation(flat(Xm[:, m4, :]), ps[:, f, :], ACT.Copy).then_inc(x1_ready, 1)
                for v in range(1, len(LEVELS)):
                    for f, m4 in enumerate(HALVES):
                        wait(w1_done, 10, 2 * v - 1 + f)
                        nc.scalar.activation(flat(W1[:, m4, :]), ps[:, f, :], ACT.Copy).then_inc(w1_ready, 1)
                for c in range(TT * 2):
                    wait(rhs_done, 4, c + 1)
                    nc.scalar.activation(rhs[:, :], ps[:, 0, 0:RHEADS * RHEAD], ACT.Copy).then_inc(rhs_ready, 1)
                    wait(u_done, 4, c + 1)
                    if c == 2:
                        wait(ysum_done, 2, 3)
                    rows = slice(c % 2 * CHUNK, (c % 2 + 1) * CHUNK)
                    nc.scalar.activation(uf[rows, :], ps[rows, 1, 0:RHEADS * RHEAD], ACT.Copy).then_inc(u_ready, 1)
                    if more:
                        rwkv_early(i, 1, c)
                wait(ysum_done, 2, 4)
                nc.scalar.activation(flat(yb[:, :, :]), ps[:, 6, :], ACT.Copy).then_inc(yb_ready, 1)
                wait(yc_ready, 1, 1)
                nc.scalar.activation(flat(ysq[:, :, :]), flat(yb[:, :, :]), ACT.Square).then_inc(ysq_ready, 1)
                wait(var_done, 1, 1)
                nc.scalar.activation(flat(spread[:, :, :]), ps[:, 7, :], ACT.Sqrt, bias=gn_eps).then_inc(gstd_ready, 1)
                wait(yc_out, 1, 1)
                nc.scalar.activation(flat(yH[:, bass.ds(2 * 4 + i * RJ, RJ), :]), flat(yb[:, :, :]), ACT.Copy).then_inc(ycH_ready, 1)

            between(3, "w_in2", ("down_1", square_of(3)))
            inputs_high(XB)
            layer("w_in2", copy_to(proj2), 2)
            last_group("w_in2", copy_to(proj2))
            act.wait_ge(evacuated, emptied("w_in2"))
            act.wait_ge(c2_in, 32)
            u, e = cum[:, 0, :], cum[:, 1, :]
            chain(nc.scalar.activation(u, proj2[0:4, SPEC + 3, :], ACT.Identity, bias=b_forget))
            chain(nc.scalar.activation(e, u, ACT.Abs))
            chain(nc.scalar.activation(e, e, ACT.Exp, scale=-1.0))
            nc.scalar.activation(e, e, ACT.Ln, bias=ones[0:4, 0:1]).then_inc(f_log, 1)
            for n in range(4):
                act.wait_ge(v2T_done, n + 1)
                nc.scalar.activation(vtok2[:, 2 * n:2 * n + 2, :, :].rearrange("p a t d -> p (a t d)"), ps[:, 4 + n % 2, :],
                                     ACT.Copy).then_inc(v2_ready, 1)
            act.wait_ge(s2_masked, 1)
            for so, pr in ((soft0, prob0), (soft1, prob1)):
                z, so_ = flat(pr[:, 0, :, :]), flat(so[:, :, :])
                chain(nc.scalar.activation(so_, z, ACT.Abs, scale=SCALE))
                chain(nc.scalar.activation(so_, so_, ACT.Exp, scale=-1.0))
                chain(nc.scalar.activation(so_, so_, ACT.Ln, bias=ones[:, 0:1]))
                nc.scalar.activation(flat(pr[:, 1, :, :]), z, ACT.Relu, scale=SCALE).then_inc(s2_soft, 1)
            act.wait_ge(s2_masked, 2)
            for t in range(TT):
                for h in range(4):
                    p = (forget0, forget1)[t][:, h, :]
                    ins = nc.scalar.activation(p, p, ACT.Exp, bias=nmx[:, 0, t, h:h + 1], scale=SCALE,
                                               accum_out=rsum[:, 0, t, h:h + 1])
            ins.then_inc(s2_exp, 1)
            act.wait_ge(s2_sub, 1)
            nc.scalar.activation(flat(prob0[:, 0, :, :]), flat(prob0[:, 0, :, :]), ACT.Exp)
            nc.scalar.activation(flat(prob1[:, 0, :, :]), flat(prob1[:, 0, :, :]), ACT.Exp).then_inc(s2_exp, 1)

            def take_t2(b):
                act.wait_ge(t2_done, 2 * b + 1)
                if b:
                    act.wait_ge(o2_done, b)
                nc.scalar.activation(flat(qT0[:, :, :]), bank2(4), ACT.Copy).then_inc(t2_ready, 1)
                act.wait_ge(t2_done, 2 * b + 2)
                nc.scalar.activation(flat(qT1[:, :, :]), ps[:, 1, :], ACT.Copy).then_inc(t2_ready, 1)
                act.wait_ge(o2_done, b + 1)
                nc.scalar.activation(flat(yH[:, 4 * b:4 * b + 4, :]), bank2(6), ACT.Copy).then_inc(y2H_ready, 1)

            take_t2(0)
            take_t2(1)
            act.wait_ge(spec_mixed, 1)
            nc.scalar.activation(proj2[0:64, SPEC, :], proj2[0:64, SPEC, :], ACT.Tanh)
            nc.scalar.activation(proj2[:, SPEC + 1, :], proj2[:, SPEC + 1, :], ACT.Sigmoid)
            nc.scalar.activation(proj2[96:P, SPEC + 2, :], proj2[96:P, SPEC + 2, :], ACT.Sigmoid).then_inc(spec_ready, 1)
            act.wait_ge(zeroed, 1)
            for part in range(4):
                rwkv_early(0, 0, part)
            with act.Fori(0, RTURNS - 1) as i:
                rwkv_turn(i, True)
            rwkv_turn(RTURNS - 1, False)
            act.wait_ge(turn_done, RTURNS + 1)
            layer("gates2", copy_to(gates, ACT.Sigmoid))
            last_group("gates2", copy_to(gates, ACT.Sigmoid))

            def mix_high(name, i, r):
                act.wait_ge(mix_ready, 1 + r + i * 2)
                nc.scalar.activation(flat(actH[:, bass.ds(GT * r + i * (2 * GT), GT), :]), mix[:, :], ACT.Copy
                                     ).then_inc(mixH_ready, 1)

            layer("branch", mix_high)
            last_group("branch", mix_high)
            layer("w_out2", copy_square(NB + 1))
            between(NB + 1, "up2_0", ("w_out2", copy_square(NB + 1)))
            inputs_high(XB + 1)
            layer("up2_0", square_relu, 2)
            layer("down2_0", copy_to(o), before=("up2_0", square_relu))
            layer("up2_1", square_relu, before=("down2_0", copy_to(o)))
            layer("down2_1", square_of(NB + 3), when=4, before=("up2_1", square_relu))
            last_group("down2_1", square_of(NB + 3))
            root(NB + 3)

        @block.vector
        def _(dve):
            link = Chain(dve, dve_chain)
            dve.sem_inc(wl_ready, RAW)
            dve.sem_inc(hidL_ready, 1)
            dve.sem_inc(ada_sum, STEP_K * RAW)
            dve.sem_inc(ada_rows, 2)

            def split(name, i, r, s):
                slot, _ = raw_loads(name, i, r, s)
                l = lin(name, i, r, s)
                b = s % SPLIT if L[name]["spg"] > 1 else r % SPLIT
                dve.wait_ge(wh_ready, l + 1)
                dve.wait_ge(step_done, l + 1)
                nc.vector.tensor_tensor(wL[:, b, :, :], raw[:, slot, :, :], wH[:, b, :, :].bitcast(F32),
                                        ALU.subtract).then_inc(wl_ready, 1)

            def last_group(name, evac):
                n, U = L[name]["groups"], L.unroll(name)
                i = (n - 2) // U
                evac(name, i, n - 1 - i * U)

            def layer(name, evac=None, done=0, beside=None, before=None):
                spg = L[name]["spg"]

                def body(i, r):
                    peeled = isinstance(i, int) and i == 0 and r == 0
                    for s in range(spg):
                        if not (peeled and s < done):
                            split(name, i, r, s)
                        if beside and not peeled:
                            beside(i, r, s)
                        if before and peeled and s == min(2, spg - 1):
                            last_group(*before)
                        if evac and s == min(2, spg - 1) and not peeled:
                            evac(name, i, r - 1)

                over_groups(dve, name, 1, body)

            def add_to(dst):
                def evac(name, i, r):
                    dve.wait_ge(step_done, SPLIT + lin(name, i, r, L[name]["spg"] - 1) + 1)
                    d = flat(dst[:, bass.ds(GT * r + i * (GT * L.unroll(name)), GT), :])
                    nc.vector.tensor_tensor(d, bank2(acc(name, r)), d, ALU.add).then_inc(evacuated, 1)
                return evac

            def hidden_low(name, i, r):
                dve.wait_ge(hidH_ready, grp(name, i, r) - up_groups_before[name] + 1)
                at_ = bass.ds(GT * r + i * (GT * L.unroll(name)), GT)
                nc.vector.tensor_tensor(flat(hidL[:, at_, :]), hid[:, :], flat(hidH[:, at_, :]).bitcast(F32),
                                        ALU.subtract).then_inc(hidL_ready, 1)

            def rstd(n):
                dve.wait_ge(std_ready, n + 1)
                link(nc.vector.reciprocal(std[:, :], std[:, :]))

            def tiles(c):
                return range(GT * c, GT * (c + 1))

            def residual(n, coefficient, update):
                rstd(n)
                if n == NB + 1:
                    dve.wait_ge(x_back, 16)
                for c in range(KT // GT + 1):
                    if c < KT // GT:
                        for k in tiles(c):
                            ins = nc.vector.scalar_tensor_tensor(o[:, k, :], o[:, k, :], coef[:, coefficient, k:k + 1], std[:, :],
                                                                 ALU.mult, ALU.mult)
                        ins.then_inc(o_scaled, 1)
                    if c:
                        dve.wait_ge(o_scaled, 4 * update + c)
                        part = slice(GT * (c - 1), GT * c)
                        nc.vector.tensor_tensor(flat(x[:, part, :]), flat(x[:, part, :]), flat(o[:, part, :]), ALU.add
                                                ).then_inc(x_ready, 1)

            def inputs_low(n, m, coefficient, shift=None):
                rstd(n)
                for c in range(KT // GT + 1):
                    if c < KT // GT:
                        for k in tiles(c):
                            ins = nc.vector.scalar_tensor_tensor(sq[:, k, :], x[:, k, :], coef[:, coefficient, k:k + 1], std[:, :],
                                                                 ALU.mult, ALU.mult)
                        ins.then_inc(y_ready, 1)
                    if c:
                        dve.wait_ge(h_ready, 4 * m + c)
                        if shift is None:
                            part = slice(GT * (c - 1), GT * c)
                            ins = nc.vector.tensor_tensor(flat(actL[:, part, :]), flat(sq[:, part, :]),
                                                          flat(actH[:, part, :]).bitcast(F32), ALU.subtract)
                        else:
                            for k in tiles(c - 1):
                                ins = nc.vector.scalar_tensor_tensor(actL[:, k, :], sq[:, k, :], mod[:, shift, k:k + 1],
                                                                     actH[:, k, :].bitcast(F32), ALU.add, ALU.subtract)
                        ins.then_inc(act_ready, 1)

            def first_splits(name):
                for s in range(2):
                    split(name, 0, 0, s)

            def ada_step(g, s_, w, sums, i=0, per=0):
                for k in range(STEP_K):
                    n = s_ * STEP_K + k
                    if n < 2:
                        ins = nc.vector.tensor_scalar(sums[:, n % 2, :], w[:, k, :], csig[:, n:n + 1], None, ALU.mult)
                    else:
                        dve.wait_ge(ada_sum, STEP_K * RAW + 4 * STEP_K * g + n - 1 + i * (4 * STEP_K * per))
                        ins = nc.vector.scalar_tensor_tensor(sums[:, n % 2, :], w[:, k, :], csig[:, n:n + 1], sums[:, n % 2, :],
                                                             ALU.mult, ALU.add)
                    ins.then_inc(ada_sum, 1)

            def ada(g, i=0, per=0):
                dve.wait_ge(ada_rows, g + 1 + i * per)
                for s_ in range(4):
                    dve.wait_ge(raw_in[s_], ada_raw(g) + i * (16 * per))
                    ada_step(g, s_, raw[:, s_, :, :], ada_acc[:, g % 2, :, :], i, per)

            def beside_w_in(i, r, s):
                s_ = 4 * (r - 1) + s - 2
                if not 0 <= s_ < 4:
                    return
                g = L["ada_a"]["groups"]
                if s_ == 0:
                    dve.wait_ge(ada_rows, 2 + g + i)
                dve.wait_ge(side_in[s_], 16 + i * 16)
                ada_step(g, s_, side[:, s_, :, :], side_acc, i, 1)

            def ada_raw(g):
                n, m = L["ada_a"]["groups"], L["ada_a"]["groups"] + SIDE
                return 16 * (L["ada_a"]["t0"] // RAW + 1 + g) if g < n else 16 * (L["ada_b"]["t0"] // RAW + 1 + g - m)

            dve.wait_ge(csig_ready, 1)
            link(nc.vector.tensor_tensor(csig[:, :], csig[:, :], cvec[:, :], ALU.mult))
            with dve.Fori(0, L["ada_a"]["groups"] // 2) as i:
                for r in range(2):
                    ada(r, i, 2)
            dve.wait_ge(ada_rows, 2 + L["ada_a"]["groups"])
            psm = ps[:, 0, 0:6 * KT].rearrange("p (j k) -> p j k", k=KT)
            ins = nc.vector.tensor_tensor(mod[:, 0:2, :], psm[:, 0:2, :], b_ada[:, 0:2, :], ALU.add)
            link(ins)
            dve.sem_inc(mod_ready, 1)
            link(nc.vector.scalar_tensor_tensor(coef[:, 0, :], mod[:, 1, :], 1.0, vecs[:, 0, :], ALU.add, ALU.mult))
            inputs_low(0, 0, 0, 0)
            first_splits("w_in")
            dve.wait_ge(gw_hi, 1)
            nc.vector.tensor_tensor(gwL[:, :, :], gw[:, :, :], gwH[:, :, :].bitcast(F32), ALU.subtract
                                    ).then_inc(gw_lo, 1)
            layer("w_in", None, 2, beside_w_in)
            ada_next = [L["ada_a"]["groups"] + SIDE]
            c0, c1_ = L["ada_a"]["groups"] * GT, (L["ada_a"]["groups"] + SIDE) * GT
            dve.wait_ge(ada_rows, 2 + L["ada_a"]["groups"] + SIDE)
            nc.vector.tensor_tensor(flat(mod[:, :, :])[:, c0:c1_], ps[:, 6, c0:c1_], flat(b_ada[:, :, :])[:, c0:c1_], ALU.add)

            def ada_groups(n):
                for _ in range(n):
                    ada(ada_next[0])
                    ada_next[0] += 1

            dve.wait_ge(evacuated, emptied("w_in"))
            ada_groups(ADA_BEFORE[0])
            for n, p in enumerate(rope_pairs):
                dve.wait_ge(rotated, n + 1)
                link(nc.vector.tensor_tensor(rope_s[:, n % 2, :, :], ps[:, 2 + n % 2, :].rearrange("p (a t) -> p a t", a=2),
                                             sin.unsqueeze(1).to_broadcast([P, 2, T]), ALU.mult))
                dve.wait_ge(rope_cos, n + 1)
                nc.vector.tensor_tensor(proj[:, p:p + 2, :], rope_s[:, n % 2, :, :], rope_c[:, n % 2, :, :],
                                        ALU.add).then_inc(roped, 1)
            dve.wait_ge(cmp_in, 80)
            half_ = CMP_STRIDE
            for n, p in enumerate((KC, VC)):
                for g in range(GROUPS):
                    for h in range(CMP_LEN // CMP_STRIDE):
                        rows = proj[:, p + g, h * half_:(h + NCMP) * half_].rearrange("p (b r) -> p r b", r=half_)
                        ins = nc.vector.tensor_tensor(xc[:, n, h * half_:(h + 1) * half_, g * NCMP:(g + 1) * NCMP], rows,
                                                      posk[:, n, h * half_:(h + 1) * half_].unsqueeze(2).to_broadcast(
                                                          [P, half_, NCMP]), ALU.add)
            ins.then_inc(xc_ready, 1)
            ada_groups(ADA_BEFORE[1])
            dve.wait_ge(cmp_sig, 1)
            nc.vector.tensor_tensor(flat(chtok[:, :, :]), ps[0:GROUPS * NCMP, 6, 0:2 * P], flat(chtok[:, :, :]), ALU.mult
                                    ).then_inc(cmp_hid, 1)

            def mask_max(b):
                dve.wait_ge(scores, b + 1)
                if b >= 2:
                    dve.wait_ge(pT_done, 2 * (b - 1))
                if subs[b][0] == "cmp":
                    s = ps[:, 1, 0:TT * 4 * NCMP].rearrange("p (t h n) -> p t h n", t=TT, h=4)
                    for t in range(TT):
                        ins = nc.vector.tensor_tensor(pcmp[:, t, :, :], s[:, t, :, :],
                                                      unseen[:, t, :].unsqueeze(1).to_broadcast([P, 4, NCMP]), ALU.add)
                    link(ins)
                    for t in range(TT):
                        ins = nc.vector.tensor_reduce(nmx[:, b % 2, t, :], pcmp[:, t, :, :], AX.X, ALU.max)
                else:
                    nc.vector.tensor_tensor(probs0[:, b % 2, :, :], ps[:, 1, :].rearrange("p (h n) -> p h n", h=4),
                                            causal[:, P:2 * P].unsqueeze(1).to_broadcast([P, 4, P]), ALU.add)
                    link(nc.vector.tensor_tensor(probs1[:, b % 2, :, :], bank2(2).rearrange("p (h n) -> p h n", h=4),
                                                 causal.unsqueeze(1).to_broadcast([P, 4, T]), ALU.add))
                    nc.vector.tensor_reduce(nmx[:, b % 2, 0, :], probs0[:, b % 2, :, :], AX.X, ALU.max)
                    ins = nc.vector.tensor_reduce(nmx[:, b % 2, 1, :], probs1[:, b % 2, :, :], AX.X, ALU.max)
                link(ins)
                nc.vector.tensor_scalar(nmx[:, b % 2, :, :], nmx[:, b % 2, :, :], -SCALE, None, ALU.mult
                                        ).then_inc(masked, 1)

            def weights_of(b):
                kind, q, _, _, gk, _, _ = subs[b]
                dve.wait_ge(exped, b + 1)
                if kind == "cmp":
                    for t in range(TT):
                        ins = nc.vector.tensor_tensor(pcmp[:, t, :, :], pcmp[:, t, :, :],
                                                      seen[:, t, :].unsqueeze(1).to_broadcast([P, 4, NCMP]), ALU.mult)
                    link(ins)
                    for t in range(TT):
                        ins = nc.vector.tensor_reduce(rsum[:, b % 2, t, :], pcmp[:, t, :, :], AX.X, ALU.add)
                    link(ins)
                r = rsum[:, b % 2, :, :]
                link(nc.vector.tensor_scalar(r, r, 1e-30, None, ALU.max))
                ins = nc.vector.reciprocal(r, r)
                if gk is not None:
                    link(ins)
                    gt = gate[:, :, :].rearrange("p t (h c) -> p t h c", c=3)[:, :, q:q + 4, gk]
                    ins = nc.vector.tensor_tensor(r, r, gt, ALU.mult)
                ins.then_inc(weight, 1)

            dve.wait_ge(gate_ready, 1)
            mask_max(0)
            for b in range(NSUB):
                if b + 1 < NSUB:
                    mask_max(b + 1)
                weights_of(b)
                ada_groups(ADA_BESIDE[b])
                if subs[b][6]:
                    g = out_of[b]
                    dve.wait_ge(oH_ready, g + 1)
                    nc.vector.tensor_tensor(flat(actL[:, 4 * g:4 * g + 4, :]), bank2(6),
                                            flat(actH[:, 4 * g:4 * g + 4, :]).bitcast(F32), ALU.subtract
                                            ).then_inc(oL_ready, 1)
            dve.wait_ge(ada_rows, 2 + 6 * KT // GT)
            link(nc.vector.tensor_tensor(flat(mod[:, :, :])[:, c1_:], ps[:, 0, c1_:6 * KT], flat(b_ada[:, :, :])[:, c1_:], ALU.add))
            dve.sem_inc(mod_ready, 1)
            nc.vector.tensor_tensor(coef[:, 1, :], mod[:, 2, :], vecs[:, 1, :], ALU.mult)
            nc.vector.scalar_tensor_tensor(coef[:, 2, :], mod[:, 4, :], 1.0, vecs[:, 2, :], ALU.add, ALU.mult)
            link(nc.vector.tensor_tensor(coef[:, 3, :], mod[:, 5, :], vecs[:, 3, :], ALU.mult))
            layer("w_o")
            first_splits("up_0")
            residual(1, 1, 0)
            inputs_low(2, 1, 2, 3)
            layer("up_0", hidden_low, 2)
            layer("down_0", before=("up_0", hidden_low))
            layer("up_1", hidden_low)
            layer("down_1", add_to(o), before=("up_1", hidden_low))
            last_group("down_1", add_to(o))
            first_splits("w_in2")
            residual(3, 3, 1)

            def rwkv_early(i, ahead, part):
                def wait(s, per, j):
                    dve.wait_ge(s, j + ahead * per + i * per)

                def turn(base):
                    return base + ahead * RJ + i * RJ
                if part == 0:
                    link(nc.vector.tensor_copy(rv[:, 0:LN_W, :], rwv10[:, 0:LN_W, bass.ds(turn(0), RJ)]))
                    wait(shifted_z, 1, 1)
                if part < 3:
                    dst, d, m, base = ((rk, d1, MU_K, RK), (rr, d0, MU_R, RR), (rvv, d2, MU_V, RV))[part]
                    for j in range(RJ):
                        ins = nc.vector.scalar_tensor_tensor(dst[:, j, :], d[:, j, :], rv[:, m, j:j + 1],
                                                             proj2[:, bass.ds(turn(base + j), 1), :].rearrange("p a t -> p (a t)"),
                                                             ALU.mult, ALU.add)
                if part == 2:
                    link(ins)
                    dve.sem_inc(mixed, 1)
                    for j in range(RJ):
                        ins = nc.vector.tensor_scalar(kk[:, j, :], rk[:, j, :], rv[:, K_K, j:j + 1], None, ALU.mult)
                    link(ins)
                    dve.sem_inc(kk_ready, 1)
                if part == 3:
                    wait(sig_ready, 3, 1)
                    for j in range(RJ):
                        ins = nc.vector.tensor_tensor_scan(cs[:, j, :], reset, sg[:, j, :], 0.0, ALU.mult, ALU.add)
                    link(ins)
                    link(nc.vector.tensor_tensor(flat(Gp[:, :, :]), flat(cs[:, :, :]), flat(sg[:, :, :]), ALU.subtract))
                    dve.sem_inc(cs_ready, 1)
                if part == 4:
                    wait(sig_ready, 3, 2)
                    for j in range(RJ):
                        ins = nc.vector.tensor_scalar(k2[:, j, :], aa[:, j, :], 1.0, rv[:, K_A, j:j + 1], ALU.subtract, ALU.mult)
                    link(ins)
                    link(nc.vector.scalar_tensor_tensor(flat(k2[:, :, :]), flat(k2[:, :, :]), 1.0, flat(rk[:, :, :]), ALU.add, ALU.mult))
                    dve.sem_inc(k2_ready, 1)
                if part == 5:
                    wait(nrm_ready, 1, 1)
                    link(nc.vector.tensor_scalar(flat(nrm[:, :, :]), flat(nrm[:, :, :]), 1e-12, None, ALU.max))
                    link(nc.vector.reciprocal(flat(nrm[:, :, :]), flat(nrm[:, :, :])))
                    link(nc.vector.tensor_tensor(flat(kk[:, :, :]), flat(kk[:, :, :]), flat(nrm[:, :, :]), ALU.mult))
                    dve.sem_inc(kkn_ready, 1)
                    for j in range(RJ):
                        ins = nc.vector.scalar_tensor_tensor(rkk[:, j, :], rr[:, j, :], rv[:, R_K, j:j + 1], k2[:, j, :],
                                                             ALU.mult, ALU.mult)
                    link(ins)
                    dve.sem_inc(rk_scaled, 1)
                    wait(gexp, 1, 1)
                    link(nc.vector.tensor_tensor(flat(KTt[:, :, :]), flat(k2[:, :, :]), flat(Gi[:, :, :]), ALU.mult))
                    wait(ysum_done, 2, 2)
                    for h, part_ in enumerate((slice(0, RHEAD), slice(RHEAD, P))):
                        ins = nc.vector.scalar_tensor_tensor(AR[h][part_, :, :, 0, :].rearrange("p j i t -> p (j i) t"),
                                                             kk[part_, :, :].rearrange("p j (i t) -> p (j i) t", i=TT), -1.0,
                                                             Gp[part_, :, :].rearrange("p j (i t) -> p (j i) t", i=TT),
                                                             ALU.mult, ALU.mult)
                    link(ins)
                    dve.sem_inc(a_ready, 1)

            def rwkv_turn(i, more):
                def wait(s, per, j):
                    dve.wait_ge(s, j + i * per)
                link(nc.vector.tensor_copy(rv[:, LN_W:, :], rwv10[:, LN_W:, bass.ds(i * RJ, RJ)]))
                link(nc.vector.memset(flat(ST[:, :, :]), 0.0))
                wait(gexp, 1, 1)
                link(nc.vector.tensor_copy(Gend[:, :, :], Gd[:, :, CHUNK - 1::CHUNK]))
                wait(bonus_sum, 1, 1)
                link(nc.vector.scalar_tensor_tensor(flat(bonus[:, :, :]), ps[:, 7, :], float(RHEAD), flat(rvv[:, :, :]),
                                                    ALU.mult, ALU.mult))
                dve.sem_inc(bonus_ready, 1)

                def masks(n, dst):
                    for h in range(RHEADS):
                        wait(mat_done, 8, 4 * n + h + 1)
                        nc.vector.tensor_tensor(dst[:, 2 * h:2 * h + 2, :], ps[:, 4 * n + h, :].rearrange("p (i c) -> p i c", i=TT),
                                                token_mask.unsqueeze(1).to_broadcast([P, TT, 2 * P]), ALU.mult).then_inc(mat_masked, 1)

                masks(0, Bc)
                wait(mat_masked, 8, 4)
                lab = Bc[:, :, 0:P]
                link(nc.vector.tensor_tensor(Ym[:, :, :], lab, level_mask[:, 0, :].unsqueeze(1).to_broadcast([P, MATS, P]), ALU.mult))
                link(nc.vector.tensor_tensor(Ym[:, :, :], Ym[:, :, :], ident.unsqueeze(1).to_broadcast([P, MATS, P]), ALU.add))
                dve.sem_inc(y1_ready, 1)
                masks(1, Kc)
                for v in range(1, len(LEVELS)):
                    for f, m4 in enumerate(HALVES):
                        wait(dx_done, 10, 2 * v - 1 + f)
                        if v < len(LEVELS) - 1:
                            nc.vector.tensor_tensor(flat(Xm[:, m4, :]), flat(Xm[:, m4, :]), ps[:, 2 + f, :], ALU.add)
                        nc.vector.tensor_tensor(flat(Ym[:, m4, :]), flat(Ym[:, m4, :]), ps[:, 4 + f, :], ALU.add
                                                ).then_inc(level_ready, 1)
                    if more and 2 <= v <= 4:
                        rwkv_early(i, 1, v - 2)
                for c in range(TT * 2):
                    wait(s_done, 4, c + 1)
                    link(nc.vector.tensor_tensor(flat(ST[:, :, :]), flat(ST[:, :, :]), ps[:, 2, 0:RJ * P], ALU.add))
                    link(nc.vector.tensor_tensor(ST[:, :, :], ST[:, :, :], Gend[:, :, c:c + 1].to_broadcast([P, RJ, P]), ALU.mult))
                    dve.sem_inc(st_ready, 1)
                    if more and c:
                        rwkv_early(i, 1, 2 + c)
                wait(mean_done, 1, 1)
                link(nc.vector.tensor_tensor(flat(yb[:, :, :]), flat(yb[:, :, :]), ps[:, 7, :], ALU.subtract))
                dve.sem_inc(yc_ready, 1)
                wait(gstd_ready, 1, 2)
                link(nc.vector.reciprocal(flat(spread[:, :, :]), flat(spread[:, :, :])))
                link(nc.vector.tensor_tensor(flat(yb[:, :, :]), flat(yb[:, :, :]), flat(spread[:, :, :]), ALU.mult))
                for j in range(RJ):
                    ins = nc.vector.tensor_scalar(yb[:, j, :], yb[:, j, :], rv[:, LN_W, j:j + 1], rv[:, LN_B, j:j + 1],
                                                  ALU.mult, ALU.add)
                link(ins)
                link(nc.vector.tensor_tensor(flat(yb[:, :, :]), flat(yb[:, :, :]), flat(bonus[:, :, :]), ALU.add))
                link(nc.vector.tensor_tensor(flat(yb[:, :, :]), flat(yb[:, :, :]), flat(gate_now[:, :, :]), ALU.mult))
                dve.sem_inc(yc_out, 1)
                wait(ycH_ready, 1, 1)
                at_ = bass.ds(2 * 4 + i * RJ, RJ)
                link(nc.vector.tensor_tensor(flat(yL[:, at_, :]), flat(yb[:, :, :]), flat(yH[:, at_, :]).bitcast(F32), ALU.subtract))
                dve.sem_inc(turn_done, 1)

            link(nc.vector.tensor_copy(coef[:, 4:8, :], vecs[:, 4:8, :]))
            inputs_low(NB, XB, 4)
            layer("w_in2", None, 2)
            u, e, up, dn = (cum[:, n, :] for n in range(4))
            dve.wait_ge(f_log, 1)
            link(nc.vector.tensor_scalar(u, u, -1.0, 0.0, ALU.mult, ALU.max))
            link(nc.vector.tensor_tensor(e, e, u, ALU.add))
            link(nc.vector.tensor_tensor_scan(u, ones[0:4, 0:1].to_broadcast([4, T]), e, 0.0, ALU.mult, ALU.add))
            nc.vector.tensor_scalar(up, u, 1.0 / SCALE, None, ALU.mult)
            link(nc.vector.tensor_scalar(dn, u, -1.0 / SCALE, None, ALU.mult))
            dve.sem_inc(cum_ready, 1)

            def masked2(b, mask, first, second):
                dve.wait_ge(s2_done, b + 1)
                nc.vector.tensor_tensor(first, ps[:, 1, :].rearrange("p (h n) -> p h n", h=4),
                                        mask[:, P:2 * P].unsqueeze(1).to_broadcast([P, 4, P]), ALU.add)
                link(nc.vector.tensor_tensor(second, bank2(2).rearrange("p (h n) -> p h n", h=4),
                                             mask.unsqueeze(1).to_broadcast([P, 4, T]), ALU.add))

            masked2(0, strict, prob0[:, 0, :, :], prob1[:, 0, :, :])
            dve.sem_inc(s2_masked, 1)
            masked2(1, causal, forget0[:, :, :], forget1[:, :, :])
            nc.vector.tensor_reduce(nmx[:, 0, 0, :], forget0[:, :, :], AX.X, ALU.max)
            link(nc.vector.tensor_reduce(nmx[:, 0, 1, :], forget1[:, :, :], AX.X, ALU.max))
            link(nc.vector.tensor_scalar(nmx[:, 0, :, :], nmx[:, 0, :, :], -SCALE, None, ALU.mult))
            dve.sem_inc(s2_masked, 1)
            for n, (so, pr, w) in enumerate(((soft0, prob0, P), (soft1, prob1, T))):
                dve.wait_ge(s2_soft, n + 1)
                link(nc.vector.tensor_tensor(flat(pr[:, 1, :, :]), flat(pr[:, 1, :, :]), flat(so[:, :, :]), ALU.add))
                for h in range(4):
                    ins = nc.vector.tensor_tensor_scan(so[:, h, ::-1], ones[:, 0:1].to_broadcast([P, w]), pr[:, 1, h, ::-1], 0.0,
                                                       ALU.mult, ALU.add)
                link(ins)
                link(nc.vector.scalar_tensor_tensor(flat(pr[:, 0, :, :]), flat(pr[:, 0, :, :]), SCALE, flat(so[:, :, :]),
                                                    ALU.mult, ALU.subtract))
            dve.sem_inc(s2_sub, 1)

            def y_low(b):
                dve.wait_ge(y2H_ready, b + 1)
                nc.vector.tensor_tensor(flat(yL[:, 4 * b:4 * b + 4, :]), bank2(6), flat(yH[:, 4 * b:4 * b + 4, :]).bitcast(F32),
                                        ALU.subtract).then_inc(y2L_ready, 1)

            dve.wait_ge(s2_exp, 1)
            link(nc.vector.reciprocal(rsum[:, 0, :, :], rsum[:, 0, :, :]))
            dve.sem_inc(s2_weight, 1)
            y_low(0)
            y_low(1)
            dve.wait_ge(y2L_ready, 2)
            z = proj2[:, SPEC:SPEC + 3, :]
            d = at_spec[:, :, :]
            nc.vector.tensor_tensor(d[:, :, 1:T], z[:, :, 0:T - 1], z[:, :, 1:T], ALU.subtract)
            link(nc.vector.tensor_scalar(d[:, :, 0:1], z[:, :, 0:1], -1.0, None, ALU.mult))
            for j in range(3):
                ins = nc.vector.scalar_tensor_tensor(z[:, j, :], d[:, j, :], mu_spec[:, j:j + 1], z[:, j, :], ALU.mult, ALU.add)
            link(ins)
            dve.sem_inc(spec_mixed, 1)
            dve.wait_ge(x_out, 16)
            for t_ in (AR[0], AR[1], btok, ktok):
                ins = nc.vector.memset(t_[:, :, :, :, :], 0.0)
            link(nc.vector.memset(uf[:, :], 0.0))
            dve.sem_inc(zeroed, 1)
            dve.sem_inc(turn_done, 1)
            for part in range(6):
                rwkv_early(0, 0, part)
            n0, K = link.n, RWKV_LINKS
            with dve.Fori(0, RTURNS - 1) as i:
                link.off = i * K
                rwkv_turn(i, True)
            assert link.n - n0 == K, link.n - n0
            link.n, link.off = n0 + (RTURNS - 1) * K, 0
            rwkv_turn(RTURNS - 1, False)
            dve.wait_ge(turn_done, RTURNS + 1)
            layer("gates2")

            def gated(n, name, i, r):
                dve.wait_ge(step_done, SPLIT + lin(name, i, r, (0, 1, 3)[n]) + 1)
                g = flat(gates[:, bass.ds(16 * n + GT * r + i * (2 * GT), GT), :])
                if n == 0:
                    nc.vector.tensor_tensor(mix[:, :], bank2(0), g, ALU.mult).then_inc(branch_used, 1)
                    return
                nc.vector.tensor_tensor(mix_t[:, :], bank2(2 * n), g, ALU.mult).then_inc(branch_used, 1)
                dve.wait_ge(branch_used, 3 * r + n + 1 + i * 6)
                ins = nc.vector.tensor_tensor(mix[:, :], mix[:, :], mix_t[:, :], ALU.add)
                if n == 1:
                    ins.then_inc(mixL_ready, 1)
                    dve.wait_ge(mixL_ready, 2 * r + 1 + i * 4)
                    return
                ins.then_inc(mix_ready, 1)
                dve.wait_ge(mixH_ready, r + 1 + i * 2)
                at_ = bass.ds(GT * r + i * (2 * GT), GT)
                nc.vector.tensor_tensor(flat(actL[:, at_, :]), mix[:, :], flat(actH[:, at_, :]).bitcast(F32), ALU.subtract
                                        ).then_inc(mixL_ready, 1)
                dve.wait_ge(mixL_ready, 2 * r + 2 + i * 4)
                dve.sem_inc(evacuated, 1)

            dve.wait_ge(evacuated, emptied("gates2"))

            def branch(i, r):
                split("branch", i, r, 0)
                split("branch", i, r, 1)
                if not (isinstance(i, int) and i == 0 and r == 0):
                    gated(2, "branch", i, r - 1)
                split("branch", i, r, 2)
                gated(0, "branch", i, r)
                split("branch", i, r, 3)
                gated(1, "branch", i, r)

            over_groups(dve, "branch", 1, branch)
            gated(2, "branch", 1, 1)
            layer("w_out2")
            first_splits("up2_0")
            residual(NB + 1, 5, XB)
            inputs_low(NB + 2, XB + 1, 6)
            layer("up2_0", hidden_low, 2)
            layer("down2_0", before=("up2_0", hidden_low))
            layer("up2_1", hidden_low)
            layer("down2_1", add_to(o), before=("up2_1", hidden_low))
            last_group("down2_1", add_to(o))
            residual(NB + 3, 7, XB + 1)

        @block.gpsimd
        def _(pool):
            pool.wait_ge(c1_in, 16)
            pool.wait_ge(evacuated, emptied("w_in"))
            for n, p in enumerate(rope_pairs):
                if n >= 2:
                    pool.wait_ge(roped, n - 1)
                nc.gpsimd.tensor_tensor(rope_c[:, n % 2, :, :], proj[:, p:p + 2, :],
                                        cos.unsqueeze(1).to_broadcast([P, 2, T]), ALU.mult).then_inc(rope_cos, 1)
            for b in range(NSUB):
                pool.wait_ge(weight, b + 1)
                for t in range(TT):
                    p = pcmp[:, t, :, :] if subs[b][0] == "cmp" else (probs0, probs1)[t][:, b % 2, :, :]
                    ins = nc.gpsimd.tensor_tensor(p, p, rsum[:, b % 2, t, :].unsqueeze(2).to_broadcast(list(p.shape)),
                                                  ALU.mult)
                ins.then_inc(probs_ready, 1)
            pool.wait_ge(s2_weight, 1)
            for t in range(TT):
                p = (forget0, forget1)[t][:, :, :]
                ins = nc.gpsimd.tensor_tensor(p, p, rsum[:, 0, t, :].unsqueeze(2).to_broadcast(list(p.shape)), ALU.mult)
            ins.then_inc(s2_probs, 1)
            pool.wait_ge(zeroed, 1)
            half = [slice(0, RHEAD), slice(RHEAD, P)]
            def rwkv_shift(i, ahead):
                for d, base in ((d0, RR), (d1, RK), (d2, RV)):
                    z = proj2[:, bass.ds(base + ahead * RJ + i * RJ, RJ), :]
                    nc.gpsimd.tensor_tensor(d[:, :, 0:1], causal[:, 0:RJ].unsqueeze(2), z[:, :, 0:1], ALU.subtract)
                    ins = nc.gpsimd.tensor_tensor(d[:, :, 1:T], z[:, :, 0:T - 1], z[:, :, 1:T], ALU.subtract)
                ins.then_inc(shifted_z, 1)

            def rwkv_turn(i, more):
                pool.wait_ge(kkn_ready, 1 + i)
                pool.wait_ge(cs_ready, 1 + i)
                nc.gpsimd.tensor_tensor(flat(ka[:, :, :]), flat(kk[:, :, :]), flat(aa[:, :, :]), ALU.mult).then_inc(pool_chain, 1)
                pool.wait_ge(pool_chain, 1 + i)
                pool.wait_ge(gexp, 1 + i)
                nc.gpsimd.tensor_tensor(flat(BT[:, :, :]), flat(ka[:, :, :]), flat(Gi[:, :, :]), ALU.mult).then_inc(b_ready, 1)
                pool.wait_ge(b_ready, 1 + i)
                pool.wait_ge(ysum_done, 2 + i * 2)
                for h, part in enumerate(half):
                    for j in range(RJ):
                        nc.gpsimd.tensor_tensor(AR[h][part, j, :, 1, :], rr[part, j, :].rearrange("p (i t) -> p i t", i=TT),
                                                Gd[part, j, :].rearrange("p (i t) -> p i t", i=TT), ALU.mult
                                                ).then_inc(r_ready, 1)
                pool.wait_ge(r_ready, 2 * RJ + i * (2 * RJ))
                pool.wait_ge(mat_masked, 4 + i * 8)
                for v in range(1, len(LEVELS)):
                    if v == 3 and more:
                        rwkv_shift(i, 1)
                    if v > 2:
                        pool.wait_ge(w1_done, 2 * (v - 2) + i * 10)
                    nc.gpsimd.tensor_tensor(Lm[:, v % 2, :, :], Bc[:, :, 0:P],
                                            level_mask[:, v, :].unsqueeze(1).to_broadcast([P, MATS, P]), ALU.mult
                                            ).then_inc(lm_ready, 1)

            rwkv_shift(0, 0)
            with pool.Fori(0, RTURNS - 1) as i:
                rwkv_turn(i, True)
            rwkv_turn(RTURNS - 1, False)

        @block.tensor
        def _(pe):
            pe.sem_inc(step_done, SPLIT)
            pe.sem_inc(evacuated, 2)
            pe.sem_inc(lora_done, 1)
            pe.sem_inc(ysum_done, 2)

            def norm_part(n, c, src):
                pe.wait_ge(sq_ready, 4 * n + c + 1)
                for k in range(GT):
                    ins = nc.tensor.matmul(ps[:, 4, 0:T], ones, src[:, k, :], start=(c == 0 and k == 0), stop=(c == 3 and k == GT - 1))
                ins.then_inc(ssum_ready, 1)

            def pre_norm(n):
                for c in range(KT // GT):
                    norm_part(n, c, sq[:, GT * c:GT * (c + 1), :])

            def ada_total(g, i=0, per=0, sums=None, bank=0):
                pe.wait_ge(ada_sum, STEP_K * (RAW + 4 * (g + 1)) + i * (STEP_K * 4 * per))
                if sums is None:
                    sums = ada_acc[:, g % 2, :, :]
                for n in range(GT):
                    for j in range(2):
                        ins = nc.tensor.matmul(ps[:, bank, bass.ds(n + g * GT + i * (GT * per), 1)], sums[:, j, n * P:(n + 1) * P],
                                               ones[:, 0:1], start=(n == 0 and j == 0), stop=(j == 1), skip_group_check=True)
                ins.then_inc(ada_rows, 1)

            def layer(name, xH, xL, arrives=None, then_norm=None):
                spg = L[name]["spg"]
                pe.wait_ge(evacuated, 2 + L[name]["g0"])

                def body(i, r):
                    pe.wait_ge(evacuated, grp(name, i, r) + 1)
                    for s in range(spg):
                        if arrives and isinstance(i, int) and i == 0 and r == 0:
                            pe.wait_ge(arrives[0], arrives[1] + s + 1)
                        pe.wait_ge(wl_ready, RAW + lin(name, i, r, s) + 1)
                        b = s % SPLIT if spg > 1 else r % SPLIT
                        for k in range(STEP_K):
                            kk = s * STEP_K + k
                            for n in range(GT):
                                out = ps[:, acc(name, r) + n // 2, (n % 2) * T:(n % 2 + 1) * T]
                                cols = slice(n * P, (n + 1) * P)
                                for j, (w, v) in enumerate(((wH, xH), (wH, xL), (wL, xH))):
                                    ins = nc.tensor.matmul(out, w[:, b, k, cols], v[:, kk, :],
                                                           start=(kk == 0 and j == 0 and n % 2 == 0),
                                                           stop=(kk == STEP_K * spg - 1 and j == 2), skip_group_check=True)
                        ins.then_inc(step_done, 1)
                        if name == "w_in" and r == 2 and s == 2:
                            ada_total(L["ada_a"]["groups"], i, 1, side_acc, 6)
                    if then_norm is not None and r + i * L.unroll(name) > 0:
                        norm_part(then_norm, r + i * L.unroll(name) - 1, sq4)

                over_groups(pe, name, 1, body)
                if then_norm is not None:
                    norm_part(then_norm, L[name]["groups"] - 1, sq4)

            pe.wait_ge(consts_in, 64)
            pre_norm(0)
            with pe.Fori(0, L["ada_a"]["groups"] // 2) as i:
                for r in range(2):
                    ada_total(r, i, 2)
            layer("w_in", actH, actL, (act_ready, 0))
            pe.wait_ge(gw_lo, 1)
            for t in range(TT):
                for k in range(KT):
                    for j, (v, w) in enumerate(((actH, gwH), (actL, gwH), (actH, gwL))):
                        ins = nc.tensor.matmul(ps[:, 5, t * GATES:(t + 1) * GATES], v[:, k, t * P:(t + 1) * P], w[:, k, :],
                                               start=(t == 0 and k == 0 and j == 0), stop=(k == KT - 1 and j == 2),
                                               skip_group_check=True)
            ins.then_inc(gate_done, 1)
            pe.wait_ge(evacuated, emptied("w_in"))
            ada_next = [L["ada_a"]["groups"] + SIDE]

            def ada_totals(n):
                for _ in range(n):
                    ada_total(ada_next[0])
                    ada_next[0] += 1

            pe.wait_ge(c1_in, 16)
            for n, p in enumerate(rope_pairs):
                if n >= 2:
                    pe.wait_ge(roped, n - 1)
                nc.tensor.matmul(ps[:, 2 + n % 2, :], rot, flat(proj[:, p:p + 2, :]), start=True, stop=True
                                 ).then_inc(rotated, 1)
                if n == 0:
                    ada_totals(ADA_BEFORE[0])
            pe.wait_ge(xc_ready, 1)
            for n in range(2):
                for l in range(CMP_LEN):
                    ins = nc.tensor.matmul(ps[0:GROUPS * NCMP, 6, n * P:(n + 1) * P], xc[:, n, l, :], cw1[:, n, l, :],
                                           start=(n == 0 and l == 0), stop=(l == CMP_LEN - 1), skip_group_check=True)
            ins.then_inc(cmp_sum, 1)
            pe.wait_ge(gate_ready, 1)
            for n, p in enumerate(v_pairs):
                if n >= 2:
                    pe.wait_ge(vtok_ready, n - 1)
                for j in range(2):
                    for t in range(TT):
                        c = (2 * j + t) * P
                        ins = nc.tensor.transpose(ps[:, 4 + n % 2, c:c + P], proj[:, p + j, t * P:(t + 1) * P], ident)
                ins.then_inc(vT_done, 1)
            ada_totals(ADA_BEFORE[1])
            pe.wait_ge(cmp_hid, 1)
            for n in range(2):
                ins = nc.tensor.transpose(ps[:, 6, n * GROUPS * NCMP:(n + 1) * GROUPS * NCMP], chtok[:, n, :],
                                          ident[0:GROUPS * NCMP, 0:GROUPS * NCMP])
            ins.then_inc(cmp_T, 1)
            pe.wait_ge(cmp_hidT, 1)
            nc.tensor.matmul(ps[:, 7, 0:GROUPS * NCMP], cw2[:, 0, :], chid[:, 0, :], start=True, stop=True,
                             skip_group_check=True)
            for g in range(GROUPS):
                ins = nc.tensor.matmul(ps[0:NCMP, 7, 64 + g * P:64 + (g + 1) * P], chid[:, 1, g * NCMP:(g + 1) * NCMP],
                                       cw2[:, 1, :], start=False, stop=True, skip_group_check=True)
            ins.then_inc(cmp_kv, 1)

            def score(b):
                kind, q, kt, _, _, _, _ = subs[b]
                if b >= 1:
                    pe.wait_ge(masked, b)
                if b >= 2:
                    pe.wait_ge(pT_ready, 2 * (b - 1))
                if kind == "cmp":
                    for t in range(TT):
                        for h in range(4):
                            c = (t * 4 + h) * NCMP
                            ins = nc.tensor.matmul(ps[:, 1, c:c + NCMP], proj[:, q + h, t * P:(t + 1) * P],
                                                   kcT[:, kt * NCMP:(kt + 1) * NCMP], start=(t == 0 and h == 0), stop=True,
                                                   skip_group_check=True)
                else:
                    for h in range(4):
                        nc.tensor.matmul(ps[:, 1, h * P:(h + 1) * P], proj[:, q + h, 0:P], proj[:, kt[h], 0:P],
                                         start=(h == 0), stop=True, skip_group_check=True)
                    for h in range(4):
                        ins = nc.tensor.matmul(ps[:, 2 + h // 2, (h % 2) * T:(h % 2 + 1) * T], proj[:, q + h, P:T],
                                               proj[:, kt[h], :], start=(h % 2 == 0), stop=True, skip_group_check=True)
                ins.then_inc(scores, 1)

            def transposes(b):
                kind = subs[b][0]
                pe.wait_ge(probs_ready, b + 1)
                if kind == "cmp":
                    for h in range(4):
                        for t in range(TT):
                            c = (h % 2) * T + t * P
                            ins = nc.tensor.transpose(ps[0:NCMP, 4 + h // 2, c:c + P], pcmp[:, t, h, :], ident)
                    ins.then_inc(pT_done, 2)
                    return
                for h in range(4):
                    c = (h % 2) * T
                    nc.tensor.transpose(ps[:, 4 + h // 2, c:c + P], probs0[:, b % 2, h, :], ident)
                    ins = nc.tensor.transpose(ps[:, 4 + h // 2, c + P:c + T], probs1[:, b % 2, h, 0:P], ident)
                ins.then_inc(pT_done, 1)
                if b + 1 < NSUB:
                    pe.wait_ge(masked, b + 2)
                for h in range(4):
                    ins = nc.tensor.transpose(ps[:, 1, h * P:(h + 1) * P], probs1[:, b % 2, h, P:T], ident)
                ins.then_inc(pT_done, 1)

            def values(b):
                kind, _, g, vs, _, first, last = subs[b]
                if first and out_of[b]:
                    pe.wait_ge(oL_ready, out_of[b])
                pe.wait_ge(pT_ready, 2 * b + 2)
                for h in range(4):
                    out = ps[:, 6 + h // 2, (h % 2) * T:(h % 2 + 1) * T]
                    if kind == "cmp":
                        ins = nc.tensor.matmul(out, vc[:, g, :], pcT[:, h, :], start=False, stop=last, skip_group_check=True)
                    else:
                        nc.tensor.matmul(out, vtok[:, vs[h], 0, :], pT0[:, h, :], start=(first and h % 2 == 0), stop=False,
                                         skip_group_check=True)
                        ins = nc.tensor.matmul(out[:, P:T], vtok[:, vs[h], 1, :], pT1[:, h, :], start=False, stop=last,
                                               skip_group_check=True)
                ins.then_inc(pv_done, 1)

            pe.wait_ge(cmp_ready, GROUPS)
            pe.wait_ge(vtok_ready, len(v_pairs))
            pe.wait_ge(roped, len(rope_pairs))
            score(0)
            for b in range(NSUB):
                if b + 1 < NSUB:
                    score(b + 1)
                if b:
                    ada_totals(ADA_BESIDE[b - 1])
                transposes(b)
                values(b)
            ada_totals(ADA_BESIDE[-1])
            pe.wait_ge(oL_ready, 4)
            pe.wait_ge(mod_ready, 2)
            layer("w_o", actH, actL, None, 1)
            pre_norm(2)
            layer("up_0", actH, actL, (act_ready, 4))
            layer("down_0", hidH, hidL, (hidL_ready, 1))
            layer("up_1", actH, actL)
            layer("down_1", hidH, hidL, (hidL_ready, 9), 3)

            def rwkv_early(i, ahead, part):
                def wait(s, per, j):
                    pe.wait_ge(s, j + ahead * per + i * per)
                if part == 0:
                    wait(lw_in, 64, 64)
                for j in range(RJ):
                    c, t = slice(j * P, (j + 1) * P), slice(j * T, (j + 1) * T)
                    if part == 0:
                        ins = nc.tensor.matmul(ps[:, 3, t], lw[0:64, 0, c], proj2[0:64, SPEC, :], start=(j == 0), stop=True,
                                               skip_group_check=True)
                    if part == 1:
                        ins = nc.tensor.matmul(ps[:, 4, t], lw[64:P, 0, c], proj2[64:P, SPEC, :], start=(j == 0), stop=True,
                                               skip_group_check=True)
                    if part == 2:
                        ins = nc.tensor.matmul(ps[:, 5, t], lw[:, 1, c], proj2[:, SPEC + 1, :], start=(j == 0), stop=False,
                                               skip_group_check=True)
                if part == 2:
                    for j in range(RJ):
                        c, t = slice(j * P, (j + 1) * P), slice(j * T, (j + 1) * T)
                        ins = nc.tensor.matmul(ps[:, 5, t], lw[96:P, 2, c], proj2[96:P, SPEC + 2, :], start=False, stop=True,
                                               skip_group_check=True)
                if part < 3:
                    ins.then_inc(lora_done, 1)
                else:
                    wait(sig_ready, 3, 1)
                    wait(kksq, 1, 1)
                    nc.tensor.matmul(ps[:, 3, :], same_head, flat(nrm[:, :, :]), start=True, stop=True).then_inc(kksum, 1)

            def rwkv_turn(i, more):
                def wait(s, per, j):
                    pe.wait_ge(s, j + i * per)
                hs = [(h // 2, h % 2) for h in range(RHEADS)]
                wait(sig_ready, 3, 3)
                wait(nrm_ready, 1, 1)
                wait(mixed, 1, 1)
                for n, src in enumerate((rvv, BT, KTt)):
                    if n == 1:
                        wait(b_ready, 1, 1)
                    if n == 2:
                        wait(a_ready, 1, 1)
                    for t in range(TT):
                        for j in range(RJ):
                            c = (t * RJ + j) * P
                            ins = nc.tensor.transpose(ps[:, 4 + n, c:c + P], src[:, j, t * P:(t + 1) * P], ident)
                    ins.then_inc(tok_done, 1)
                wait(rk_scaled, 1, 1)
                wait(gstd_ready, 1, 1)
                nc.tensor.matmul(ps[:, 7, :], same_head, flat(rkk[:, :, :]), start=True, stop=True).then_inc(bonus_sum, 1)
                wait(r_ready, 2 * RJ, 2 * RJ)
                for n, src in enumerate((BT, KTt)):
                    if n:
                        wait(tok_ready, 3, 3)
                        wait(bonus_ready, 1, 1)
                    for h, (j, hh) in enumerate(hs):
                        for t in range(TT):
                            ins = nc.tensor.matmul(ps[:, 4 * n + h, t * 2 * P:(t + 1) * 2 * P], src[:, j, t * P:(t + 1) * P],
                                                   AR[hh][:, j, t, :, :].rearrange("p a t -> p (a t)"), start=(t == 0), stop=True,
                                                   skip_group_check=True)
                        ins.then_inc(mat_done, 1)
                wait(y1_ready, 1, 1)

                def each(f, out, lhs, rhs_):
                    for m in range(4 * f, 4 * f + 4):
                        ins = nc.tensor.matmul(ps[:, out + f, m % 4 * P:(m % 4 + 1) * P], lhs[:, m, :], rhs_[:, m, :],
                                               start=(m % 4 == 0), stop=True, skip_group_check=True)
                    return ins

                for f in range(2):
                    for m in range(4 * f, 4 * f + 4):
                        ins = nc.tensor.transpose(ps[:, f, m % 4 * P:(m % 4 + 1) * P], Ym[:, m, :], ident)
                    ins.then_inc(x1_done, 1)
                for v in range(1, len(LEVELS)):
                    wait(lm_ready, 5, v)
                    for f in range(2):
                        if v > 1:
                            wait(level_ready, 10, 2 * v - 3 + f)
                        else:
                            wait(x1_ready, 2, f + 1)
                        each(f, 0, Lm[:, v % 2, :, :], Xm).then_inc(w1_done, 1)
                    if v == 1:
                        wait(mat_masked, 8, 8)
                    for f in range(2):
                        wait(w1_ready, 10, 2 * v - 1 + f)
                        if v < len(LEVELS) - 1:
                            each(f, 2, Ym, W1)
                        each(f, 4, W1, Ym).then_inc(dx_done, 1)
                wait(level_ready, 10, 10)
                for c in range(TT * 2):
                    t, o_ = c // 2, c % 2 * CHUNK
                    if c:
                        wait(st_ready, 4, c)
                    for h, (j, hh) in enumerate(hs):
                        out = ps[:, 0, h * RHEAD:(h + 1) * RHEAD]
                        nc.tensor.matmul(out, AR[hh][:, j, t, 0, :], ST[:, j, hh * RHEAD:(hh + 1) * RHEAD], start=(h == 0), stop=False,
                                         skip_group_check=True)
                        ins = nc.tensor.matmul(out, Kc[:, 2 * h + t, 0:P], rtok[:, t, j, hh * RHEAD:(hh + 1) * RHEAD], start=False,
                                               stop=True, skip_group_check=True)
                    ins.then_inc(rhs_done, 1)
                    for h, (j, hh) in enumerate(hs):
                        part = slice(hh * RHEAD, (hh + 1) * RHEAD)
                        nc.tensor.matmul(ps[part, 6, j * T + c * CHUNK:j * T + (c + 1) * CHUNK], ST[:, j, part],
                                         AR[hh][:, j, t, 1, o_:o_ + CHUNK], start=(c == 0 and j == 0), stop=False, skip_group_check=True)
                    wait(rhs_ready, 4, c + 1)
                    for h in range(RHEADS):
                        ins = nc.tensor.matmul(ps[:, 1, h * RHEAD:(h + 1) * RHEAD], Ym[:, 2 * h + t, :], rhs[:, h * RHEAD:(h + 1) * RHEAD],
                                               start=(h == 0), stop=True, skip_group_check=True)
                    ins.then_inc(u_done, 1)
                    wait(u_ready, 4, c + 1)
                    for j in range(RJ):
                        out = ps[:, 2, j * P:(j + 1) * P]
                        nc.tensor.matmul(out, btok[:, c % 2, t, j, :], uf[:, j * P:(j + 1) * P], start=(j == 0), stop=False,
                                         skip_group_check=True)
                        ins = nc.tensor.matmul(out, ktok[:, c % 2, t, j, :], rtok[:, t, j, :], start=False, stop=True,
                                               skip_group_check=True)
                    ins.then_inc(s_done, 1)
                    if more:
                        for part in ((0, 1), (2,), (3,), ())[c]:
                            rwkv_early(i, 1, part)
                    if c % 2:
                        for h, (j, hh) in enumerate(hs):
                            part = slice(hh * RHEAD, (hh + 1) * RHEAD)
                            out = ps[part, 6, j * T + t * P:j * T + (t + 1) * P]
                            nc.tensor.matmul(out, uf[:, h * RHEAD:(h + 1) * RHEAD], Bc[:, 2 * h + t, P:2 * P], start=False, stop=False,
                                             skip_group_check=True)
                            ins = nc.tensor.matmul(out, rtok[:, t, j, part], Kc[:, 2 * h + t, P:2 * P], start=False, stop=True,
                                                   skip_group_check=True)
                        ins.then_inc(ysum_done, 1)
                wait(yb_ready, 1, 1)
                nc.tensor.matmul(ps[:, 7, :], same_head, flat(yb[:, :, :]), start=True, stop=True).then_inc(mean_done, 1)
                wait(ysq_ready, 1, 1)
                nc.tensor.matmul(ps[:, 7, :], same_head, flat(ysq[:, :, :]), start=True, stop=True).then_inc(var_done, 1)

            pre_norm(NB)
            layer("w_in2", actH, actL, (act_ready, 4 * XB))
            pe.wait_ge(evacuated, emptied("w_in2"))
            for n, p in enumerate((SBV, SBV + 2, FXV, FXV + 2)):
                if n >= 2:
                    pe.wait_ge(v2_ready, n - 1)
                for j in range(2):
                    for t in range(TT):
                        c = (2 * j + t) * P
                        ins = nc.tensor.transpose(ps[:, 4 + n % 2, c:c + P], proj2[:, p + j, t * P:(t + 1) * P], ident)
                ins.then_inc(v2T_done, 1)

            def score2(q, k, forget):
                for t in range(TT):
                    w = P * (t + 1)
                    for h in range(4):
                        out = ps[:, 1, h * P:(h + 1) * P] if t == 0 else ps[:, 2 + h // 2, (h % 2) * T:(h % 2 + 1) * T]
                        ts = slice(t * P, (t + 1) * P)
                        ins = nc.tensor.matmul(out, proj2[:, q + h, ts], proj2[:, k + h, 0:w],
                                               start=(h % (4, 2)[t] == 0), stop=not forget, skip_group_check=True)
                        if forget:
                            pick = ident[0:4, h:h + 1]
                            nc.tensor.matmul(out, cum[:, 3, ts], pick.to_broadcast([4, w]), start=False, stop=False,
                                             skip_group_check=True)
                            ins = nc.tensor.matmul(out, pick.to_broadcast([4, P]), cum[:, 2, 0:w], start=False, stop=True,
                                                   skip_group_check=True)
                ins.then_inc(s2_done, 1)

            def outputs2(b, first, second):
                for h in range(4):
                    c = (h % 2) * T
                    nc.tensor.transpose(ps[:, 4 + h // 2, c:c + P], first[:, h, :], ident)
                    ins = nc.tensor.transpose(ps[:, 4 + h // 2, c + P:c + T], second[:, h, 0:P], ident)
                ins.then_inc(t2_done, 1)
                for h in range(4):
                    ins = nc.tensor.transpose(ps[:, 1, h * P:(h + 1) * P], second[:, h, P:T], ident)
                ins.then_inc(t2_done, 1)
                pe.wait_ge(t2_ready, 2 * b + 2)
                if b:
                    pe.wait_ge(y2L_ready, b)
                for h in range(4):
                    out = ps[:, 6 + h // 2, (h % 2) * T:(h % 2 + 1) * T]
                    nc.tensor.matmul(out, vtok2[:, 4 * b + h, 0, :], qT0[:, h, :], start=(h % 2 == 0), stop=False,
                                     skip_group_check=True)
                    ins = nc.tensor.matmul(out[:, P:T], vtok2[:, 4 * b + h, 1, :], qT1[:, h, :], start=False, stop=True,
                                           skip_group_check=True)
                ins.then_inc(o2_done, 1)

            score2(SBQ, SBK, False)
            pe.wait_ge(v2_ready, 4)
            pe.wait_ge(cum_ready, 1)
            pe.wait_ge(s2_masked, 1)
            score2(FXQ, FXK, True)
            pe.wait_ge(s2_masked, 2)
            pe.wait_ge(s2_exp, 2)
            outputs2(0, prob0[:, 0, :, :], prob1[:, 0, :, :])
            pe.wait_ge(s2_probs, 1)
            outputs2(1, forget0, forget1)
            pe.wait_ge(y2L_ready, 2)
            pe.wait_ge(spec_ready, 1)
            pe.wait_ge(zeroed, 1)
            for part in range(4):
                rwkv_early(0, 0, part)
            with pe.Fori(0, RTURNS - 1) as i:
                rwkv_turn(i, True)
            rwkv_turn(RTURNS - 1, False)
            pe.wait_ge(turn_done, RTURNS + 1)
            layer("gates2", actH, actL)
            pe.wait_ge(evacuated, emptied("gates2"))

            def branch(i, r):
                for s, (n, k0, start, stop) in enumerate(((0, 0, True, True), (1, 4, True, True), (2, 8, True, False), (2, 12, False, True))):
                    pe.wait_ge(wl_ready, RAW + lin("branch", i, r, s) + 1)
                    if start and not (isinstance(i, int) and i == 0 and r == 0):
                        pe.wait_ge(branch_used, 3 * (r - 1) + n + 1 + i * 6)
                    b = s % SPLIT
                    for k in range(STEP_K):
                        for m in range(GT):
                            out = ps[:, 2 * n + m // 2, (m % 2) * T:(m % 2 + 1) * T]
                            cols = slice(m * P, (m + 1) * P)
                            for j, (w, v) in enumerate(((wH, yH), (wH, yL), (wL, yH))):
                                ins = nc.tensor.matmul(out, w[:, b, k, cols], v[:, k0 + k, :],
                                                       start=(start and k == 0 and j == 0 and m % 2 == 0),
                                                       stop=(stop and k == STEP_K - 1 and j == 2), skip_group_check=True)
                    ins.then_inc(step_done, 1)

            over_groups(pe, "branch", 1, branch)
            layer("w_out2", actH, actL, None, NB + 1)
            pre_norm(NB + 2)
            layer("up2_0", actH, actL, (act_ready, 4 * XB + 4))
            layer("down2_0", hidH, hidL, (hidL_ready, UB + 1))
            layer("up2_1", actH, actL)
            layer("down2_1", hidH, hidL, (hidL_ready, UB + 9), NB + 3)


def host_layout(inputs):
    given = {n: np.asarray(v) for n, v in inputs.items()}

    def own(n):
        return given[n][0]

    def col(v):
        return v.reshape(-1, P).T

    d = {"x": own("x").T, "c": col(given["c"]), "common": common_consts(), "c1": first_consts(), "c2": second_consts(),
         "vecs": np.stack([col(own(n)) for n in VECS], 1), "b_ada": col(own("b_ada")).reshape(P, 6, KT),
         "pos": np.stack([own("cmp_k_pos").T, own("cmp_v_pos").T], 1)}
    for n in ("w_ada", "w_o", "w_up", "w_down", "cmp_k_w1", "cmp_k_w2", "cmp_v_w1", "cmp_v_w2", "rwkv_w_up_2", "rwkv_a_up_2",
              "rwkv_g_up_2", "w_branch_a_2", "w_branch_b_2", "w_branch_c_2", "w_out_2", "w_mlp_up_2", "w_mlp_down_2"):
        d[n] = own(n)
    w, g0 = own("w_in"), QM * P
    d["w_in"], d["w_gate"] = np.concatenate([w[:, :g0], w[:, g0 + GATES:]], 1), w[:, g0:g0 + GATES]
    w = own("w_in_2")
    f0 = RR * P
    r0 = f0 + FORGET_H
    n0 = r0 + 3 * RW
    end = n0 + P + GATE_RANK
    d["w_in_2"] = np.concatenate([w[:, :f0], w[:, r0:n0], w[:, n0:n0 + 2 * P], w[:, end - P:end], w[:, f0:f0 + P]], 1)
    d["w_gates_2"] = w[:, end:]
    mu, m0 = own("rwkv_mu_2"), 3 * RW
    forget = np.zeros((P, 1), np.float32)
    forget[:FORGET_H, 0] = own("b_forget_2")
    d["rwv"] = np.concatenate(
        [col(mu[:m0]), *[col(own(f"rwkv_{n}_2")) for n in ("w0", "a0", "k_k", "k_a", "r_k", "ln_w", "ln_b")],
         col(mu[m0:m0 + P]), col(mu[m0 + P:m0 + 2 * P]), col(mu[-P:]), forget, np.full((P, 1), GN_EPS, np.float32)], 1)
    return {n: np.ascontiguousarray(v) for n, v in d.items()}


def kernel(**inputs):
    import concourse.bacc as bacc
    from concourse.bass_utils import run_bass_kernel_spmd

    nc = bacc.Bacc("TRN2", target_bir_lowering=False, num_devices=1)
    arrays = host_layout(inputs)
    args = {n: nc.dram_tensor(n, v.shape, F32, kind="ExternalInput").ap() for n, v in arrays.items()}
    args["out"] = nc.dram_tensor("out", (D, T), F32, kind="ExternalOutput").ap()
    build_program(nc, args)
    r = run_bass_kernel_spmd(nc, [arrays], core_ids=[0])
    return np.ascontiguousarray(r.results[0]["out"].T)[None]
```
